# Optimizing a Trainium2 kernel written in Bass

```python
import math
import jax, jax.numpy as jnp
from jax import lax
import numpy as np

D_MODEL = 1024
BATCH = 1
SEQ = 1024
DEPTH = 1

N_META = 16
CHUNK = 128
Q_BLOCK = 128
PAD = CHUNK - N_META
D_SSD = 2 * D_MODEL
SSD_HEAD_DIM = 64
H_SSD = D_SSD // SSD_HEAD_DIM
SSD_GROUPS = 4
D_STATE = 128
CONV_K = 4
CONV_DIM = D_SSD + 2 * SSD_GROUPS * D_STATE
H_ATT = 16
ATT_HEAD_DIM = 64
D_ATT = H_ATT * ATT_HEAD_DIM
N_COLS = D_SSD + CONV_DIM + H_SSD + D_ATT + 3 * D_ATT + H_ATT + 2 * D_MODEL
EPS = 1e-6


def rmsnorm(x, g):
    xf = x.astype(jnp.float32)
    y = xf * lax.rsqrt(jnp.mean(xf * xf, axis=-1, keepdims=True) + EPS)
    return (y * g.astype(jnp.float32)).astype(x.dtype)

def gated_group_rmsnorm(y, z, g):
    u = (y * jax.nn.silu(z)).astype(jnp.float32)
    shp = u.shape
    u = u.reshape(shp[:-1] + (SSD_GROUPS, shp[-1] // SSD_GROUPS))
    u = u * lax.rsqrt(jnp.mean(u * u, axis=-1, keepdims=True) + EPS)
    return (u.reshape(shp) * g.astype(jnp.float32)).astype(y.dtype)

def causal_depthwise_conv(u, w, b):
    C = u.shape[-1]
    out = lax.conv_general_dilated(u, w[:, None, :].astype(u.dtype), window_strides=(1,),
                                   padding=[(CONV_K - 1, 0)],
                                   dimension_numbers=("NWC", "WIO", "NWC"),
                                   feature_group_count=C)
    return out + b

def ssd_chunked(xh, dt, a, bmat, cmat):
    Bsz, Lp, H, P = xh.shape
    G, N = bmat.shape[-2:]
    R = H // G
    nc = Lp // CHUNK
    xdt = (xh.astype(jnp.float32) * dt[..., None]).reshape(Bsz, nc, CHUNK, G, R, P)
    adt = (dt * a).reshape(Bsz, nc, CHUNK, G, R).transpose(0, 1, 3, 4, 2)
    a_cs = jnp.cumsum(adt, axis=-1)
    bm = bmat.astype(jnp.float32).reshape(Bsz, nc, CHUNK, G, N)
    cm = cmat.astype(jnp.float32).reshape(Bsz, nc, CHUNK, G, N)
    causal = jnp.tril(jnp.ones((CHUNK, CHUNK), dtype=bool))
    seg = a_cs[..., :, None] - a_cs[..., None, :]
    decay = jnp.exp(jnp.where(causal, seg, -jnp.inf))
    cb = jnp.einsum("bclgn,bcsgn->bcgls", cm, bm)
    y_diag = jnp.einsum("bcgls,bcgrls,bcsgrp->bclgrp", cb, decay, xdt)
    decay_states = jnp.exp(a_cs[..., -1:] - a_cs)
    states = jnp.einsum("bclgn,bcgrl,bclgrp->bcgrpn", bm, decay_states, xdt)
    chunk_decay = jnp.exp(a_cs[..., -1])

    def step(h, inp):
        s, d = inp
        return h * d[..., None, None] + s, h

    h0 = jnp.zeros((Bsz, G, R, P, N), jnp.float32)
    _, h_in = lax.scan(step, h0, (jnp.swapaxes(states, 0, 1), jnp.swapaxes(chunk_decay, 0, 1)))
    h_in = jnp.swapaxes(h_in, 0, 1)
    y_off = jnp.einsum("bclgn,bcgrpn,bcgrl->bclgrp", cm, h_in, jnp.exp(a_cs))
    return (y_diag + y_off).reshape(Bsz, Lp, H, P)

def forgetting_attention(q, k, v, logf):
    Bsz, Lp, H, Dh = q.shape
    scale = 1.0 / math.sqrt(Dh)
    c = jnp.cumsum(logf, axis=1)
    c_k = jnp.transpose(c, (0, 2, 1))
    nb = Lp // Q_BLOCK
    qb = q.reshape(Bsz, nb, Q_BLOCK, H, Dh).transpose(1, 0, 2, 3, 4)
    cqb = c.reshape(Bsz, nb, Q_BLOCK, H).transpose(1, 0, 3, 2)
    kpos = jnp.arange(Lp)

    def block(args):
        i, qi, cqi = args
        qpos = i * Q_BLOCK + jnp.arange(Q_BLOCK)
        s = jnp.einsum("bthd,bshd->bhts", qi, k).astype(jnp.float32) * scale
        s = s + (cqi[..., :, None] - c_k[..., None, :])
        s = jnp.where(kpos[None, :] <= qpos[:, None], s, -jnp.inf)
        p = jax.nn.softmax(s, axis=-1).astype(v.dtype)
        return jnp.einsum("bhts,bshd->bthd", p, v)

    out = lax.map(block, (jnp.arange(nb), qb, cqb))
    return out.transpose(1, 0, 2, 3, 4).reshape(Bsz, Lp, H, Dh)

def hybrid_layer(h, norm_pre, w_in, conv_w, conv_b, dt_bias, a_log, d_skip, ssd_norm,
                 fgate_bias, gate_bias, w_proj_ssd, w_proj_att, w_out, norm_post):
    Bsz, L, _ = h.shape
    Lp = L + PAD
    u = rmsnorm(h, norm_pre)
    proj = u @ w_in
    cuts = [D_SSD, D_SSD + CONV_DIM, D_SSD + CONV_DIM + H_SSD,
            D_SSD + CONV_DIM + H_SSD + D_ATT,
            D_SSD + CONV_DIM + H_SSD + 2 * D_ATT,
            D_SSD + CONV_DIM + H_SSD + 3 * D_ATT,
            D_SSD + CONV_DIM + H_SSD + 4 * D_ATT,
            D_SSD + CONV_DIM + H_SSD + 4 * D_ATT + H_ATT]
    z_ssd, xbc, dt_raw, z_att, q, k, v, f_raw, g_raw = jnp.split(proj, cuts, axis=-1)

    xbc = jax.nn.silu(causal_depthwise_conv(xbc, conv_w, conv_b))
    xs, bm, cm = jnp.split(xbc, [D_SSD, D_SSD + SSD_GROUPS * D_STATE], axis=-1)
    dt = jax.nn.softplus(dt_raw.astype(jnp.float32) + dt_bias.astype(jnp.float32))
    a = -jnp.exp(a_log.astype(jnp.float32))
    front = ((0, 0), (PAD, 0), (0, 0))
    xs_p = jnp.pad(xs, front).reshape(Bsz, Lp, H_SSD, SSD_HEAD_DIM)
    bm_p = jnp.pad(bm, front).reshape(Bsz, Lp, SSD_GROUPS, D_STATE)
    cm_p = jnp.pad(cm, front).reshape(Bsz, Lp, SSD_GROUPS, D_STATE)
    dt_p = jnp.pad(dt, front)
    y = ssd_chunked(xs_p, dt_p, a, bm_p, cm_p)
    y = y + d_skip.astype(jnp.float32)[:, None] * xs_p.astype(jnp.float32)
    y = y[:, PAD:].reshape(Bsz, L, D_SSD).astype(h.dtype)
    y_ssd = gated_group_rmsnorm(y, z_ssd, ssd_norm)

    logf = jax.nn.log_sigmoid(f_raw.astype(jnp.float32) + fgate_bias.astype(jnp.float32))
    back = ((0, 0), (0, PAD), (0, 0))
    qh = jnp.pad(q, back).reshape(Bsz, Lp, H_ATT, ATT_HEAD_DIM)
    kh = jnp.pad(k, back).reshape(Bsz, Lp, H_ATT, ATT_HEAD_DIM)
    vh = jnp.pad(v, back).reshape(Bsz, Lp, H_ATT, ATT_HEAD_DIM)
    o = forgetting_attention(qh, kh, vh, jnp.pad(logf, back))
    o = o[:, :L].reshape(Bsz, L, D_ATT)
    y_att = o * jax.nn.silu(z_att)

    gates = jax.nn.sigmoid(g_raw + gate_bias)
    g_ssd, g_att = jnp.split(gates, 2, axis=-1)
    merged = g_ssd * (y_ssd @ w_proj_ssd) + g_att * (y_att @ w_proj_att)
    return h + rmsnorm(merged @ w_out, norm_post)

def first_inputs(seed: int = 0) -> dict:
    key = jax.random.key(seed)
    ks = jax.random.split(key, 16)
    D = D_MODEL
    nrm = jax.random.normal
    x = nrm(ks[0], (BATCH, SEQ, D), jnp.float32)
    meta_tokens = nrm(ks[1], (N_META, D), jnp.float32)
    norm_pre = 1.0 + 0.05 * nrm(ks[2], (DEPTH, D), jnp.float32)
    w_in = nrm(ks[3], (DEPTH, D, N_COLS), jnp.float32) * D ** -0.5
    conv_w = jax.random.uniform(ks[4], (DEPTH, CONV_K, CONV_DIM), jnp.float32, -0.5, 0.5)
    conv_b = 0.05 * nrm(ks[5], (DEPTH, CONV_DIM), jnp.float32)
    dt0 = jnp.exp(jax.random.uniform(ks[6], (DEPTH, H_SSD), jnp.float32,
                                     math.log(1e-3), math.log(1e-1)))
    dt_bias = dt0 + jnp.log(-jnp.expm1(-dt0))
    a_log = jnp.log(jax.random.uniform(ks[7], (DEPTH, H_SSD), jnp.float32, 1.0, 16.0))
    d_skip = 1.0 + 0.1 * nrm(ks[8], (DEPTH, H_SSD), jnp.float32)
    ssd_norm = 1.0 + 0.05 * nrm(ks[9], (DEPTH, D_SSD), jnp.float32)
    fgate_bias = jax.random.uniform(ks[10], (DEPTH, H_ATT), jnp.float32, 1.0, 6.0)
    gate_bias = 0.1 * nrm(ks[11], (DEPTH, 2 * D), jnp.float32)
    w_proj_ssd = nrm(ks[12], (DEPTH, D_SSD, D), jnp.float32) * D_SSD ** -0.5
    w_proj_att = nrm(ks[13], (DEPTH, D_ATT, D), jnp.float32) * D_ATT ** -0.5
    w_out = nrm(ks[14], (DEPTH, D, D), jnp.float32) * D ** -0.5
    norm_post = 1.0 + 0.05 * nrm(ks[15], (DEPTH, D), jnp.float32)
    return {"x": x, "meta_tokens": meta_tokens, "norm_pre": norm_pre, "w_in": w_in,
            "conv_w": conv_w, "conv_b": conv_b, "dt_bias": dt_bias, "a_log": a_log,
            "d_skip": d_skip, "ssd_norm": ssd_norm, "fgate_bias": fgate_bias,
            "gate_bias": gate_bias, "w_proj_ssd": w_proj_ssd, "w_proj_att": w_proj_att,
            "w_out": w_out, "norm_post": norm_post}

def first_block(x, meta_tokens, norm_pre, w_in, conv_w, conv_b, dt_bias, a_log, d_skip,
              ssd_norm, fgate_bias, gate_bias, w_proj_ssd, w_proj_att, w_out, norm_post):
    Bsz = x.shape[0]
    meta = jnp.broadcast_to(meta_tokens[None].astype(x.dtype), (Bsz, N_META, D_MODEL))
    h = jnp.concatenate([meta, x], axis=1)
    for i in range(DEPTH):
        h = hybrid_layer(h, norm_pre[i], w_in[i], conv_w[i], conv_b[i], dt_bias[i], a_log[i],
                         d_skip[i], ssd_norm[i], fgate_bias[i], gate_bias[i], w_proj_ssd[i],
                         w_proj_att[i], w_out[i], norm_post[i])
    return h[:, N_META:]


PLE_DIM = 256
HEAD_DIM = 64
DIFF_HEADS = 4
DIFF_QK = 2 * HEAD_DIM
DIFF_V = 2 * HEAD_DIM
DIFF_WIDTH = DIFF_HEADS * DIFF_V
DIL_HEADS = 8
DIL_WIDTH = DIL_HEADS * HEAD_DIM
DIL_PATTERNS = ((128, 1), (512, 4), (2048, 16))
MIX_WIDTH = DIFF_WIDTH + DIL_WIDTH
NORM_EPS = 1e-6
MASK_VALUE = -1e30

IN_SPLIT_SIZES = (
    DIFF_HEADS * DIFF_QK,
    DIFF_HEADS * DIFF_QK,
    DIFF_WIDTH,
    DIL_WIDTH,
    DIL_WIDTH,
    DIL_WIDTH,
    MIX_WIDTH,
)
IN_WIDTH = sum(IN_SPLIT_SIZES)
IN_SPLIT_IDX = tuple(int(v) for v in np.cumsum(IN_SPLIT_SIZES)[:-1])


def rms_norm(t, g):
    tf = t.astype(jnp.float32)
    y = tf * lax.rsqrt(jnp.mean(tf * tf, axis=-1, keepdims=True) + NORM_EPS)
    return (y * g.astype(jnp.float32)).astype(t.dtype)

def alibi_slopes(n_heads):
    return jnp.exp2(-8.0 * jnp.arange(1, n_heads + 1, dtype=jnp.float32) / n_heads)

def diff_attention(q, k, v, lam, slopes):
    B, S, H, _, Dh = q.shape
    scale = Dh ** -0.5
    nqb = S // Q_BLOCK
    pos = jnp.arange(S)
    qb = q.reshape(B, nqb, Q_BLOCK, H, 2, Dh).transpose(1, 0, 2, 3, 4, 5)
    qpos = pos.reshape(nqb, Q_BLOCK)

    def block(args):
        qblk, qp = args
        s = jnp.einsum('bqhce,bkhce->bchqk', qblk, k).astype(jnp.float32) * scale
        dist = jnp.abs(qp[:, None] - pos[None, :]).astype(jnp.float32)
        s = s - slopes[:, None, None] * dist
        a = jax.nn.softmax(s, axis=-1)
        w = a[:, 0] - lam * a[:, 1]
        return jnp.einsum('bhqk,bkhe->bqhe', w.astype(v.dtype), v)

    out = lax.map(block, (qb, qpos))
    return out.transpose(1, 0, 2, 3, 4).reshape(B, S, H, 2 * Dh)

def dilated_branch(q, k, v, slopes, window, dilation):
    B, S, H, Dh = q.shape
    r = window // (2 * dilation)
    blk = r
    unit = dilation * blk
    Lp = -(-S // unit) * unit
    n = Lp // dilation
    nb = n // blk
    scale = Dh ** -0.5

    def split(t):
        t = jnp.pad(t, ((0, 0), (0, Lp - S), (0, 0), (0, 0)))
        return t.reshape(B, nb, blk, dilation, H, Dh)

    def window3(t):
        tp = jnp.pad(t, ((0, 0), (1, 1), (0, 0), (0, 0), (0, 0), (0, 0)))
        return jnp.concatenate([tp[:, :-2], tp[:, 1:-1], tp[:, 2:]], axis=2)

    qs = split(q)
    kw = window3(split(k))
    vw = window3(split(v))

    qi = jnp.arange(nb)[:, None] * blk + jnp.arange(blk)[None, :]
    kj = (jnp.arange(nb)[:, None] - 1) * blk + jnp.arange(3 * blk)[None, :]
    rel = qi[:, :, None] - kj[:, None, :]
    kpos = kj[:, :, None] * dilation + jnp.arange(dilation)[None, None, :]
    key_ok = ((kj >= 0)[:, :, None] & (kpos < S)).transpose(0, 2, 1)
    mask = (jnp.abs(rel) <= r)[:, None, None] & key_ok[:, :, None, None, :]
    dist = (dilation * jnp.abs(rel)).astype(jnp.float32)[:, None, None]
    bias = -slopes[:, None, None] * dist

    s = jnp.einsum('bnqche,bnkche->bnchqk', qs, kw).astype(jnp.float32) * scale + bias
    s = jnp.where(mask, s, MASK_VALUE)
    m = jnp.max(s, axis=-1, keepdims=True)
    e = jnp.exp(s - m)
    l = jnp.sum(e, axis=-1, keepdims=True)
    o = jnp.einsum('bnchqk,bnkche->bnqche', e.astype(v.dtype), vw)
    inv_l = (1.0 / l[..., 0]).transpose(0, 1, 4, 2, 3)[..., None]
    o = (o.astype(jnp.float32) * inv_l).reshape(B, Lp, H, Dh)[:, :S]
    lse = (m[..., 0] + jnp.log(l[..., 0])).transpose(0, 1, 4, 2, 3).reshape(B, Lp, H)[:, :S]
    return o, lse

def dilated_attention(q, k, v, slopes):
    outs, lses = [], []
    for window, dilation in DIL_PATTERNS:
        o, lse = dilated_branch(q, k, v, slopes, window, dilation)
        outs.append(o)
        lses.append(lse)
    w = jax.nn.softmax(jnp.stack(lses, axis=0), axis=0)
    out = jnp.sum(w[..., None] * jnp.stack(outs, axis=0), axis=0)
    return out.astype(q.dtype)

def second_inputs(seed: int = 0) -> dict:
    key = jax.random.key(seed)
    ks = jax.random.split(key, 20)
    f32 = jnp.float32

    def gain(k, n):
        return 1.0 + 0.02 * jax.random.normal(k, (DEPTH, n), f32)

    return {
        "x": jax.random.normal(ks[0], (BATCH, SEQ, D_MODEL), f32),
        "p": jax.random.normal(ks[1], (DEPTH, BATCH, SEQ, PLE_DIM), f32),
        "mix_norm_g": gain(ks[2], D_MODEL),
        "w_in": jax.random.normal(ks[3], (DEPTH, D_MODEL, IN_WIDTH), f32) * D_MODEL ** -0.5,
        "diff_q_norm_g": gain(ks[4], HEAD_DIM),
        "diff_k_norm_g": gain(ks[5], HEAD_DIM),
        "lambda_q1": 0.1 * jax.random.normal(ks[6], (DEPTH, HEAD_DIM), f32),
        "lambda_k1": 0.1 * jax.random.normal(ks[7], (DEPTH, HEAD_DIM), f32),
        "lambda_q2": 0.1 * jax.random.normal(ks[8], (DEPTH, HEAD_DIM), f32),
        "lambda_k2": 0.1 * jax.random.normal(ks[9], (DEPTH, HEAD_DIM), f32),
        "diff_sub_norm_g": gain(ks[10], DIFF_V),
        "dil_q_norm_g": gain(ks[11], HEAD_DIM),
        "dil_k_norm_g": gain(ks[12], HEAD_DIM),
        "w_out": jax.random.normal(ks[13], (DEPTH, MIX_WIDTH, D_MODEL), f32) * MIX_WIDTH ** -0.5,
        "ple_norm_g": gain(ks[14], D_MODEL),
        "w_ple_gate": jax.random.normal(ks[15], (DEPTH, D_MODEL, D_MODEL), f32) * D_MODEL ** -0.5,
        "w_ple_proj": jax.random.normal(ks[16], (DEPTH, PLE_DIM, D_MODEL), f32) * PLE_DIM ** -0.5,
    }

def second_block(x, p, mix_norm_g, w_in, diff_q_norm_g, diff_k_norm_g,
              lambda_q1, lambda_k1, lambda_q2, lambda_k2, diff_sub_norm_g,
              dil_q_norm_g, dil_k_norm_g, w_out, ple_norm_g, w_ple_gate, w_ple_proj):
    B, S, _ = x.shape
    diff_slopes = alibi_slopes(DIFF_HEADS)
    dil_slopes = alibi_slopes(DIL_HEADS)
    for i in range(DEPTH):
        lam_init = 0.8 - 0.6 * math.exp(-0.3 * i)
        h = rms_norm(x, mix_norm_g[i])
        u = h @ w_in[i]
        dq, dk, dv, bq, bk, bv, z = jnp.split(u, IN_SPLIT_IDX, axis=-1)

        dq = rms_norm(dq.reshape(B, S, DIFF_HEADS, 2, HEAD_DIM), diff_q_norm_g[i])
        dk = rms_norm(dk.reshape(B, S, DIFF_HEADS, 2, HEAD_DIM), diff_k_norm_g[i])
        dv = dv.reshape(B, S, DIFF_HEADS, DIFF_V)
        lam = (jnp.exp(jnp.sum(lambda_q1[i].astype(jnp.float32) * lambda_k1[i].astype(jnp.float32)))
               - jnp.exp(jnp.sum(lambda_q2[i].astype(jnp.float32) * lambda_k2[i].astype(jnp.float32)))
               + lam_init)
        a = diff_attention(dq, dk, dv, lam, diff_slopes)
        a = rms_norm(a, diff_sub_norm_g[i]) * (1.0 - lam_init)
        a = a.reshape(B, S, DIFF_WIDTH)

        bq = rms_norm(bq.reshape(B, S, DIL_HEADS, HEAD_DIM), dil_q_norm_g[i])
        bk = rms_norm(bk.reshape(B, S, DIL_HEADS, HEAD_DIM), dil_k_norm_g[i])
        bv = bv.reshape(B, S, DIL_HEADS, HEAD_DIM)
        b = dilated_attention(bq, bk, bv, dil_slopes).reshape(B, S, DIL_WIDTH)

        y = jnp.concatenate([a, b], axis=-1) * jax.nn.silu(z)
        x = x + y @ w_out[i]

        gate = jax.nn.sigmoid(rms_norm(x, ple_norm_g[i]) @ w_ple_gate[i])
        x = x + gate * (p[i] @ w_ple_proj[i])
    return x


def setup_inputs(seed=0):
    out = dict(first_inputs(seed))
    for name, value in second_inputs(seed + 1).items():
        if name != "x":
            out[name + "_2"] = value
    return out


def reference(
    x, meta_tokens, norm_pre, w_in, conv_w, conv_b, dt_bias, a_log, d_skip, ssd_norm,
    fgate_bias, gate_bias, w_proj_ssd, w_proj_att, w_out, norm_post, p_2, mix_norm_g_2, w_in_2,
    diff_q_norm_g_2, diff_k_norm_g_2, lambda_q1_2, lambda_k1_2, lambda_q2_2, lambda_k2_2,
    diff_sub_norm_g_2, dil_q_norm_g_2, dil_k_norm_g_2, w_out_2, ple_norm_g_2, w_ple_gate_2,
    w_ple_proj_2,
):
    x = first_block(
        x, meta_tokens, norm_pre, w_in, conv_w, conv_b, dt_bias, a_log, d_skip, ssd_norm,
        fgate_bias, gate_bias, w_proj_ssd, w_proj_att, w_out, norm_post,
    )
    return second_block(
        x, p_2, mix_norm_g_2, w_in_2, diff_q_norm_g_2, diff_k_norm_g_2, lambda_q1_2,
        lambda_k1_2, lambda_q2_2, lambda_k2_2, diff_sub_norm_g_2, dil_q_norm_g_2,
        dil_k_norm_g_2, w_out_2, ple_norm_g_2, w_ple_gate_2, w_ple_proj_2,
    )


_drawn_inputs = setup_inputs


def setup_inputs(seed=0):
    import zlib

    import numpy as np

    out = dict(_drawn_inputs(seed))
    spreads = {}
    factors = {'mix_norm_g_2': 6.635,
     'diff_q_norm_g_2': 8.0,
     'diff_k_norm_g_2': 8.0,
     'lambda_q1_2': 6.07,
     'lambda_k1_2': 4.399,
     'lambda_k2_2': 3.909,
     'diff_sub_norm_g_2': 8.0,
     'dil_q_norm_g_2': 8.0,
     'dil_k_norm_g_2': 8.0,
     'ple_norm_g_2': 8.0}
    for name, (base, spread) in spreads.items():
        noise = np.random.default_rng([zlib.crc32(name.encode()), seed]).standard_normal(out[name].shape)
        drawn = base * np.exp(spread * noise) if base else spread * noise
        out[name] = __import__('jax').numpy.asarray(drawn.astype(out[name].dtype))
    for name, factor in factors.items():
        out[name] = (out[name] * factor).astype(out[name].dtype)
    return out
```

```python
import concourse.bass as bass
from concourse import mybir
from contextlib import ExitStack
import math

F32 = mybir.dt.float32
F32R = mybir.dt.float32r
BF16 = mybir.dt.bfloat16
ALU = mybir.AluOpType
ACT = mybir.ActivationFunctionType
P = 128
D = 1024
T = 1024
META = 16
L = META + T
KT = D // P
CH = T // P
GROUPS, HG = 4, 8
SSD_H, ATT_H = 32, 16
SM = 48
EPS = 1e-6
NEG = -1e30
THIRDS = [(0, 348), (348, 696), (696, 1040)]
HALVES = [(META, META + 512), (META + 512, L)]


def chunk_cols(c):
    return (0, META) if c == 0 else (META + P * (c - 1), META + P * c)


USED = []


def semaphore(nc, ctx, name):
    USED.append(ctx.enter_context(nc.semaphore(name)))
    return USED[-1]


def clear_semaphores(nc):
    with nc.Block() as block:
        @block.gpsimd
        def _(pool):
            for s in USED:
                pool.sem_clear(s)
    USED.clear()


class Chain:

    def __init__(self, eng, sem, per=0, i=0):
        self.eng, self.sem, self.per, self.i, self.n = eng, sem, per, i, 0

    def step(self, ins):
        ins.then_inc(self.sem, 1)
        self.n += 1
        return self.n

    def after(self, n):
        self.eng.wait_ge(self.sem, self.i * self.per + n)

    def link(self, ins):
        self.after(self.step(ins))


def gemm(nc, out, w_hi, w_lo, a_hi, a_lo, kk=KT, first=True, final=True):
    for k in range(kk):
        nc.tensor.matmul(out, w_hi[:, k], a_hi(k), start=(k == 0 and first), stop=False)
        nc.tensor.matmul(out, w_hi[:, k], a_lo(k), start=False, stop=False)
        last = nc.tensor.matmul(out, w_lo[:, k], a_hi(k), start=False, stop=(k == kk - 1 and final))
    return last


class Kernel:

    def __init__(self, d, s):
        self.d, self.s = d, s


class Weights:

    def __init__(self, nc, ctx, name, raw_slots=4):
        self.nc, self.R = nc, raw_slots
        self.raw = ctx.enter_context(nc.sbuf_tensor(name + "_raw", [P, raw_slots, KT, P], F32))
        self.hi = ctx.enter_context(nc.sbuf_tensor(name + "_hi", [P, 2, KT, P], F32R))
        self.lo = ctx.enter_context(nc.sbuf_tensor(name + "_lo", [P, 2, KT, P], F32R))
        s = lambda n: semaphore(nc, ctx, name + n)
        self.loaded = [s(f"_loaded{r}") for r in range(raw_slots)]
        self.raw_free = s("_raw_free")
        self.hi_done = s("_hi_done")
        self.turns = s("_turns")
        self.ready = s("_split")
        self.used = s("_used")

    def credits_raw(self, eng):
        eng.sem_inc(self.raw_free, self.R)

    def credits_used(self, eng):
        eng.sem_inc(self.used, 2)

    def load(self, eng, i, per, n, src):
        eng.wait_ge(self.raw_free, i * per + n + 1)
        eng.dma_start(self.raw[:, n % self.R].rearrange("p k n -> p (k n)"), src).then_inc(self.loaded[n % self.R], 16)

    def split(self, eng, i, per, n):
        r = n % self.R
        eng.wait_ge(self.loaded[r], 16 * (i * (per // self.R) + n // self.R + 1))
        eng.wait_ge(self.used, i * per + n + 1)
        eng.sem_inc(self.turns, 1)
        self.nc.gpsimd.tensor_scalar(self.hi[:, n % 2], self.raw[:, r], 1.0, 1.0, ALU.mult, ALU.mult).then_inc(self.hi_done, 1)
        eng.wait_ge(self.hi_done, i * per + n + 1)
        self.nc.gpsimd.tensor_tensor(self.lo[:, n % 2], self.raw[:, r], self.hi[:, n % 2].bitcast(F32),
                                     ALU.subtract).then_inc(self.ready, 1)
        eng.wait_ge(self.ready, i * per + n + 1)
        eng.sem_inc(self.raw_free, 1)

    def wait(self, eng, i, per, n):
        eng.wait_ge(self.ready, i * per + n + 1)


def norm_phase(nc, K, name, xT, cols, pieces, gain, u_hi, u_lo):
    C = cols
    with ExitStack() as ctx:
        sq = ctx.enter_context(nc.sbuf_tensor(name + "_sq", [P, 2, C], F32))
        rs = ctx.enter_context(nc.sbuf_tensor(name + "_rs", [P, C], F32))
        rt = ctx.enter_context(nc.sbuf_tensor(name + "_rt", [P, C], F32))
        un = ctx.enter_context(nc.sbuf_tensor(name + "_un", [P, 2, C], F32))
        s = lambda n: semaphore(nc, ctx, name + n)
        squared, summed, rooted, inverted = s("_squared"), s("_summed"), s("_rooted"), s("_inverted")
        scaled, hi_ok, lo_ok = s("_scaled"), s("_hi"), s("_lo")
        block = ctx.enter_context(nc.Block())
        ps = K.psum

        @block.scalar
        def _(act):
            for k in range(KT):
                if k >= 2:
                    act.wait_ge(summed, k - 1)
                nc.scalar.activation(sq[:, k % 2], xT[:, k], ACT.Square).then_inc(squared, 1)
            act.wait_ge(summed, KT)
            for j, (a, b) in enumerate(pieces):
                nc.scalar.activation(rt[:, a:b], ps[:, 512 * j:512 * j + b - a], ACT.Sqrt, scale=1.0 / D,
                                     bias=K.eps[:, 0:1]).then_inc(rooted, 1)
            for k in range(KT):
                act.wait_ge(scaled, k + 1)
                nc.scalar.activation(u_hi[:, k], un[:, k % 2], ACT.Copy).then_inc(hi_ok, 1)

        @block.tensor
        def _(pe):
            for k in range(KT):
                pe.wait_ge(squared, k + 1)
                for j, (a, b) in enumerate(pieces):
                    last = nc.tensor.matmul(ps[:, 512 * j:512 * j + b - a], K.ones[:, :], sq[:, k % 2, a:b],
                                            start=(k == 0), stop=(k == KT - 1))
                last.then_inc(summed, 1)

        @block.vector
        def _(dve):
            dve.wait_ge(rooted, len(pieces))
            nc.vector.reciprocal(rs[:, :], rt[:, :]).then_inc(inverted, 1)
            dve.wait_ge(inverted, 1)
            for k in range(KT):
                if k >= 2:
                    dve.wait_ge(lo_ok, k - 1)
                nc.vector.scalar_tensor_tensor(un[:, k % 2], xT[:, k], gain[:, k:k + 1], rs[:, :],
                                               ALU.mult, ALU.mult).then_inc(scaled, 1)

        @block.gpsimd
        def _(pool):
            for k in range(KT):
                pool.wait_ge(hi_ok, k + 1)
                nc.gpsimd.tensor_tensor(u_lo[:, k], un[:, k % 2], u_hi[:, k].bitcast(F32),
                                        ALU.subtract).then_inc(lo_ok, 1)


def load_phase(nc, K, xT):
    with ExitStack() as ctx:
        xt = ctx.enter_context(nc.sbuf_tensor("x_tok", [P, CH + 1, D], F32))
        s = lambda n: semaphore(nc, ctx, n)
        const_in, out_xT = s("const_in"), s("xT_stored")
        x_in = [s(f"x_in{c}") for c in range(CH + 1)]
        turned, copied = s("x_turned"), s("x_copied")
        ms = s("eps_set")
        block = ctx.enter_context(nc.Block())
        ps = K.psum
        consts = [(K.ident, K.d["ident"]), (K.tri, K.d["tri"]), (K.gains, K.d["gains"]), (K.mask, K.d["mask"]), (K.pairs, K.d["pairs"])]

        @block.sync
        def _(sp):
            for dst, src in consts:
                sp.dma_start(dst[:, :], src).then_inc(const_in, 16)
            for c in range(CH + 1):
                n = META if c == 0 else P
                src = K.d["meta"] if c == 0 else K.d["x"][0, P * (c - 1):P * c, :]
                sp.dma_start(xt[0:n, c, :], src).then_inc(x_in[c], 16)
            for k in range(KT):
                sp.wait_ge(copied, 2 * (CH + 1))
                sp.dma_start(K.s["xT"][k], xT[:, k, META:L]).then_inc(out_xT, 16)
            sp.wait_ge(out_xT, 16 * KT)

        @block.vector
        def _(dve):
            dve.wait_ge(const_in, 16 * len(consts))
            nc.vector.tensor_copy(K.identb[:, :], K.ident[:, :])
            nc.vector.tensor_scalar(K.maskb[:, :], K.mask[:, :], NEG, None, ALU.mult)
            nc.vector.memset(K.eps[:, :], EPS)
            nc.vector.memset(K.ones[:, :], 1.0).then_inc(ms, 1)
            dve.wait_ge(ms, 1)

        @block.tensor
        def _(pe):
            pe.wait_ge(const_in, 16 * len(consts))
            for c in range(CH + 1):
                n = META if c == 0 else P
                pe.wait_ge(x_in[c], 16)
                for h in range(2):
                    u = 2 * c + h
                    if u >= 4:
                        pe.wait_ge(copied, u - 3)
                    for f in range(4):
                        last = nc.tensor.transpose(ps[:, 512 * (u % 4) + P * f:512 * (u % 4) + P * f + n],
                                                   xt[0:n, c, P * (4 * h + f):P * (4 * h + f + 1)], K.ident[0:n, 0:n])
                    last.then_inc(turned, 1)

        @block.scalar
        def _(act):
            for c in range(CH + 1):
                a, b = chunk_cols(c)
                for h in range(2):
                    u = 2 * c + h
                    act.wait_ge(turned, u + 1)
                    bank = ps[:, 512 * (u % 4):512 * (u % 4) + 512].rearrange("p (f n) -> p f n", f=4)
                    nc.scalar.activation(xT[:, 4 * h:4 * h + 4, a:b], bank[:, :, 0:b - a], ACT.Copy).then_inc(copied, 1)


def small_phase(nc, K, u_hi, u_lo, sm):
    NCH = CH + 1
    with ExitStack() as ctx:
        sb = lambda n, sh, dt=F32: ctx.enter_context(nc.sbuf_tensor(n, sh, dt))
        wraw, whi, wlo = sb("wdf_raw", [P, KT, SM]), sb("wdf_hi", [P, KT, SM], F32R), sb("wdf_lo", [P, KT, SM], F32R)
        brow = sb("dtf_bias", [P, SM])
        arow = sb("a_row", [P, SSD_H])
        aneg = sb("a_neg", [P, SSD_H])
        sgn = sb("dtf_sign", [P, SM])
        names = ["raw", "v", "e", "w", "l", "q", "t", "z", "sp"]
        B = {n: sb("dtf_" + n, [P, NCH, SM]) for n in names}
        adt = sb("adt", [P, NCH, SSD_H])
        acs = sb("acs", [P, NCH, SSD_H])
        alast = sb("alast", [P, NCH, SSD_H])
        fT = sb("fT", [ATT_H, L])
        ncT = sb("ncT", [ATT_H, L])
        onesL = sb("onesL", [ATT_H, L])
        s = lambda n: semaphore(nc, ctx, n)
        w_in, w_split, proj, V, A, G, X, pemm, st = (s("dtf_" + n) for n in
            ["loaded", "wsplit", "projected", "dve", "act", "pool", "x", "pe", "stored"])
        block = ctx.enter_context(nc.Block())
        ps = K.psum

        @block.sync
        def _(sp):
            sp.dma_start(wraw[:, :, :], K.d["wdf"]).then_inc(w_in, 16)
            sp.dma_start(brow[:, :], K.d["dtf_bias"].to_broadcast([P, SM])).then_inc(w_in, 16)
            sp.dma_start(arow[:, :], K.d["a_log"].to_broadcast([P, SSD_H])).then_inc(w_in, 16)
            sp.wait_ge(X, 1)
            sp.dma_start(K.s["nc"], ncT[:, :]).then_inc(st, 16)
            sp.wait_ge(st, 16)

        @block.gpsimd
        def _(pool):
            pool.wait_ge(w_in, 48)
            nc.gpsimd.tensor_copy(whi[:, :, :], wraw[:, :, :]).then_inc(G, 1)
            pool.wait_ge(G, 1)
            nc.gpsimd.tensor_tensor(wlo[:, :, :], wraw[:, :, :], whi[:, :, :].bitcast(F32), ALU.subtract).then_inc(w_split, 1)

        @block.tensor
        def _(pe):
            pe.wait_ge(w_split, 1)
            for c in range(NCH):
                a, b = chunk_cols(c)
                out = ps[0:b - a, SM * c:SM * (c + 1)]
                for k in range(KT):
                    nc.tensor.matmul(out, u_hi[:, k, a:b], whi[:, k], start=(k == 0), stop=False)
                    nc.tensor.matmul(out, u_hi[:, k, a:b], wlo[:, k], start=False, stop=False)
                    last = nc.tensor.matmul(out, u_lo[:, k, a:b], whi[:, k], start=False, stop=(k == KT - 1))
            last.then_inc(pemm, 1)
            pe.wait_ge(proj, 1)
            nc.tensor.matmul(ps[:, 512:768], K.tri[:, :], adt[:, 1:, :], start=True, stop=True)
            nc.tensor.matmul(ps[0:META, 768:800], K.tri[0:META, 0:META], adt[0:META, 0, :], start=True, stop=True)
            nc.tensor.matmul(ps[:, 1024:1280], K.ones[:, :], adt[:, 1:, :], start=True, stop=True)
            nc.tensor.matmul(ps[:, 1280:1312], K.ones[0:META, :], adt[0:META, 0, :], start=True, stop=True)
            for c in range(NCH):
                a, b = chunk_cols(c)
                last = nc.tensor.transpose(ps[0:ATT_H, 1536 + 512 * (c // 3) + P * (c % 3):1536 + 512 * (c // 3) + P * (c % 3) + b - a],
                                           B["sp"][0:b - a, c, SSD_H:SM], K.ident[0:b - a, 0:b - a])
            last.then_inc(pemm, 1)

        @block.scalar
        def _(act):
            act.wait_ge(w_in, 48)
            nc.scalar.activation(aneg[:, :], arow[:, :], ACT.Exp).then_inc(A, 1)
            act.wait_ge(V, 5)
            nc.scalar.activation(B["e"][:, :, :], B["e"][:, :, :], ACT.Exp, scale=-1.0).then_inc(A, 1)
            act.wait_ge(V, 6)
            nc.scalar.activation(B["l"][:, :, :], B["w"][:, :, :], ACT.Ln).then_inc(A, 1)
            act.wait_ge(V, 21)
            for g in range(GROUPS):
                nc.scalar.activation(sm[:, g, 3], sm[:, g, 3], ACT.Exp).then_inc(A, 1)
                nc.scalar.activation(sm[:, g, 4], alast[:, :, HG * g:HG * (g + 1)], ACT.Exp).then_inc(A, 1)
                nc.scalar.activation(sm[:, g, 5], acs[:, :, HG * g:HG * (g + 1)], ACT.Exp).then_inc(A, 1)

        @block.vector
        def _(dve):
            ch = Chain(dve, V)
            raw, v, e, w, l, q, t, z, sp = (B[n][:, :, :] for n in names)
            nc.vector.memset(sgn[:, 0:SSD_H], 1.0)
            nc.vector.memset(sgn[:, SSD_H:SM], -1.0)
            nc.vector.memset(onesL[:, :], 1.0)
            nc.vector.memset(acs[:, :, :], 0.0)
            ch.link(nc.vector.memset(raw, 0.0))
            dve.wait_ge(pemm, 1)
            nc.vector.tensor_copy(B["raw"][0:META, 0, :], ps[0:META, 0:SM])
            ch.link(nc.vector.tensor_copy(B["raw"][:, 1:, :], ps[:, SM:SM * NCH].rearrange("p (c n) -> p c n", n=SM)))
            dve.wait_ge(w_in, 48)
            bb = brow[:, :].unsqueeze(1).to_broadcast([P, NCH, SM])
            sg = sgn[:, :].unsqueeze(1).to_broadcast([P, NCH, SM])
            tt, ts = nc.vector.tensor_tensor, nc.vector.tensor_scalar
            ch.link(tt(v, raw, bb, ALU.add))
            ch.link(tt(v, v, sg, ALU.mult))
            ch.link(nc.vector.scalar_tensor_tensor(e, v, -1.0, v, ALU.mult, ALU.max))
            dve.wait_ge(A, 2)
            ch.link(ts(w, e, 1.0, None, ALU.add))
            ch.link(ts(t, w, -1.0, 1e-30, ALU.add, ALU.max))
            ch.link(nc.vector.reciprocal(q, t))
            ch.link(tt(q, q, e, ALU.mult))
            ch.link(ts(t, w, 1.0, None, ALU.is_equal))
            ch.link(tt(t, t, e, ALU.mult))
            dve.wait_ge(A, 3)
            ch.link(tt(q, q, l, ALU.mult))
            ch.link(tt(t, t, q, ALU.add))
            ch.link(nc.vector.scalar_tensor_tensor(sp, v, 0.0, t, ALU.max, ALU.add))
            dve.wait_ge(A, 1)
            ch.link(ts(aneg[:, :], aneg[:, :], -1.0, None, ALU.mult))
            tt(adt[:, :, :], B["sp"][:, :, 0:SSD_H], aneg[:, :].unsqueeze(1).to_broadcast([P, NCH, SSD_H]), ALU.mult).then_inc(proj, 1)
            dve.wait_ge(pemm, 2)
            nc.vector.tensor_copy(acs[:, 1:, :], ps[:, 512:768].rearrange("p (c h) -> p c h", h=SSD_H))
            nc.vector.tensor_copy(acs[0:META, 0, :], ps[0:META, 768:800])
            nc.vector.tensor_copy(alast[:, 1:, :], ps[:, 1024:1280].rearrange("p (c h) -> p c h", h=SSD_H))
            nc.vector.tensor_copy(alast[:, 0, :], ps[:, 1280:1312])
            for c in range(NCH):
                a, b = chunk_cols(c)
                o = 1536 + 512 * (c // 3) + P * (c % 3)
                m = nc.vector.tensor_scalar(fT[:, a:b], ps[0:ATT_H, o:o + b - a], 8.0, None, ALU.mult)
            ch.link(m)
            nc.vector.tensor_tensor_scan(ncT[:, :], onesL[:, :], fT[:, :], 0.0, ALU.mult, ALU.add).then_inc(X, 1)
            for g in range(GROUPS):
                h = slice(HG * g, HG * (g + 1))
                nc.vector.tensor_copy(sm[:, g, 0], adt[:, :, h])
                nc.vector.tensor_copy(sm[:, g, 1], acs[:, :, h])
                nc.vector.tensor_copy(sm[:, g, 2], B["sp"][:, :, h])
                ch.link(tt(sm[:, g, 3], alast[:, :, h], acs[:, :, h], ALU.subtract))
            ch.link(nc.vector.memset(onesL[:, 0:1], 1.0))


def ssd_phase(nc, K, u_hi, u_lo, sm):
    NCH, NP = CH + 1, 6 * 3
    with ExitStack() as ctx:
        sb = lambda n, sh, dt=F32: ctx.enter_context(nc.sbuf_tensor(n, sh, dt))
        W = Weights(nc, ctx, "ws", 2)
        raw = sb("conv_in", [P, 2, 3 + L])
        feats = sb("conv_out", [P, 6, L])
        z = sb("z_gate", [P, 4, T])
        seg = sb("decay", [P, 2, HG, P])
        xdt, xst = sb("x_dt", [P, 2, 512]), sb("x_dt_decay", [P, 2, 512])
        ytok, yoff = sb("y_tok", [P, 2, 512]), sb("y_off", [P, 512])
        state = sb("state", [P, 512])
        btok, cb = sb("b_tok", [P, 2, P]), sb("cb", [P, 2, P])
        rms = sb("ssd_rms", [P, T])
        smg = sb("small_g", [P, 6, NCH, HG])
        cpg = sb("conv_par_g", [P, 38])
        par = sb("conv_par", [P, GROUPS, 38])
        s = lambda n: semaphore(nc, ctx, "s1_" + n)
        par_in, small_ok = s("par_in"), s("small_ok")
        proj_ok, raw_ok, conv_ok, silu_ok = s("proj"), s("raw"), s("conv"), s("silu")
        xturn, bturn, sums_ok = s("xturn"), s("bturn"), s("sums")
        zproj, zcopy, zsilu = s("zproj"), s("zcopy"), s("zsilu")
        ydiag_ok, yoff_ok, st_ok, yturn = s("ydiag"), s("yoff"), s("states"), s("yturn")
        xdt_ok, cb_ok, seg_ok, m_ok = s("xdt"), s("cb"), s("seg"), s("m")
        h_ok, t_ok, y_ok, y1_ok = s("h"), s("t"), s("y"), s("y1")
        b_ok, exp_ok, xst_ok = s("btok"), s("exp"), s("xst")
        u_ok, sq_ok, norm_sum, rooted, yf_ok, stored = s("u"), s("sq"), s("normsum"), s("rooted"), s("yf"), s("stored")
        dchain = s("dve_chain")
        block = ctx.enter_context(nc.Block())
        ps = K.psum
        bank = lambda n, w=512: ps[:, 512 * n:512 * n + w]
        w_src = K.d["w_ssd"].rearrange("(g n) p k -> g n p k", g=GROUPS)
        y_dst = K.s["y"].rearrange("(g f) p t -> g f p t", g=GROUPS)

        @block.sync
        def _(sp):
            sp.dma_start(par[:, :, :], K.d["conv_par"]).then_inc(par_in, 16)
            sp.sem_inc(stored, 16)
            W.credits_raw(sp)
            with sp.Fori(0, GROUPS) as g:
                for n in range(10):
                    W.load(sp, g, 10, n, w_src[g, n])
            sp.wait_ge(stored, 64 * GROUPS + 16)

        @block.gpsimd
        def _(pool):
            with pool.Fori(0, GROUPS) as g:
                for n in range(8):
                    W.split(pool, g, 10, n)
                for c in range(8):
                    Lc = META if c == 0 else P
                    pool.wait_ge(xdt_ok, g * 9 + c + 1)
                    if c >= 2:
                        pool.wait_ge(st_ok, g * 8 + c - 1)
                    nc.gpsimd.tensor_tensor(xst[0:Lc, c % 2].rearrange("p (h d) -> p h d", h=HG),
                                            xdt[0:Lc, c % 2].rearrange("p (h d) -> p h d", h=HG),
                                            smg[0:Lc, 3, c].unsqueeze(2).to_broadcast([Lc, HG, 64]), ALU.mult).then_inc(xst_ok, 1)
                    if c == 2:
                        W.split(pool, g, 10, 8)
                    if c == 4:
                        W.split(pool, g, 10, 9)

        @block.tensor
        def _(pe):
            W.credits_used(pe)
            with pe.Fori(0, GROUPS) as g:
                pe.wait_ge(rooted, g * 2 + 2)
                for t in range(6):
                    W.wait(pe, g, 10, t)
                    for j, (a, b) in enumerate(THIRDS):
                        if t >= 2:
                            pe.wait_ge(raw_ok, g * NP + 3 * (t - 2) + j + 1)
                        gemm(nc, bank(3 * (t % 2) + j, b - a), W.hi[:, t % 2], W.lo[:, t % 2],
                             lambda k: u_hi[:, k, a:b], lambda k: u_lo[:, k, a:b]).then_inc(proj_ok, 1)
                    pe.wait_ge(proj_ok, g * NP + 3 * t + 3)
                    pe.sem_inc(W.used, 1)

                def front(c):
                    a, b = chunk_cols(c)
                    n = b - a
                    if c >= 1:
                        pe.wait_ge(xdt_ok, g * 9 + c)
                    for f in range(4):
                        last = nc.tensor.transpose(ps[0:n, 1024 + P * f:1024 + P * f + P], feats[:, f, a:b], K.ident[:, :])
                    last.then_inc(xturn, 1)
                    if c >= 1:
                        pe.wait_ge(b_ok, g * 8 + c)
                    if c >= 2:
                        pe.wait_ge(cb_ok, g * 8 + c - 1)
                    if c <= 7:
                        last = nc.tensor.transpose(ps[0:n, 1536:1536 + P], feats[:, 4, a:b], K.ident[:, :])
                    if c >= 1:
                        last = nc.tensor.matmul(ps[:, 1664:1664 + P], feats[:, 4, a:b], feats[:, 5, a:b], start=True, stop=True)
                    last.then_inc(bturn, 1)
                    if c >= 1:
                        if c >= 2:
                            pe.wait_ge(seg_ok, g * 8 + c - 1)
                        for r in range(HG):
                            last = nc.tensor.matmul(ps[:, 2048 + P * r:2048 + P * (r + 1)],
                                                    smg[:, 0, c, r:r + 1].to_broadcast([P, P]), K.tri[:, :], start=True, stop=True)
                        last.then_inc(sums_ok, 1)

                def zunit(u):
                    t, h = 6 + u // 2, u % 2
                    if h == 0:
                        W.wait(pe, g, 10, t)
                    if u >= 1:
                        pe.wait_ge(zcopy, g * 8 + u)
                    a, b = HALVES[h]
                    gemm(nc, bank(0), W.hi[:, t % 2], W.lo[:, t % 2],
                         lambda k: u_hi[:, k, a:b], lambda k: u_lo[:, k, a:b]).then_inc(zproj, 1)
                    if h == 1:
                        pe.wait_ge(zproj, g * 8 + u + 1)
                        pe.sem_inc(W.used, 1)

                def turn_back(c):
                    pe.wait_ge(y_ok, g * 8 + c)
                    if c >= 2:
                        pe.wait_ge(y1_ok, g * 8 + c - 1)
                    for f in range(4):
                        last = nc.tensor.transpose(ps[:, 512 + P * f:512 + P * (f + 1)], ytok[:, c % 2, P * f:P * (f + 1)], K.ident[:, :])
                    last.then_inc(yturn, 1)

                pe.wait_ge(silu_ok, g * 6 + 6)
                pe.wait_ge(small_ok, g + 1)
                front(0)
                for c in range(NCH):
                    a, b = chunk_cols(c)
                    n = b - a
                    if c < 8:
                        front(c + 1)
                        zunit(c)
                    if c >= 1:
                        pe.wait_ge(m_ok, g * 8 + c)
                        if c >= 2:
                            pe.wait_ge(y_ok, g * 8 + c - 1)
                        for r in range(HG):
                            last = nc.tensor.matmul(ps[:, 3072 + 64 * r:3072 + 64 * (r + 1)], seg[:, c % 2, r],
                                                    xdt[:, c % 2, 64 * r:64 * (r + 1)], start=True, stop=True)
                        last.then_inc(ydiag_ok, 1)
                        pe.wait_ge(h_ok, g * 8 + c)
                        nc.tensor.matmul(bank(7), feats[:, 5, a:b], state[:, :], start=True, stop=True).then_inc(yoff_ok, 1)
                    if c >= 2:
                        turn_back(c - 1)
                    if c <= 7:
                        pe.wait_ge(xst_ok, g * 8 + c + 1)
                        pe.wait_ge(b_ok, g * 8 + c + 1)
                        if c >= 1:
                            pe.wait_ge(t_ok, g * 8 + c)
                        nc.tensor.matmul(bank(7), btok[0:n, c % 2], xst[0:n, c % 2], start=True, stop=True).then_inc(st_ok, 1)
                turn_back(8)
                for f in range(4):
                    pe.wait_ge(sq_ok, g * 4 + f + 1)
                    for h in range(2):
                        last = nc.tensor.matmul(bank(2 + h), K.ones[:, :], raw[:, f % 2, 3 + 512 * h:3 + 512 * (h + 1)],
                                                start=(f == 0), stop=(f == 3))
                    last.then_inc(norm_sum, 1)

        @block.scalar
        def _(act):
            act.sem_inc(rooted, 2)
            with act.Fori(0, GROUPS) as g:
                for t in range(6):
                    act.wait_ge(conv_ok, g * 6 + t + 1)
                    for j, (a, b) in enumerate(THIRDS):
                        act.wait_ge(proj_ok, g * NP + 3 * t + j + 1)
                        nc.scalar.activation(raw[:, t % 2, 3 + a:3 + b], bank(3 * (t % 2) + j, b - a), ACT.Copy).then_inc(raw_ok, 1)
                    if t >= 1:
                        act.wait_ge(conv_ok, g * 6 + t + 2)
                        nc.scalar.activation(feats[:, t - 1], feats[:, t - 1], ACT.Silu).then_inc(silu_ok, 1)
                act.wait_ge(conv_ok, g * 6 + 8)
                nc.scalar.activation(feats[:, 5], feats[:, 5], ACT.Silu).then_inc(silu_ok, 1)
                for c in range(8):
                    act.wait_ge(seg_ok, g * 8 + c + 1)
                    nc.scalar.activation(seg[:, (c + 1) % 2], seg[:, (c + 1) % 2], ACT.Exp).then_inc(exp_ok, 1)
                    act.wait_ge(zproj, g * 8 + c + 1)
                    nc.scalar.activation(z[:, c // 2, 512 * (c % 2):512 * (c % 2 + 1)], bank(0), ACT.Copy).then_inc(zcopy, 1)
                act.wait_ge(zcopy, g * 8 + 8)
                for f in range(4):
                    nc.scalar.activation(z[:, f], z[:, f], ACT.Silu).then_inc(zsilu, 1)
                for f in range(4):
                    act.wait_ge(u_ok, g * 4 + f + 1)
                    if f >= 2:
                        act.wait_ge(norm_sum, g * 4 + f - 1)
                    nc.scalar.activation(raw[:, f % 2, 3:3 + T], feats[:, f, META:L], ACT.Square).then_inc(sq_ok, 1)
                act.wait_ge(norm_sum, g * 4 + 4)
                for h in range(2):
                    nc.scalar.activation(rms[:, 512 * h:512 * (h + 1)], bank(2 + h), ACT.Sqrt, scale=1.0 / 512,
                                         bias=K.eps[:, 0:1]).then_inc(rooted, 1)
                for f in range(4):
                    act.wait_ge(yf_ok, g * 4 + f + 1)
                    act.dma_start(y_dst[g, f], feats[:, f, META:L]).then_inc(stored, 16)

        @block.vector
        def _(dve):
            dve.sem_inc(conv_ok, 2)
            nc.vector.memset(raw[:, :, 0:3], 0.0).then_inc(par_in, 16)
            dve.wait_ge(par_in, 32)
            with dve.Fori(0, GROUPS) as g:
                ch = Chain(dve, dchain, 1 + 6 * 3 + 7 + 1, g)
                tt, stt = nc.vector.tensor_tensor, nc.vector.scalar_tensor_tensor
                nc.vector.tensor_copy(smg[:, :, :, :], sm[:, g])
                ch.link(nc.vector.tensor_copy(cpg[:, :], par[:, g]))
                dve.sem_inc(small_ok, 1)
                dve.wait_ge(stored, g * 64 + 16)
                for t in range(6):
                    w = lambda k: cpg[:, 5 * t + k:5 * t + k + 1]
                    r, o = raw[:, t % 2], feats[:, t]
                    dve.wait_ge(raw_ok, g * NP + 3 * t + 3)
                    ch.link(nc.vector.tensor_scalar(o, r[:, 3:3 + L], w(3), w(4), ALU.mult, ALU.add))
                    ch.link(stt(o, r[:, 2:2 + L], w(2), o, ALU.mult, ALU.add))
                    ch.link(stt(o, r[:, 1:1 + L], w(1), o, ALU.mult, ALU.add))
                    stt(o, r[:, 0:L], w(0), o, ALU.mult, ALU.add).then_inc(conv_ok, 1)

                def make_xdt(c):
                    n = META if c == 0 else P
                    dve.wait_ge(xturn, g * 9 + c + 1)
                    if c >= 2:
                        dve.wait_ge(xst_ok, g * 8 + c - 1)
                    if c >= 3:
                        dve.wait_ge(ydiag_ok, g * 8 + c - 2)
                    tt(xdt[0:n, c % 2].rearrange("p (h d) -> p h d", h=HG), ps[0:n, 1024:1536].rearrange("p (h d) -> p h d", h=HG),
                       smg[0:n, 2, c].unsqueeze(2).to_broadcast([n, HG, 64]), ALU.mult).then_inc(xdt_ok, 1)

                def copy_b(c):
                    n = META if c == 0 else P
                    dve.wait_ge(bturn, g * 9 + c + 1)
                    if c >= 2:
                        dve.wait_ge(st_ok, g * 8 + c - 1)
                    nc.vector.tensor_copy(btok[0:n, c % 2], ps[0:n, 1536:1536 + P]).then_inc(b_ok, 1)

                make_xdt(0)
                copy_b(0)
                for c in range(NCH):
                    a, b = chunk_cols(c)
                    if c < 8:
                        d = c + 1
                        make_xdt(d)
                        if d < 8:
                            copy_b(d)
                        dve.wait_ge(bturn, g * 9 + d + 1)
                        tt(cb[:, d % 2], ps[:, 1664:1664 + P], K.tri[:, :], ALU.mult).then_inc(cb_ok, 1)
                        dve.wait_ge(sums_ok, g * 8 + d)
                        if d >= 3:
                            dve.wait_ge(ydiag_ok, g * 8 + d - 2)
                        for r in range(HG):
                            last = nc.vector.tensor_scalar(seg[:, d % 2, r], ps[:, 2048 + P * r:2048 + P * (r + 1)],
                                                           smg[:, 1, d, r:r + 1], smg[:, 1, d, r:r + 1], ALU.min, ALU.subtract)
                        last.then_inc(seg_ok, 1)
                    if c >= 1:
                        dve.wait_ge(yoff_ok, g * 8 + c)
                        tt(yoff[:, :].rearrange("p (h d) -> p h d", h=HG), bank(7).rearrange("p (h d) -> p h d", h=HG),
                           smg[:, 5, c].unsqueeze(2).to_broadcast([P, HG, 64]), ALU.mult).then_inc(t_ok, 1)
                        dve.wait_ge(t_ok, g * 8 + c)
                        dve.wait_ge(ydiag_ok, g * 8 + c)
                        if c >= 3:
                            dve.wait_ge(yturn, g * 8 + c - 2)
                        tt(ytok[:, c % 2], bank(6), yoff[:, :], ALU.add).then_inc(y_ok, 1)
                    if c <= 7:
                        if c == 0:
                            dve.wait_ge(st_ok, g * 8 + 1)
                            nc.vector.tensor_copy(state[:, :], bank(7)).then_inc(h_ok, 1)
                        else:
                            ch.link(tt(state[:, :].rearrange("p (h d) -> p h d", h=HG), state[:, :].rearrange("p (h d) -> p h d", h=HG),
                                       smg[:, 4, c].unsqueeze(2).to_broadcast([P, HG, 64]), ALU.mult))
                            dve.wait_ge(st_ok, g * 8 + c + 1)
                            tt(state[:, :], state[:, :], bank(7), ALU.add).then_inc(h_ok, 1)
                    if c < 8:
                        dve.wait_ge(exp_ok, g * 8 + c + 1)
                        dve.wait_ge(cb_ok, g * 8 + c + 1)
                        tt(seg[:, (c + 1) % 2], seg[:, (c + 1) % 2], cb[:, (c + 1) % 2].unsqueeze(1).to_broadcast([P, HG, P]),
                           ALU.mult).then_inc(m_ok, 1)
                    for e in ([c - 1] if 2 <= c < 8 else [7, 8] if c == 8 else []):
                        a, b = chunk_cols(e)
                        dve.wait_ge(yturn, g * 8 + e)
                        for f in range(4):
                            last = stt(feats[:, f, a:b], feats[:, f, a:b], cpg[:, 30 + f:31 + f], ps[:, 512 + P * f:512 + P * (f + 1)],
                                       ALU.mult, ALU.add)
                        last.then_inc(y1_ok, 1)
                dve.wait_ge(y1_ok, g * 8 + 8)
                for f in range(4):
                    dve.wait_ge(zsilu, g * 4 + f + 1)
                    tt(feats[:, f, META:L], feats[:, f, META:L], z[:, f], ALU.mult).then_inc(u_ok, 1)
                dve.wait_ge(rooted, g * 2 + 4)
                ch.link(nc.vector.reciprocal(rms[:, :], rms[:, :]))
                dve.wait_ge(sq_ok, g * 4 + 4)
                for f in range(4):
                    stt(feats[:, f, META:L], feats[:, f, META:L], cpg[:, 34 + f:35 + f], rms[:, :], ALU.mult, ALU.mult).then_inc(yf_ok, 1)
                dve.wait_ge(yf_ok, g * 4 + 4)
                assert ch.n == ch.per, ch.n


def ssd_out_phase(nc, K):
    with ExitStack() as ctx:
        sb = lambda n, sh, dt=F32: ctx.enter_context(nc.sbuf_tensor(n, sh, dt))
        W = Weights(nc, ctx, "wo1", 4)
        yraw = sb("yo_raw", [P, 4, 512])
        y_hi, y_lo = sb("yo_hi", [P, 16, 512], F32R), sb("yo_lo", [P, 16, 512], F32R)
        res = sb("yo_out", [P, 2, 512])
        s = lambda n: semaphore(nc, ctx, "so_" + n)
        y_in = [s(f"yin{r}") for r in range(4)]
        hi_ok, lo_ok, done, copied, stored = s("hi"), s("lo"), s("done"), s("copied"), [s("stored0"), s("stored1")]
        block = ctx.enter_context(nc.Block())
        ps = K.psum
        y_src = K.s["y"].rearrange("t p (h c) -> h t p c", h=2)
        out = K.s["pssd"].rearrange("f p (h c) -> h f p c", h=2)

        @block.sync
        def _(sp):
            W.credits_raw(sp)
            with sp.Fori(0, 2) as h:
                for k in range(16):
                    W.load(sp, h, 16, k, K.d["w_proj_ssd"][k])
            for r in range(2):
                sp.wait_ge(stored[r], 16 * 8 + 16)

        @block.gpsimd
        def _(pool):
            with pool.Fori(0, 2) as h:
                for n in range(16):
                    W.split(pool, h, 16, n)

        @block.tensor
        def _(pe):
            W.credits_used(pe)
            with pe.Fori(0, 2) as h:
                for f in range(8):
                    pe.wait_ge(copied, h * 8 + f + 1)
                    for p in range(2):
                        W.wait(pe, h, 16, 2 * f + p)
                        if f == 0:
                            pe.wait_ge(lo_ok, h * 16 + 8 * p + 8 + 4)
                        last = gemm(nc, ps[:, 512 * (f % 4):512 * (f % 4 + 1)], W.hi[:, p], W.lo[:, p],
                                    lambda k: y_hi[:, 8 * p + k], lambda k: y_lo[:, 8 * p + k], first=(p == 0), final=(p == 1))
                        last.then_inc(done, 1)
                        pe.wait_ge(done, h * 16 + 2 * f + p + 1)
                        pe.sem_inc(W.used, 1)

        @block.scalar
        def _(act):
            act.sem_inc(copied, 4)
            for r in range(2):
                act.sem_inc(stored[r], 16)
            with act.Fori(0, 2) as h:
                for k in range(-4, 16):
                    if k >= 0:
                        act.wait_ge(y_in[k % 4], h * 64 + 16 * (k // 4 + 1))
                        nc.scalar.activation(y_hi[:, k], yraw[:, k % 4], ACT.Copy).then_inc(hi_ok, 1)
                    if k + 4 < 16:
                        act.wait_ge(lo_ok, h * 16 + k + 5)
                        act.dma_start(yraw[:, k % 4], y_src[h, k + 4]).then_inc(y_in[k % 4], 16)
                for f in range(8):
                    act.wait_ge(done, h * 16 + 2 * f + 2)
                    act.wait_ge(stored[f % 2], h * 64 + 16 * (f // 2 + 1))
                    nc.scalar.activation(res[:, f % 2], ps[:, 512 * (f % 4):512 * (f % 4 + 1)], ACT.Copy).then_inc(copied, 1)
                    act.wait_ge(copied, h * 8 + f + 5)
                    act.dma_start(out[h, f], res[:, f % 2]).then_inc(stored[f % 2], 16)

        @block.vector
        def _(dve):
            dve.sem_inc(lo_ok, 4)
            with dve.Fori(0, 2) as h:
                for k in range(16):
                    dve.wait_ge(hi_ok, h * 16 + k + 1)
                    nc.vector.tensor_tensor(y_lo[:, k], yraw[:, k % 4], y_hi[:, k].bitcast(F32), ALU.subtract).then_inc(lo_ok, 1)


def pieces_of(n):
    return [(a, min(a + 512, n)) for a in range(0, n, 512)]


def fox_phase(nc, K, u_hi, u_lo):
    PAIRS = ATT_H // 2
    NB = 16
    step = [(b // 8, b % 8) for b in range(NB)]
    keys = lambda i: META + P * (i + 1)
    groups = [[(k0, min(4, i + 2 - k0)) for k0 in range(0, i + 2, 4)] for _, i in step]
    index, d_at, a_at = {}, {}, {}
    for b in range(NB):
        for g in range(len(groups[b])):
            index[b, g] = len(index)
            if g == 1:
                a_at[b, g] = len(a_at) + 1
            else:
                d_at[b, g] = len(d_at) + 1
    NG, ND, NA = len(index), len(d_at), len(a_at)
    order = sorted(index, key=index.get)
    with ExitStack() as ctx:
        sb = lambda n, sh, dt=F32: ctx.enter_context(nc.sbuf_tensor(n, sh, dt))
        W = Weights(nc, ctx, "wf", 4)
        qT, kT, vT, zT = sb("f_qT", [P, T]), sb("f_kT", [P, L]), sb("f_vT", [P, L]), sb("f_zT", [P, T])
        vtok = sb("f_v", [P, CH + 1, P])
        ncb = sb("f_decay", [P, 2, L])
        S = sb("f_scores", [P, 3, L])
        pt = sb("f_pT", [P, 2, 4, P])
        otok = sb("f_o", [P, CH, P])
        yt = sb("f_y", [P, T])
        mx, nm, ls, rl = sb("f_max", [P, NB]), sb("f_negmax", [P, NB]), sb("f_sum", [P, NB]), sb("f_rsum", [P, NB])
        s = lambda n: semaphore(nc, ctx, "f_" + n)
        nc_in, proj, proj_ok, vturn, v_ok = s("decay_in"), s("proj"), s("proj_ok"), s("vturn"), s("v_ok")
        qk_ok, ttr_ok, neg_ok, exp_ok = s("qk"), s("biased"), s("negmax"), s("exp")
        turned, ptd, pta, pv_ok = s("turned"), s("ptd"), s("pta"), s("pv")
        carried = s("carried")
        rl_ok, o_ok, oturn, y_ok, stored = s("rl"), s("o"), s("oturn"), s("y"), s("stored")
        block = ctx.enter_context(nc.Block())
        ps = K.psum
        sbase = lambda i: 0 if i % 2 else 1536
        w_src = K.d["w_fox"].rearrange("(g n) p k -> g n p k", g=PAIRS)
        nc_src = K.s["nc"].rearrange("(g j) l -> g j l", g=PAIRS)
        units = [(0, a, b, qT[:, a - META:b - META]) for a, b in HALVES] + [(1, a, b, kT[:, a:b]) for a, b in THIRDS] + \
                [(2, a, b, vT[:, a:b]) for a, b in THIRDS] + [(3, a, b, zT[:, a - META:b - META]) for a, b in HALVES]
        NU = len(units)

        @block.sync
        def _(sp):
            W.credits_raw(sp)
            with sp.Fori(0, PAIRS) as h:
                for n in range(4):
                    W.load(sp, h, 4, n, w_src[h, n])
                sp.wait_ge(ttr_ok, h * NB + NB)
                for j in range(2):
                    sp.dma_start(ncb[:, j], nc_src[h, j:j + 1].to_broadcast([P, L])).then_inc(nc_in, 16)
            sp.wait_ge(stored, 16 * PAIRS + 16)

        @block.gpsimd
        def _(pool):
            with pool.Fori(0, PAIRS) as h:
                for n in range(4):
                    W.split(pool, h, 4, n)

        @block.tensor
        def _(pe):
            W.credits_used(pe)
            with pe.Fori(0, PAIRS) as h:
                pe.wait_ge(y_ok, h * 2 + 2)
                for u, (t, a, b, _) in enumerate(units):
                    if u == 0 or units[u - 1][0] != t:
                        W.wait(pe, h, 4, t)
                    if u >= 5:
                        pe.wait_ge(proj_ok, h * NU + u - 4)
                    gemm(nc, ps[:, 512 * (u % 5):512 * (u % 5) + b - a], W.hi[:, t % 2], W.lo[:, t % 2],
                         lambda k: u_hi[:, k, a:b], lambda k: u_lo[:, k, a:b]).then_inc(proj, 1)
                    if u + 1 == NU or units[u + 1][0] != t:
                        pe.wait_ge(proj, h * NU + u + 1)
                        pe.sem_inc(W.used, 1)
                pe.wait_ge(proj_ok, h * NU + NU)
                for c in range(CH + 1):
                    a, b = (META + P * c, META + P * (c + 1)) if c < CH else (0, META)
                    last = nc.tensor.transpose(ps[0:b - a, 2560 + P * c:2560 + P * (c + 1)], vT[:, a:b], K.ident[:, :])
                last.then_inc(vturn, 1)

                def scores(b):
                    j, i = step[b]
                    if b >= 2:
                        pe.wait_ge(ttr_ok, h * NB + NB + b - 1)
                    d0, d1 = META + P * i, META + P * (i + 1)
                    for a, e in pieces_of(keys(i)):
                        masked = d0 < e and d1 > a
                        last = nc.tensor.matmul(ps[:, sbase(i) + a:sbase(i) + e], qT[64 * j:64 * j + 64, P * i:P * (i + 1)],
                                                kT[64 * j:64 * j + 64, a:e], start=True, stop=not masked)
                        if masked:
                            x, y = max(a, d0), min(e, d1)
                            last = nc.tensor.matmul(ps[:, sbase(i) + x:sbase(i) + y], K.identb[:, :],
                                                    K.maskb[:, x - d0:y - d0], start=False, stop=True)
                    last.then_inc(qk_ok, 1)

                def turn(b, g):
                    x = index[b, g]
                    k0, n = groups[b][g]
                    if g == 0:
                        pe.wait_ge(exp_ok, h * NB + b + 1)
                    if x >= 2:
                        wait_copy(pe, x - 2)
                    for m in range(n):
                        c = 0 if k0 + m == 0 else META + P * (k0 + m - 1)
                        last = nc.tensor.transpose(ps[:, 2560 + 512 * (x % 2) + P * m:2560 + 512 * (x % 2) + P * (m + 1)],
                                                   S[:, b % 3, c:c + P], K.ident[:, :])
                    last.then_inc(turned, 1)

                def wait_copy(eng, x):
                    if order[x] in a_at:
                        eng.wait_ge(pta, h * NA + a_at[order[x]])
                    else:
                        eng.wait_ge(ptd, h * ND + d_at[order[x]])

                def values(b, g):
                    x = index[b, g]
                    j, i = step[b]
                    k0, n = groups[b][g]
                    if g == 0 and b >= 1:
                        pe.wait_ge(o_ok, h * NB + b)
                    if g == 0 and b == 0:
                        pe.wait_ge(v_ok, h * 2 + 2)
                    wait_copy(pe, x)
                    for m in range(n):
                        kb = k0 + m
                        rows, c = (META, CH) if kb == 0 else (P, kb - 1)
                        last = nc.tensor.matmul(ps[:, 3584:3648], pt[0:rows, x % 2, m], vtok[0:rows, c, 64 * j:64 * j + 64],
                                                start=(kb == 0), stop=(kb == i + 1))
                    last.then_inc(pv_ok, 1)

                scores(0)
                scores(1)
                pe.wait_ge(v_ok, h * 2 + 2)
                for b in range(NB):
                    n = len(groups[b])
                    turn(b, 0)
                    if n > 1:
                        turn(b, 1)
                    if b + 2 < NB:
                        scores(b + 2)
                    values(b, 0)
                    if n > 2:
                        turn(b, 2)
                    if n > 1:
                        values(b, 1)
                    if n > 2:
                        values(b, 2)
                for hf in range(2):
                    pe.wait_ge(o_ok, h * NB + NB)
                    for m in range(4):
                        last = nc.tensor.transpose(ps[:, 512 * hf + P * m:512 * hf + P * (m + 1)], otok[:, 4 * hf + m], K.ident[:, :])
                    last.then_inc(oturn, 1)

        @block.scalar
        def _(act):
            with act.Fori(0, PAIRS) as h:
                for u, (t, a, b, dst) in enumerate(units):
                    act.wait_ge(proj, h * NU + u + 1)
                    nc.scalar.activation(dst, ps[:, 512 * (u % 5):512 * (u % 5) + b - a], ACT.Silu if t == 3 else ACT.Copy).then_inc(proj_ok, 1)
                act.wait_ge(vturn, h + 1)
                nc.scalar.activation(vtok[:, 0:CH].rearrange("p c n -> p (c n)"), ps[:, 2560:3584], ACT.Copy).then_inc(v_ok, 1)
                nc.scalar.activation(vtok[0:META, CH], ps[0:META, 3584:3584 + P], ACT.Copy).then_inc(v_ok, 1)

                def exps(b):
                    n = keys(step[b][1])
                    act.wait_ge(neg_ok, h * NB + b + 1)
                    nc.scalar.activation(S[:, b % 3, 0:n], S[:, b % 3, 0:n], ACT.Exp, bias=nm[:, b:b + 1],
                                         accum_out=ls[:, b:b + 1]).then_inc(exp_ok, 1)

                exps(0)
                exps(1)
                for b in range(NB):
                    if (b, 1) in a_at:
                        x, n = index[b, 1], groups[b][1][1]
                        act.wait_ge(turned, h * NG + x + 1)
                        act.wait_ge(pv_ok, h * NG + x - 1)
                        nc.scalar.activation(pt[:, x % 2, 0:n], ps[:, 2560 + 512 * (x % 2):2560 + 512 * (x % 2) + P * n]
                                             .rearrange("p (m n) -> p m n", n=P), ACT.Copy).then_inc(pta, 1)
                    if b + 2 < NB:
                        exps(b + 2)
                act.wait_ge(y_ok, h * 2 + 4)
                act.dma_start(K.s["yatt"][h], yt[:, :]).then_inc(stored, 16)

        @block.vector
        def _(dve):
            dve.sem_inc(ttr_ok, NB)
            dve.sem_inc(y_ok, 2)
            dve.sem_inc(stored, 16)
            with dve.Fori(0, PAIRS) as h:
                def bias(b):
                    j, i = step[b]
                    n = keys(i)
                    if b in (0, 8):
                        dve.wait_ge(nc_in, h * 32 + 32)
                    dve.wait_ge(qk_ok, h * NB + b + 1)
                    if b >= 3:
                        dve.wait_ge(turned, h * NG + index[b - 3, len(groups[b - 3]) - 1] + 1)
                    dve.sem_inc(carried, 1)
                    nc.vector.tensor_tensor_reduce(out=S[:, b % 3, 0:n], in0=ps[:, sbase(i):sbase(i) + n], in1=ncb[:, j, 0:n],
                                                   scale=0.125, scalar=-3e38, op0=ALU.add, op1=ALU.max,
                                                   accum_out=mx[:, b:b + 1]).then_inc(ttr_ok, 1)
                    dve.wait_ge(ttr_ok, h * NB + NB + b + 1)
                    nc.vector.tensor_scalar(nm[:, b:b + 1], mx[:, b:b + 1], -1.0, None, ALU.mult).then_inc(neg_ok, 1)

                def copy(b, g):
                    x, n = index[b, g], groups[b][g][1]
                    dve.wait_ge(turned, h * NG + x + 1)
                    if x >= 2:
                        dve.wait_ge(pv_ok, h * NG + x - 1)
                    nc.vector.tensor_copy(pt[:, x % 2, 0:n], ps[:, 2560 + 512 * (x % 2):2560 + 512 * (x % 2) + P * n]
                                          .rearrange("p (m n) -> p m n", n=P)).then_inc(ptd, 1)

                bias(0)
                bias(1)
                for b in range(NB):
                    j, i = step[b]
                    copy(b, 0)
                    if b + 2 < NB:
                        bias(b + 2)
                    if (b, 2) in d_at:
                        copy(b, 2)
                    dve.wait_ge(exp_ok, h * NB + b + 1)
                    nc.vector.reciprocal(rl[:, b:b + 1], ls[:, b:b + 1]).then_inc(rl_ok, 1)
                    dve.wait_ge(rl_ok, h * NB + b + 1)
                    dve.wait_ge(pv_ok, h * NG + index[b, len(groups[b]) - 1] + 1)
                    nc.vector.tensor_scalar(otok[:, i, 64 * j:64 * j + 64], ps[:, 3584:3648], rl[:, b:b + 1], None,
                                            ALU.mult).then_inc(o_ok, 1)
                dve.wait_ge(stored, h * 16 + 16)
                for hf in range(2):
                    dve.wait_ge(oturn, h * 2 + hf + 1)
                    nc.vector.tensor_tensor(yt[:, 512 * hf:512 * (hf + 1)], ps[:, 512 * hf:512 * (hf + 1)],
                                            zT[:, 512 * hf:512 * (hf + 1)], ALU.mult).then_inc(y_ok, 1)


def merge_phase(nc, K, u_hi, u_lo):
    with ExitStack() as ctx:
        sb = lambda n, sh, dt=F32: ctx.enter_context(nc.sbuf_tensor(n, sh, dt))
        W = Weights(nc, ctx, "wm", 3)
        raw = sb("m_raw", [P, 2, T])
        y_hi, y_lo = sb("m_yhi", [P, KT, T], F32R), sb("m_ylo", [P, KT, T], F32R)
        pssd = sb("m_pssd", [P, 2, T])
        sg, sa = sb("m_sg", [P, T]), sb("m_sa", [P, T])
        bias = sb("m_bias", [P, 2 * KT])
        s = lambda n: semaphore(nc, ctx, "m_" + n)
        y_in, hi_ok, lo_ok, p_in = [s("yin0"), s("yin1")], s("hi"), s("lo"), [s("pin0"), s("pin1")]
        b_in, unit, sig_ok, g1_ok, g2_ok, gm, m_ok = s("bin"), s("unit"), s("sig"), s("g1"), s("g2"), s("gm"), s("m")
        stored = [s("stored0"), s("stored1")]
        block = ctx.enter_context(nc.Block())
        ps = K.psum
        w_src = K.d["w_merge"].rearrange("(g n) p k -> g n p k", n=6)

        def store(act, f):
            act.wait_ge(m_ok, f + 1)
            act.dma_start(K.s["merged"][f], pssd[:, f % 2]).then_inc(stored[f % 2], 16)
            if f + 2 < KT:
                act.wait_ge(stored[f % 2], 16 * (f // 2 + 1))
                act.dma_start(pssd[:, f % 2], K.s["pssd"][f + 2]).then_inc(p_in[f % 2], 16)

        @block.sync
        def _(sp):
            W.credits_raw(sp)
            sp.dma_start(bias[:, :], K.d["gate_bias"]).then_inc(b_in, 16)
            with sp.Fori(0, 4) as g:
                for n in range(6):
                    W.load(sp, g, 6, n, w_src[g, n])

        @block.gpsimd
        def _(pool):
            with pool.Fori(0, 4) as g:
                for n in range(6):
                    W.split(pool, g, 6, n)

        @block.tensor
        def _(pe):
            W.credits_used(pe)
            with pe.Fori(0, 4) as g:
                for q in range(2):
                    for n in range(3):
                        W.wait(pe, g, 6, 3 * q + n)
                        if n < 2:
                            pe.wait_ge(sig_ok, g * 8 + 4 * q + 2 * n + 2)
                        else:
                            pe.wait_ge(g2_ok, g * 4 + 2 * q + 2)
                            if q == 0:
                                pe.wait_ge(lo_ok, KT)
                        wl, wh = W.lo[:, (3 * q + n) % 2], W.hi[:, (3 * q + n) % 2]
                        for h in range(2):
                            if n < 2:
                                act_hi = lambda k: u_hi[:, k, META + 512 * h:META + 512 * (h + 1)]
                                act_lo = lambda k: u_lo[:, k, META + 512 * h:META + 512 * (h + 1)]
                            else:
                                act_hi = lambda k: y_hi[:, k, 512 * h:512 * (h + 1)]
                                act_lo = lambda k: y_lo[:, k, 512 * h:512 * (h + 1)]
                            gemm(nc, ps[:, 1024 * n + 512 * h:1024 * n + 512 * (h + 1)], wh, wl, act_hi, act_lo).then_inc(unit, 1)
                        pe.wait_ge(unit, g * 12 + 6 * q + 2 * n + 2)
                        pe.sem_inc(W.used, 1)

        @block.scalar
        def _(act):
            act.sem_inc(sig_ok, 4)
            for k in range(2):
                act.dma_start(raw[:, k], K.s["yatt"][k]).then_inc(y_in[k], 16)
                act.dma_start(pssd[:, k], K.s["pssd"][k]).then_inc(p_in[k], 16)
            for k in range(KT):
                act.wait_ge(y_in[k % 2], 16 * (k // 2 + 1))
                nc.scalar.activation(y_hi[:, k], raw[:, k % 2], ACT.Copy).then_inc(hi_ok, 1)
                if k + 2 < KT:
                    act.wait_ge(lo_ok, k + 1)
                    act.dma_start(raw[:, k % 2], K.s["yatt"][k + 2]).then_inc(y_in[k % 2], 16)
            act.wait_ge(b_in, 16)
            for f in range(KT):
                for n in range(2):
                    for h in range(2):
                        act.wait_ge(unit, 6 * f + 2 * n + h + 1)
                        if f >= 1:
                            act.wait_ge(g1_ok if n == 0 else g2_ok, 2 * f if n == 0 else 2 * f + 2)
                        nc.scalar.activation((sa if n else sg)[:, 512 * h:512 * (h + 1)], ps[:, 1024 * n + 512 * h:1024 * n + 512 * (h + 1)],
                                             ACT.Sigmoid, bias=bias[:, KT * n + f:KT * n + f + 1]).then_inc(sig_ok, 1)
                if f >= 1:
                    store(act, f - 1)
            store(act, KT - 1)
            for f in (KT - 2, KT - 1):
                act.wait_ge(stored[f % 2], 64)

        @block.vector
        def _(dve):
            dve.sem_inc(g2_ok, 2)
            for k in range(KT):
                dve.wait_ge(hi_ok, k + 1)
                nc.vector.tensor_tensor(y_lo[:, k], raw[:, k % 2], y_hi[:, k].bitcast(F32), ALU.subtract).then_inc(lo_ok, 1)
            for f in range(KT):
                dve.wait_ge(p_in[f % 2], 16 * (f // 2 + 1))
                p = pssd[:, f % 2]
                for h in range(2):
                    c = slice(512 * h, 512 * (h + 1))
                    dve.wait_ge(sig_ok, 4 + 4 * f + h + 1)
                    nc.vector.tensor_tensor(p[:, c], p[:, c], sg[:, c], ALU.mult).then_inc(g1_ok, 1)
                for h in range(2):
                    c = slice(512 * h, 512 * (h + 1))
                    dve.wait_ge(unit, 6 * f + 4 + h + 1)
                    dve.wait_ge(sig_ok, 4 + 4 * f + 2 + h + 1)
                    nc.vector.tensor_tensor(sa[:, c], sa[:, c], ps[:, 2048 + 512 * h:2048 + 512 * (h + 1)], ALU.mult).then_inc(gm, 1)
                    dve.wait_ge(gm, 2 * f + h + 1)
                    dve.wait_ge(g1_ok, 2 * f + h + 1)
                    last = nc.vector.tensor_tensor(p[:, c], p[:, c], sa[:, c], ALU.add)
                    last.then_inc(g2_ok, 1)
                dve.wait_ge(g2_ok, 2 * f + 4)
                dve.sem_inc(m_ok, 1)


def linear_phase(nc, K, name, src, w_src, dst, raw_slots=4):
    with ExitStack() as ctx:
        sb = lambda n, sh, dt=F32: ctx.enter_context(nc.sbuf_tensor(name + n, sh, dt))
        W = Weights(nc, ctx, name + "w", raw_slots)
        raw = sb("_raw", [P, 4, T])
        a_hi, a_lo = sb("_hi", [P, KT, T], F32R), sb("_lo", [P, KT, T], F32R)
        s = lambda n: semaphore(nc, ctx, name + n)
        a_in, hi_ok, lo_ok, unit, copied = [s(f"_in{r}") for r in range(4)], s("_hi_ok"), s("_lo_ok"), s("_unit"), s("_copied")
        block = ctx.enter_context(nc.Block())
        ps = K.psum

        @block.sync
        def _(sp):
            W.credits_raw(sp)
            for k in range(2):
                W.load(sp, 0, 8, k, w_src[k])
            for k in range(KT):
                if k >= 4:
                    sp.wait_ge(lo_ok, k - 3)
                sp.dma_start(raw[:, k % 4], src[k]).then_inc(a_in[k % 4], 16)
            for k in range(2, KT):
                W.load(sp, 0, 8, k, w_src[k])

        @block.gpsimd
        def _(pool):
            for n in range(KT):
                W.split(pool, 0, 8, n)

        @block.tensor
        def _(pe):
            W.credits_used(pe)
            pe.wait_ge(lo_ok, KT)
            for f in range(KT):
                W.wait(pe, 0, 8, f)
                for h in range(2):
                    u = 2 * f + h
                    if u >= 8:
                        pe.wait_ge(copied, u - 7)
                    gemm(nc, ps[:, 512 * (u % 8):512 * (u % 8 + 1)], W.hi[:, f % 2], W.lo[:, f % 2],
                         lambda k: a_hi[:, k, 512 * h:512 * (h + 1)], lambda k: a_lo[:, k, 512 * h:512 * (h + 1)]).then_inc(unit, 1)
                pe.wait_ge(unit, 2 * f + 2)
                pe.sem_inc(W.used, 1)

        @block.scalar
        def _(act):
            for k in range(KT):
                act.wait_ge(a_in[k % 4], 16 * (k // 4 + 1))
                nc.scalar.activation(a_hi[:, k], raw[:, k % 4], ACT.Copy).then_inc(hi_ok, 1)
            for u in range(2 * KT):
                act.wait_ge(unit, u + 1)
                nc.scalar.activation(dst[:, u // 2, 512 * (u % 2):512 * (u % 2 + 1)], ps[:, 512 * (u % 8):512 * (u % 8 + 1)],
                                     ACT.Copy).then_inc(copied, 1)

        @block.vector
        def _(dve):
            for k in range(KT):
                dve.wait_ge(hi_ok, k + 1)
                nc.vector.tensor_tensor(a_lo[:, k], raw[:, k % 4], a_hi[:, k].bitcast(F32), ALU.subtract).then_inc(lo_ok, 1)


def residual_phase(nc, K, o, gain, xr):
    with ExitStack() as ctx:
        sb = lambda n, sh, dt=F32: ctx.enter_context(nc.sbuf_tensor(n, sh, dt))
        sq, rs = sb("r_sq", [P, 2, T]), sb("r_rs", [P, T])
        s = lambda n: semaphore(nc, ctx, "r_" + n)
        x_in, squared, summed, rooted, inv, scaled, added = (s(n) for n in ["xin", "squared", "summed", "rooted", "inv", "scaled", "added"])
        block = ctx.enter_context(nc.Block())
        ps = K.psum

        @block.sync
        def _(sp):
            sp.dma_start(xr[:, :, :], K.s["xT"].rearrange("k p t -> p k t")).then_inc(x_in, 16)

        @block.scalar
        def _(act):
            for k in range(KT):
                if k >= 2:
                    act.wait_ge(summed, k - 1)
                nc.scalar.activation(sq[:, k % 2], o[:, k], ACT.Square).then_inc(squared, 1)
            act.wait_ge(summed, KT)
            for h in range(2):
                nc.scalar.activation(rs[:, 512 * h:512 * (h + 1)], ps[:, 512 * h:512 * (h + 1)], ACT.Sqrt, scale=1.0 / D,
                                     bias=K.eps[:, 0:1]).then_inc(rooted, 1)

        @block.tensor
        def _(pe):
            for k in range(KT):
                pe.wait_ge(squared, k + 1)
                for h in range(2):
                    last = nc.tensor.matmul(ps[:, 512 * h:512 * (h + 1)], K.ones[:, :], sq[:, k % 2, 512 * h:512 * (h + 1)],
                                            start=(k == 0), stop=(k == KT - 1))
                last.then_inc(summed, 1)

        @block.vector
        def _(dve):
            dve.wait_ge(rooted, 2)
            nc.vector.reciprocal(rs[:, :], rs[:, :]).then_inc(inv, 1)
            dve.wait_ge(inv, 1)
            for k in range(KT):
                nc.vector.scalar_tensor_tensor(o[:, k], o[:, k], gain[:, k:k + 1], rs[:, :], ALU.mult, ALU.mult).then_inc(scaled, 1)
            dve.wait_ge(x_in, 16)
            for k in range(KT):
                dve.wait_ge(scaled, k + 1)
                nc.vector.tensor_tensor(xr[:, k], xr[:, k], o[:, k], ALU.add).then_inc(added, 1)


def mixer_phase(nc, K, name, dil, u_hi, u_lo):
    NPASS, NB, NI = 4, 16, 8
    step = [(b // 8, b % 8) for b in range(NB)] if dil else [(b % 2, b // 2) for b in range(NB)]
    LEN = 2 * T - P
    NT = NB if dil else NI
    VW = 64 if dil else P
    with ExitStack() as ctx:
        sb = lambda n, sh, dt=F32: ctx.enter_context(nc.sbuf_tensor(name + n, sh, dt))
        W = Weights(nc, ctx, name + "w", 2)
        qk, vT, zT = sb("_qk", [P, 2, T]), sb("_vT", [P, T]), sb("_zT", [P, T])
        vtok = sb("_v", [P, CH, P])
        dist = sb("_dist", [P, LEN])
        count = sb("_count", [P, LEN]) if dil else None
        bias = sb("_bias", [P, 2 if dil else 1, LEN])
        slopes = sb("_slopes", [P, 8])
        par = sb("_par", [P, 3])
        S = sb("_scores", [P, 4, T])
        sq, rs = S[:, 0:2], S[:, 2:4]
        pt = sb("_pT", [P, 2, 4, P])
        otok = sb("_o", [P, CH, P])
        osq = sb("_osq", [P, P])
        yt = vT
        mx, nm, ls, rl = (sb(n, [P, NB]) for n in ("_max", "_negmax", "_sum", "_rsum"))
        oss, ors = sb("_oss", [P, NI]), sb("_ors", [P, NI])
        s = lambda n: semaphore(nc, ctx, name + n)
        par_in, proj, proj_ok, squared, summed, rooted, inv, qk_ready = (s("_" + n) for n in
            ["par", "proj", "proj_ok", "squared", "summed", "rooted", "inv", "qk_ready"])
        vturn, v_ok, bias_ok, qk_ok, ttr_ok, neg_ok, exp_ok, carried = (s("_" + n) for n in
            ["vturn", "v_ok", "bias_ok", "qk_ok", "ttr", "neg", "exp", "carried"])
        turned, pt0, pt1, pv_ok, rl_ok, part_ok, w_ok, o_ok, ss_ok, or_ok, on_ok, oturn, y_ok, stored = (s("_" + n) for n in
            ["turned", "pt0", "pt1", "pv", "rl", "part", "w", "o", "ss", "or", "on", "oturn", "y", "stored"])
        block = ctx.enter_context(nc.Block())
        ps = K.psum
        w_src = (K.d["w_dil"] if dil else K.d["w_diff"]).rearrange("(g n) p k -> g n p k", g=NPASS)
        tile0 = 4 if dil else 0
        y_dst = K.s["mix"]
        units = [(t, 512 * h, 512 * (h + 1)) for t in range(4) for h in range(2)]
        n_par = 4 if dil else 3

        @block.sync
        def _(sp):
            W.credits_raw(sp)
            sp.dma_start(dist[:, :], K.d["dist"]).then_inc(par_in, 16)
            if dil:
                sp.dma_start(count[:, :], K.d["count"]).then_inc(par_in, 16)
            sp.dma_start(slopes[:, :], K.d["slopes_dil"] if dil else K.d["slopes_diff"]).then_inc(par_in, 16)
            sp.dma_start(par[:, :], K.d["par_dil"] if dil else K.d["par_diff"]).then_inc(par_in, 16)
            with sp.Fori(0, NPASS) as h:
                for n in range(4):
                    W.load(sp, h, 4, n, w_src[h, n])

        @block.gpsimd
        def _(pool):
            with pool.Fori(0, NPASS) as h:
                for n in range(4):
                    W.split(pool, h, 4, n)

        @block.tensor
        def _(pe):
            W.credits_used(pe)
            with pe.Fori(0, NPASS) as h:
                pe.wait_ge(y_ok, h * 2 + 2)
                for u, (t, a, b) in enumerate(units):
                    if u % 2 == 0:
                        W.wait(pe, h, 4, t)
                    if u >= 4:
                        pe.wait_ge(proj_ok, h * 8 + u - 3)
                    gemm(nc, ps[:, 512 * (u % 4):512 * (u % 4 + 1)], W.hi[:, t % 2], W.lo[:, t % 2],
                         lambda k: u_hi[:, k, a:b], lambda k: u_lo[:, k, a:b]).then_inc(proj, 1)
                    if u % 2 == 1:
                        pe.wait_ge(proj, h * 8 + u + 1)
                        pe.sem_inc(W.used, 1)
                    if u in (3, 5):
                        m = (u - 3) // 2
                        pe.wait_ge(squared, h * 2 + m + 1)
                        for f in range(2):
                            last = nc.tensor.matmul(ps[:, 2048 + 1024 * m + 512 * f:2048 + 1024 * m + 512 * (f + 1)], K.pairs[:, :],
                                                    sq[:, m, 512 * f:512 * (f + 1)], start=True, stop=True)
                        last.then_inc(summed, 1)
                pe.wait_ge(proj_ok, h * 8 + 6)
                pe.wait_ge(rooted, h * 2 + 2)
                for c in range(CH):
                    last = nc.tensor.transpose(ps[:, 2048 + P * c:2048 + P * (c + 1)], vT[:, P * c:P * (c + 1)], K.ident[:, :])
                last.then_inc(vturn, 1)
                pe.wait_ge(proj_ok, h * 8 + 8)
                pe.wait_ge(qk_ready, h * 2 + 2)

                def scores(b):
                    j, i = step[b]
                    if b >= 2:
                        pe.wait_ge(ttr_ok, h * NB + b - 1)
                    for f in range(2):
                        last = nc.tensor.matmul(ps[:, 1024 * (b % 2) + 512 * f:1024 * (b % 2) + 512 * (f + 1)],
                                                qk[64 * j:64 * j + 64, 0, P * i:P * (i + 1)],
                                                qk[64 * j:64 * j + 64, 1, 512 * f:512 * (f + 1)], start=True, stop=True)
                    last.then_inc(qk_ok, 1)

                def turn(r, g):
                    x = 2 * r + g
                    slot = r % 4 if dil else 2 * r % 4
                    if g == 0:
                        pe.wait_ge(exp_ok if dil else w_ok, h * NT + r + 1)
                    if r >= 1:
                        pe.wait_ge(pt1 if g else pt0, h * NT + r)
                    for m in range(4):
                        last = nc.tensor.transpose(ps[:, 2048 + 512 * g + P * m:2048 + 512 * g + P * (m + 1)],
                                                   S[:, slot, 512 * g + P * m:512 * g + P * (m + 1)], K.ident[:, :])
                    last.then_inc(turned, 1)

                def values(r, g):
                    j = step[r][0] if dil else 0
                    if g == 0 and r >= 1:
                        pe.wait_ge(o_ok, h * NT + r)
                    pe.wait_ge(pt1 if g else pt0, h * NT + r + 1)
                    for m in range(4):
                        last = nc.tensor.matmul(ps[:, 3072:3072 + VW], pt[:, g, m], vtok[:, 4 * g + m, 64 * j:64 * j + VW],
                                                start=(g == 0 and m == 0), stop=(g == 1 and m == 3))
                    last.then_inc(pv_ok, 1)

                scores(0)
                scores(1)
                pe.wait_ge(v_ok, h + 1)
                for r in range(NT):
                    nxt = [r + 2] if dil else [2 * r + 2, 2 * r + 3]
                    turn(r, 0)
                    turn(r, 1)
                    if nxt[0] < NB:
                        scores(nxt[0])
                    values(r, 0)
                    if len(nxt) > 1 and nxt[1] < NB:
                        scores(nxt[1])
                    values(r, 1)
                for hf in range(2):
                    pe.wait_ge(o_ok if dil else on_ok, h * NT + NT if dil else h + 1)
                    for m in range(4):
                        last = nc.tensor.transpose(ps[:, 512 * hf + P * m:512 * hf + P * (m + 1)], otok[:, 4 * hf + m], K.ident[:, :])
                    last.then_inc(oturn, 1)

        @block.scalar
        def _(act):
            with act.Fori(0, NPASS) as h:
                for u, (t, a, b) in enumerate(units):
                    if u == 4:
                        act.wait_ge(stored, h * 16 + 16)
                    act.wait_ge(proj, h * 8 + u + 1)
                    dst = [qk[:, 0, a:b], qk[:, 1, a:b], vT[:, a:b], zT[:, a:b]][t]
                    nc.scalar.activation(dst, ps[:, 512 * (u % 4):512 * (u % 4 + 1)], ACT.Silu if t == 3 else ACT.Copy).then_inc(proj_ok, 1)
                    if u in (1, 3):
                        m = u // 2
                        act.wait_ge(proj_ok, h * 8 + u + 1)
                        nc.scalar.activation(sq[:, m], qk[:, m], ACT.Square).then_inc(squared, 1)
                    if u == 5:
                        for m in range(2):
                            act.wait_ge(summed, h * 2 + m + 1)
                            nc.scalar.activation(rs[:, m], ps[:, 2048 + 1024 * m:3072 + 1024 * m], ACT.Sqrt, scale=1.0 / 64,
                                                 bias=K.eps[:, 0:1]).then_inc(rooted, 1)
                act.wait_ge(vturn, h + 1)
                nc.scalar.activation(vtok[:, :, :].rearrange("p c n -> p (c n)"), ps[:, 2048:3072], ACT.Copy).then_inc(v_ok, 1)

                def exps(b):
                    act.wait_ge(neg_ok, h * NB + b + 1)
                    nc.scalar.activation(S[:, b % 4], S[:, b % 4], ACT.Exp, bias=nm[:, b:b + 1],
                                         accum_out=ls[:, b:b + 1]).then_inc(exp_ok, 1)

                def copy(r, g):
                    act.wait_ge(turned, h * 2 * NT + 2 * r + g + 1)
                    if r >= 1:
                        act.wait_ge(pv_ok, h * 2 * NT + 2 * r - 1 + g)
                    nc.scalar.activation(pt[:, g].rearrange("p m n -> p (m n)"), ps[:, 2048 + 512 * g:2048 + 512 * (g + 1)],
                                         ACT.Copy).then_inc(pt1 if g else pt0, 1)

                exps(0)
                exps(1)
                for r in range(NT):
                    if not dil:
                        copy(r, 0)
                    copy(r, 1)
                    for b in ([r + 2] if dil else [2 * r + 2, 2 * r + 3]):
                        if b < NB:
                            exps(b)
                    if not dil:
                        act.wait_ge(o_ok, h * NT + r + 1)
                        nc.scalar.activation(osq[:, :], otok[:, r], ACT.Square, accum_out=oss[:, r:r + 1]).then_inc(ss_ok, 1)
                        act.wait_ge(ss_ok, h * (NT + 1) + r + 1)
                if not dil:
                    nc.scalar.activation(oss[:, :], oss[:, :], ACT.Sqrt, scale=1.0 / P, bias=K.eps[:, 0:1]).then_inc(ss_ok, 1)
                act.wait_ge(y_ok, h * 2 + 4)
                act.dma_start(y_dst[tile0:tile0 + 4][h], yt[:, :]).then_inc(stored, 16)
            act.wait_ge(stored, 16 * NPASS + 16)

        @block.vector
        def _(dve):
            dve.sem_inc(y_ok, 2)
            dve.sem_inc(stored, 16)
            dve.wait_ge(par_in, 16 * n_par)
            stt, tt = nc.vector.scalar_tensor_tensor, nc.vector.tensor_tensor
            with dve.Fori(0, NPASS) as h:
                for m in range(2 if dil else 1):
                    if dil:
                        stt(bias[:, m], dist[:, :], slopes.rearrange("p (h m) -> p h m", m=2)[:, h, m:m + 1], count[:, :],
                            ALU.mult, ALU.add).then_inc(bias_ok, 1)
                    else:
                        nc.vector.tensor_scalar(bias[:, m], dist[:, :], slopes[:, bass.ds(h, 1)], None, ALU.mult).then_inc(bias_ok, 1)
                for m in range(2):
                    dve.wait_ge(rooted, h * 2 + m + 1)
                    nc.vector.reciprocal(rs[:, m], rs[:, m]).then_inc(inv, 1)
                    dve.wait_ge(inv, h * 2 + m + 1)
                    dve.wait_ge(squared, h * 2 + m + 1)
                    stt(qk[:, m], qk[:, m], par[:, m:m + 1], rs[:, m], ALU.mult, ALU.mult).then_inc(qk_ready, 1)
                dve.wait_ge(bias_ok, h + 1 if not dil else h * 2 + 2)

                def biased(b):
                    j, i = step[b]
                    dve.wait_ge(qk_ok, h * NB + b + 1)
                    if b >= 4:
                        r = b - 4 if dil else b // 2 - 2
                        dve.wait_ge(turned, h * 2 * NT + 2 * r + 2)
                    dve.sem_inc(carried, 1)
                    o = T - P - P * i
                    nc.vector.tensor_tensor_reduce(out=S[:, b % 4], in0=ps[:, 1024 * (b % 2):1024 * (b % 2 + 1)],
                                                   in1=bias[:, j if dil else 0, o:o + T], scale=0.125, scalar=-3e38,
                                                   op0=ALU.add, op1=ALU.max, accum_out=mx[:, b:b + 1]).then_inc(ttr_ok, 1)
                    dve.wait_ge(ttr_ok, h * NB + b + 1)
                    nc.vector.tensor_scalar(nm[:, b:b + 1], mx[:, b:b + 1], -1.0, None, ALU.mult).then_inc(neg_ok, 1)

                def inverse(b):
                    dve.wait_ge(exp_ok, h * NB + b + 1)
                    nc.vector.reciprocal(rl[:, b:b + 1], ls[:, b:b + 1]).then_inc(rl_ok, 1)

                def mix(r):
                    b = 2 * r
                    inverse(b)
                    inverse(b + 1)
                    dve.wait_ge(rl_ok, h * NB + b + 2)
                    nc.vector.tensor_scalar(S[:, (b + 1) % 4], S[:, (b + 1) % 4], rl[:, b + 1:b + 2], K.neglam[:, 0:1],
                                            ALU.mult, ALU.mult).then_inc(part_ok, 1)
                    dve.wait_ge(part_ok, h * NT + r + 1)
                    stt(S[:, b % 4], S[:, b % 4], rl[:, b:b + 1], S[:, (b + 1) % 4], ALU.mult, ALU.add).then_inc(w_ok, 1)

                biased(0)
                biased(1)
                for r in range(NT):
                    j, i = step[r] if dil else (0, r)
                    if dil:
                        dve.wait_ge(turned, h * 2 * NT + 2 * r + 1)
                        if r >= 1:
                            dve.wait_ge(pv_ok, h * 2 * NT + 2 * r - 1)
                        nc.vector.tensor_copy(pt[:, 0].rearrange("p m n -> p (m n)"), ps[:, 2048:2560]).then_inc(pt0, 1)
                    else:
                        mix(r)
                    for b in ([r + 2] if dil else [2 * r + 2, 2 * r + 3]):
                        if b < NB:
                            biased(b)
                    if dil:
                        inverse(r)
                        dve.wait_ge(rl_ok, h * NB + r + 1)
                        dve.wait_ge(pv_ok, h * 2 * NT + 2 * r + 2)
                        nc.vector.tensor_scalar(otok[:, i, 64 * j:64 * j + 64], ps[:, 3072:3136], rl[:, r:r + 1], None,
                                                ALU.mult).then_inc(o_ok, 1)
                    else:
                        dve.wait_ge(pv_ok, h * 2 * NT + 2 * r + 2)
                        nc.vector.tensor_copy(otok[:, i], ps[:, 3072:3072 + P]).then_inc(o_ok, 1)
                if not dil:
                    dve.wait_ge(ss_ok, h * (NT + 1) + NT + 1)
                    nc.vector.reciprocal(ors[:, :], oss[:, :]).then_inc(or_ok, 1)
                    dve.wait_ge(or_ok, h + 1)
                    tt(otok[:, :, :], otok[:, :, :], ors[:, :].unsqueeze(2).to_broadcast([P, NI, P]), ALU.mult).then_inc(on_ok, 1)
                for hf in range(2):
                    c = slice(512 * hf, 512 * (hf + 1))
                    dve.wait_ge(oturn, h * 2 + hf + 1)
                    if dil:
                        tt(yt[:, c], ps[:, c], zT[:, c], ALU.mult).then_inc(y_ok, 1)
                    else:
                        stt(yt[:, c], ps[:, c], K.outgain[:, 0:1], zT[:, c], ALU.mult, ALU.mult).then_inc(y_ok, 1)


def lambda_phase(nc, K):
    LAM0 = 0.8 - 0.6 * math.exp(0.0)
    with ExitStack() as ctx:
        sb = lambda n, sh: ctx.enter_context(nc.sbuf_tensor("lam_" + n, sh, F32))
        v, pr, e, par = sb("v", [P, 4, 64]), sb("pr", [P, 2, 64]), sb("e", [P, 2]), sb("par", [P, 3])
        s = lambda n: semaphore(nc, ctx, "lam_" + n)
        v_in, V, A = s("in"), s("dve"), s("act")
        block = ctx.enter_context(nc.Block())

        @block.sync
        def _(sp):
            sp.dma_start(v[:, :, :].rearrange("p a b -> p (a b)"), K.d["lambdas"].to_broadcast([P, 256])).then_inc(v_in, 16)
            sp.dma_start(par[:, :], K.d["par_diff"]).then_inc(v_in, 16)

        @block.scalar
        def _(act):
            act.wait_ge(V, 2)
            nc.scalar.activation(e[:, :], e[:, :], ACT.Exp).then_inc(A, 1)

        @block.vector
        def _(dve):
            ch = Chain(dve, V)
            dve.wait_ge(v_in, 32)
            vv = v[:, :, :].rearrange("p (a b) n -> p a b n", b=2)
            ch.link(nc.vector.tensor_tensor(pr[:, :, :], vv[:, :, 0], vv[:, :, 1], ALU.mult))
            ch.link(nc.vector.reduce_sum(e[:, :], pr[:, :, :], axis=mybir.AxisListType.X))
            dve.wait_ge(A, 1)
            ch.link(nc.vector.tensor_tensor(K.neglam[:, :], e[:, 1:2], e[:, 0:1], ALU.subtract))
            ch.link(nc.vector.tensor_scalar(K.neglam[:, :], K.neglam[:, :], -LAM0, None, ALU.add))
            ch.link(nc.vector.tensor_scalar(K.outgain[:, :], par[:, 2:3], 1.0 - LAM0, None, ALU.mult))


def add_phase(nc, K, xr, o):
    with ExitStack() as ctx:
        added = semaphore(nc, ctx, "added2")
        block = ctx.enter_context(nc.Block())

        @block.vector
        def _(dve):
            for k in range(KT):
                nc.vector.tensor_tensor(xr[:, k], xr[:, k], o[:, k], ALU.add).then_inc(added, 1)


def final_phase(nc, K, u_hi, u_lo, xr):
    with ExitStack() as ctx:
        sb = lambda n, sh, dt=F32: ctx.enter_context(nc.sbuf_tensor("g_" + n, sh, dt))
        W = Weights(nc, ctx, "gw", 4)
        p_in = sb("p", [P, CH, 2 * P])
        pT, p_hi, p_lo = sb("pT", [P, 2, T]), sb("p_hi", [P, 2, T], F32R), sb("p_lo", [P, 2, T], F32R)
        pw, pw_hi, pw_lo = sb("pw", [P, KT, 2 * P]), sb("pw_hi", [P, KT, 2, P], F32R), sb("pw_lo", [P, KT, 2, P], F32R)
        gate = sb("gate", [P, T])
        ot = sb("out", [P, 2, CH, P])
        s = lambda n: semaphore(nc, ctx, "g_" + n)
        in_p, in_w, pturn, p_ok, p_hi_ok, p_lo_ok, w_hi_ok, w_lo_ok = (s(n) for n in
            ["in_p", "in_w", "pturn", "p_ok", "p_hi", "p_lo", "w_hi", "w_lo"])
        gate_mm, ple_mm, sig_ok, prod_ok, sum_ok, turned, copied = (s(n) for n in
            ["gate_mm", "ple_mm", "sig", "prod", "sum", "turned", "copied"])
        stored = [s("stored0"), s("stored1")]
        block = ctx.enter_context(nc.Block())
        ps = K.psum
        out = K.d["out"][0].rearrange("(c p) (f n) -> f p c n", p=P, n=P)

        def back(act, f):
            for h in range(2):
                act.wait_ge(turned, 2 * f + h + 1)
                if f >= 2:
                    act.wait_ge(stored[f % 2], 16 * (f // 2))
                nc.scalar.activation(ot[:, f % 2, 4 * h:4 * h + 4].rearrange("p c n -> p (c n)"),
                                     ps[:, 2048 + 512 * h:2048 + 512 * (h + 1)], ACT.Copy).then_inc(copied, 1)

        @block.sync
        def _(sp):
            W.credits_raw(sp)
            sp.dma_start(p_in[:, :, :], K.d["p"][0, 0].rearrange("(c p) n -> p c n", p=P)).then_inc(in_p, 16)
            sp.dma_start(pw[:, :, :], K.d["w_ple"].rearrange("f p k -> p f k")).then_inc(in_w, 16)
            for n in range(KT):
                W.load(sp, 0, 8, n, K.d["w_gate"][n])
            for f in range(KT):
                sp.wait_ge(copied, 2 * f + 2)
                sp.dma_start(out[f], ot[:, f % 2]).then_inc(stored[f % 2], 16)
            for r in range(2):
                sp.wait_ge(stored[r], 64)

        @block.gpsimd
        def _(pool):
            W.split(pool, 0, 8, 0)
            W.split(pool, 0, 8, 1)
            pool.wait_ge(in_w, 16)
            w4 = pw[:, :, :].rearrange("p f (k n) -> p f k n", k=2)
            nc.gpsimd.tensor_copy(pw_hi[:, :, :, :], w4).then_inc(w_hi_ok, 1)
            pool.wait_ge(w_hi_ok, 1)
            nc.gpsimd.tensor_tensor(pw_lo[:, :, :, :].rearrange("p f k n -> p (f k n)"), pw[:, :, :].rearrange("p f k -> p (f k)"),
                                    pw_hi[:, :, :, :].rearrange("p f k n -> p (f k n)").bitcast(F32), ALU.subtract).then_inc(w_lo_ok, 1)
            for n in range(2, KT):
                W.split(pool, 0, 8, n)

        @block.tensor
        def _(pe):
            W.credits_used(pe)
            pe.wait_ge(in_p, 16)
            for c in range(CH):
                if c == 4:
                    pe.wait_ge(p_ok, 2)
                for k in range(2):
                    last = nc.tensor.transpose(ps[:, 3072 + 512 * k + P * (c % 4):3072 + 512 * k + P * (c % 4 + 1)],
                                               p_in[:, c, P * k:P * (k + 1)], K.ident[:, :])
                last.then_inc(pturn, 1)

            def turn(f):
                pe.wait_ge(sum_ok, f + 1)
                for h in range(2):
                    if f >= 1:
                        pe.wait_ge(copied, 2 * f + h - 1)
                    for m in range(4):
                        last = nc.tensor.transpose(ps[:, 2048 + 512 * h + P * m:2048 + 512 * h + P * (m + 1)],
                                                   xr[:, f, 512 * h + P * m:512 * h + P * (m + 1)], K.ident[:, :])
                    last.then_inc(turned, 1)

            for f in range(KT):
                W.wait(pe, 0, 8, f)
                for h in range(2):
                    c = slice(512 * h, 512 * (h + 1))
                    if f >= 1:
                        pe.wait_ge(sig_ok, 2 * (f - 1) + h + 1)
                    gemm(nc, ps[:, c], W.hi[:, f % 2], W.lo[:, f % 2], lambda k: u_hi[:, k, c], lambda k: u_lo[:, k, c]).then_inc(gate_mm, 1)
                pe.wait_ge(gate_mm, 2 * f + 2)
                pe.sem_inc(W.used, 1)
                if f == 0:
                    pe.wait_ge(w_lo_ok, 1)
                    pe.wait_ge(p_lo_ok, 1)
                for h in range(2):
                    c = slice(512 * h, 512 * (h + 1))
                    if f >= 1:
                        pe.wait_ge(prod_ok, f)
                    gemm(nc, ps[:, 1024 + 512 * h:1024 + 512 * (h + 1)], pw_hi[:, f], pw_lo[:, f],
                         lambda k: p_hi[:, k, c], lambda k: p_lo[:, k, c], kk=2).then_inc(ple_mm, 1)
                if f >= 1:
                    turn(f - 1)
            turn(KT - 1)

        @block.scalar
        def _(act):
            for g in range(2):
                act.wait_ge(pturn, 4 * g + 4)
                for k in range(2):
                    nc.scalar.activation(pT[:, k, 512 * g:512 * (g + 1)], ps[:, 3072 + 512 * k:3072 + 512 * (k + 1)], ACT.Copy).then_inc(p_ok, 1)
            act.wait_ge(p_ok, 4)
            nc.scalar.activation(p_hi[:, :, :], pT[:, :, :], ACT.Copy).then_inc(p_hi_ok, 1)
            for f in range(KT):
                for h in range(2):
                    act.wait_ge(gate_mm, 2 * f + h + 1)
                    if f >= 1:
                        act.wait_ge(sum_ok, f)
                    nc.scalar.activation(gate[:, 512 * h:512 * (h + 1)], ps[:, 512 * h:512 * (h + 1)], ACT.Sigmoid).then_inc(sig_ok, 1)
                if f >= 1:
                    back(act, f - 1)
            back(act, KT - 1)

        @block.vector
        def _(dve):
            dve.wait_ge(p_hi_ok, 1)
            nc.vector.tensor_tensor(p_lo[:, :, :], pT[:, :, :], p_hi[:, :, :].bitcast(F32), ALU.subtract).then_inc(p_lo_ok, 1)
            for f in range(KT):
                dve.wait_ge(ple_mm, 2 * f + 2)
                dve.wait_ge(sig_ok, 2 * f + 2)
                nc.vector.tensor_tensor(gate[:, :], gate[:, :], ps[:, 1024:2048], ALU.mult).then_inc(prod_ok, 1)
                dve.wait_ge(prod_ok, f + 1)
                nc.vector.tensor_tensor(xr[:, f], xr[:, f], gate[:, :], ALU.add).then_inc(sum_ok, 1)


def program(nc, d, s):
    K = Kernel(d, s)
    with ExitStack() as top:
        sb = lambda n, sh, dt=F32: top.enter_context(nc.sbuf_tensor(n, sh, dt))
        K.psum = top.enter_context(nc.psum_tensor("psum", [P, 4096], F32))
        K.ident, K.tri, K.ones = sb("ident", [P, P]), sb("tri", [P, P]), sb("ones", [P, P])
        K.identb, K.maskb = sb("identb", [P, P], BF16), sb("maskb", [P, P], BF16)
        K.eps = sb("eps", [P, 1])
        K.mask = sb("mask", [P, P])
        K.pairs = sb("pairs", [P, P])
        K.neglam, K.outgain = sb("neglam", [P, 1]), sb("outgain", [P, 1])
        K.gains = sb("gains", [P, 4 * KT])
        with ExitStack() as one:
            sb1 = lambda n, sh, dt=F32: one.enter_context(nc.sbuf_tensor(n, sh, dt))
            u_hi, u_lo = sb1("u_hi", [P, KT, L], F32R), sb1("u_lo", [P, KT, L], F32R)
            sm = sb1("ssd_small", [P, GROUPS, 6, CH + 1, HG])
            with ExitStack() as c0:
                xT = c0.enter_context(nc.sbuf_tensor("xT", [P, KT, L], F32))
                load_phase(nc, K, xT)
                clear_semaphores(nc)
                norm_phase(nc, K, "n0", xT, L, THIRDS, K.gains[:, 0:KT], u_hi, u_lo)
                clear_semaphores(nc)
            small_phase(nc, K, u_hi, u_lo, sm)
            clear_semaphores(nc)
            ssd_phase(nc, K, u_hi, u_lo, sm)
            clear_semaphores(nc)
            ssd_out_phase(nc, K)
            clear_semaphores(nc)
            fox_phase(nc, K, u_hi, u_lo)
            clear_semaphores(nc)
            merge_phase(nc, K, u_hi, u_lo)
            clear_semaphores(nc)
        with ExitStack() as two:
            sb2 = lambda n, sh, dt=F32: two.enter_context(nc.sbuf_tensor(n, sh, dt))
            xr = sb2("x_res", [P, KT, T])
            with ExitStack() as c1:
                o = c1.enter_context(nc.sbuf_tensor("w_out_o", [P, KT, T], F32))
                linear_phase(nc, K, "l1", K.s["merged"], K.d["w_out"], o)
                clear_semaphores(nc)
                residual_phase(nc, K, o, K.gains[:, KT:2 * KT], xr)
                clear_semaphores(nc)
            lambda_phase(nc, K)
            clear_semaphores(nc)
            with ExitStack() as c2:
                h_hi, h_lo = (c2.enter_context(nc.sbuf_tensor("h_" + n, [P, KT, T], F32R)) for n in ("hi", "lo"))
                norm_phase(nc, K, "n2", xr, T, [(0, 512), (512, 1024)], K.gains[:, 2 * KT:3 * KT], h_hi, h_lo)
                clear_semaphores(nc)
                mixer_phase(nc, K, "md", False, h_hi, h_lo)
                clear_semaphores(nc)
                mixer_phase(nc, K, "ml", True, h_hi, h_lo)
                clear_semaphores(nc)
            with ExitStack() as c3:
                o = c3.enter_context(nc.sbuf_tensor("w_out2_o", [P, KT, T], F32))
                linear_phase(nc, K, "l2", K.s["mix"], K.d["w_out_2"], o)
                clear_semaphores(nc)
                add_phase(nc, K, xr, o)
                clear_semaphores(nc)
            with ExitStack() as c4:
                r_hi, r_lo = (c4.enter_context(nc.sbuf_tensor("r_" + n, [P, KT, T], F32R)) for n in ("hi", "lo"))
                norm_phase(nc, K, "n3", xr, T, [(0, 512), (512, 1024)], K.gains[:, 3 * KT:4 * KT], r_hi, r_lo)
                clear_semaphores(nc)
                final_phase(nc, K, r_hi, r_lo, xr)
                clear_semaphores(nc)


def tiles(np, w):
    k, n = w.shape[0] // P, w.shape[1] // P
    return w.reshape(k, P, n, P).transpose(2, 1, 0, 3).reshape(n, P, k * P)


def cols(v):
    return v.reshape(-1, P).transpose(1, 0)


def kernel(**inputs):
    import numpy as np
    import concourse.bacc as bacc
    from concourse import mybir as mb
    from concourse.bass_utils import run_bass_kernel_spmd as run

    I = {k: np.asarray(v) for k, v in inputs.items()}
    g = lambda n: I[n][0]
    A = {}
    A["x"], A["meta"] = I["x"], I["meta_tokens"]
    w = g("w_in")
    o_x, o_dt, o_za = 2048, 5120, 5152
    o_q, o_k, o_v, o_f, o_g = 6176, 7200, 8224, 9248, 9264
    tz, txs = tiles(np, w[:, 0:2048]), tiles(np, w[:, o_x:o_x + 2048])
    tb, tc = tiles(np, w[:, o_x + 2048:o_x + 2560]), tiles(np, w[:, o_x + 2560:o_x + 3072])
    A["w_ssd"] = np.concatenate([np.concatenate([txs[4 * i:4 * i + 4], tb[i:i + 1], tc[i:i + 1], tz[4 * i:4 * i + 4]]) for i in range(GROUPS)])
    A["wdf"] = np.concatenate([w[:, o_dt:o_dt + 32], w[:, o_f:o_f + 16]], axis=1).reshape(KT, P, SM).transpose(1, 0, 2)
    A["dtf_bias"] = np.concatenate([g("dt_bias"), g("fgate_bias")])[None]
    A["a_log"] = g("a_log")[None]
    A["gains"] = np.concatenate([cols(g("norm_pre")), cols(g("norm_post")), cols(g("mix_norm_g_2")), cols(g("ple_norm_g_2"))], axis=1)
    cw = np.concatenate([g("conv_w"), g("conv_b")[None]])
    cw = cw.reshape(5, 24, P).transpose(2, 1, 0)
    dsk = cols(np.broadcast_to(g("d_skip")[:, None], (SSD_H, 64)).reshape(-1))
    gn = cols(g("ssd_norm"))
    A["conv_par"] = np.stack([np.concatenate([cw[:, 4 * i:4 * i + 4].reshape(P, 20), cw[:, 16 + i], cw[:, 20 + i],
                                              dsk[:, 4 * i:4 * i + 4], gn[:, 4 * i:4 * i + 4]], axis=1) for i in range(GROUPS)], axis=1)
    A["mask"] = np.triu(np.ones((P, P), np.float32), 1)
    A["w_proj_ssd"] = tiles(np, g("w_proj_ssd")).reshape(KT, P, 2, KT * P).transpose(0, 2, 1, 3).reshape(16, P, KT * P)
    tq, tk, tv, tza = (tiles(np, w[:, o:o + 1024]) for o in (o_q, o_k, o_v, o_za))
    A["w_fox"] = np.stack([tq, tk, tv, tza], axis=1).reshape(32, P, KT * P)
    tgs, tga, twa = tiles(np, w[:, o_g:o_g + 1024]), tiles(np, w[:, o_g + 1024:o_g + 2048]), tiles(np, g("w_proj_att"))
    A["w_merge"] = np.stack([tgs, tga, twa], axis=1).reshape(24, P, KT * P)
    A["w_out"] = tiles(np, g("w_out"))
    A["gate_bias"] = cols(g("gate_bias"))
    A["pairs"] = np.kron(np.eye(2, dtype=np.float32), np.ones((64, 64), np.float32))
    w2 = tiles(np, g("w_in_2"))
    A["w_diff"] = np.stack([w2[0:4], w2[4:8], w2[8:12], w2[24:28]], axis=1).reshape(16, P, KT * P)
    A["w_dil"] = np.stack([w2[12:16], w2[16:20], w2[20:24], w2[28:32]], axis=1).reshape(16, P, KT * P)
    A["w_out_2"], A["w_gate"], A["w_ple"] = (tiles(np, g(n)) for n in ("w_out_2", "w_ple_gate_2", "w_ple_proj_2"))
    A["p"] = I["p_2"]
    A["lambdas"] = np.concatenate([g("lambda_q1_2"), g("lambda_k1_2"), g("lambda_q2_2"), g("lambda_k2_2")])[None]
    twice = lambda v: np.concatenate([v, v])
    A["par_diff"] = np.stack([twice(g("diff_q_norm_g_2")), twice(g("diff_k_norm_g_2")), g("diff_sub_norm_g_2")], axis=1)
    A["par_dil"] = np.stack([twice(g("dil_q_norm_g_2")), twice(g("dil_k_norm_g_2")), twice(g("dil_k_norm_g_2"))], axis=1)
    dist = np.abs(np.arange(P)[:, None] + (T - P) - np.arange(2 * T - P)[None, :])
    A["dist"] = dist.astype(np.float32)
    held = (dist <= 64) * 1 + ((dist <= 256) & (dist % 4 == 0)) + (dist % 16 == 0)
    A["count"] = np.where(held > 0, 8.0 * np.log(np.maximum(held, 1)), NEG).astype(np.float32)
    A["slopes_diff"] = np.broadcast_to(np.array([-8.0 * 2.0 ** (-2.0 * (i % 4 + 1)) for i in range(8)], np.float32), (P, 8))
    A["slopes_dil"] = np.broadcast_to(np.array([-8.0 * 2.0 ** (-(i + 1.0)) for i in range(8)], np.float32), (P, 8))
    A["ident"] = np.eye(P, dtype=np.float32)
    A["tri"] = np.triu(np.ones((P, P), np.float32))
    nc = bacc.Bacc("TRN2", target_bir_lowering=False, num_devices=1)
    arrays, ins = {}, {}
    for n, a in A.items():
        a = np.ascontiguousarray(a)
        arrays["in_" + n] = a
        ins[n] = (nc.dram_tensor("in_" + n, a.shape, mb.dt.from_np(a.dtype), kind="ExternalInput").ap())
    ins["out"] = nc.dram_tensor("out_0", (1, T, D), F32, kind="ExternalOutput").ap()
    s = {}
    s["xT"] = nc.dram_tensor("s_xT", (KT, P, T), F32, kind="Internal").ap()
    s["y"] = nc.dram_tensor("s_y", (16, P, T), F32, kind="Internal").ap()
    for n in ("pssd", "yatt", "merged", "mix"):
        s[n] = nc.dram_tensor("s_" + n, (KT, P, T), F32, kind="Internal").ap()
    s["nc"] = nc.dram_tensor("s_nc", (ATT_H, L), F32, kind="Internal").ap()
    program(nc, ins, s)
    r = run(nc, [arrays], core_ids=[0])
    return r.results[0]["out_0"]
```

```python
import concourse.bass as bass
from concourse import mybir
from contextlib import ExitStack
import math

F32 = mybir.dt.float32
F32R = mybir.dt.float32r
BF16 = mybir.dt.bfloat16
ALU = mybir.AluOpType
ACT = mybir.ActivationFunctionType
P = 128
D = 1024
T = 1024
META = 16
L = META + T
KT = D // P
CH = T // P
GROUPS, HG = 4, 8
SSD_H, ATT_H = 32, 16
SM = 48
EPS = 1e-6
NEG = -1e30
THIRDS = [(0, 348), (348, 696), (696, 1040)]
HALVES = [(META, META + 512), (META + 512, L)]


def chunk_cols(c):
    return (0, META) if c == 0 else (META + P * (c - 1), META + P * c)


USED = []
NUMBERS = 85


def semaphore(nc, ctx, name):
    USED.append(ctx.enter_context(nc.semaphore(name)))
    return USED[-1]


def clear_semaphores(nc):
    if len(USED) < NUMBERS:
        return
    with nc.Block() as block:
        @block.gpsimd
        def _(pool):
            for s in USED:
                pool.sem_clear(s)
    USED.clear()


class Chain:

    def __init__(self, eng, sem, per=0, i=0):
        self.eng, self.sem, self.per, self.i, self.n = eng, sem, per, i, 0

    def step(self, ins):
        ins.then_inc(self.sem, 1)
        self.n += 1
        return self.n

    def after(self, n):
        self.eng.wait_ge(self.sem, self.i * self.per + n)

    def link(self, ins):
        self.after(self.step(ins))


def gemm_k(nc, out, w_hi, w_lo, a_hi, a_lo, k, kk=KT):
    nc.tensor.matmul(out, w_hi[:, k], a_hi, start=(k == 0), stop=False)
    nc.tensor.matmul(out, w_hi[:, k], a_lo, start=False, stop=False)
    return nc.tensor.matmul(out, w_lo[:, k], a_hi, start=False, stop=(k == kk - 1))


def gemm(nc, out, w_hi, w_lo, a_hi, a_lo, kk=KT, first=True, final=True):
    for k in range(kk):
        nc.tensor.matmul(out, w_hi[:, k], a_hi(k), start=(k == 0 and first), stop=False)
        nc.tensor.matmul(out, w_hi[:, k], a_lo(k), start=False, stop=False)
        last = nc.tensor.matmul(out, w_lo[:, k], a_hi(k), start=False, stop=(k == kk - 1 and final))
    return last


class Kernel:

    def __init__(self, d, s):
        self.d, self.s = d, s


class Weights:

    def __init__(self, nc, ctx, name, raw_slots=4):
        self.nc, self.R = nc, raw_slots
        self.raw = ctx.enter_context(nc.sbuf_tensor(name + "_raw", [P, raw_slots, KT, P], F32))
        self.hi = ctx.enter_context(nc.sbuf_tensor(name + "_hi", [P, 2, KT, P], F32R))
        self.lo = ctx.enter_context(nc.sbuf_tensor(name + "_lo", [P, 2, KT, P], F32R))
        s = lambda n: semaphore(nc, ctx, name + n)
        self.loaded = [s(f"_loaded{r}") for r in range(raw_slots)]
        self.raw_free = s("_raw_free")
        self.hi_done = s("_hi_done")
        self.turns = s("_turns")
        self.ready = s("_split")
        self.used = s("_used")

    def credits_raw(self, eng):
        eng.sem_inc(self.raw_free, self.R)

    def credits_used(self, eng):
        eng.sem_inc(self.used, 2)

    def load(self, eng, i, per, n, src):
        eng.wait_ge(self.raw_free, i * per + n + 1)
        eng.dma_start(self.raw[:, n % self.R].rearrange("p k n -> p (k n)"), src).then_inc(self.loaded[n % self.R], 16)

    def split(self, eng, i, per, n):
        r = n % self.R
        eng.wait_ge(self.loaded[r], 16 * (i * (per // self.R) + n // self.R + 1))
        eng.wait_ge(self.used, i * per + n + 1)
        eng.sem_inc(self.turns, 1)
        self.nc.gpsimd.tensor_scalar(self.hi[:, n % 2], self.raw[:, r], 1.0, 1.0, ALU.mult, ALU.mult).then_inc(self.hi_done, 1)
        eng.wait_ge(self.hi_done, i * per + n + 1)
        self.nc.gpsimd.tensor_tensor(self.lo[:, n % 2], self.raw[:, r], self.hi[:, n % 2].bitcast(F32),
                                     ALU.subtract).then_inc(self.ready, 1)
        eng.wait_ge(self.ready, i * per + n + 1)
        eng.sem_inc(self.raw_free, 1)

    def wait(self, eng, i, per, n):
        eng.wait_ge(self.ready, i * per + n + 1)


def norm_phase(nc, K, name, xT, cols, pieces, gain, u_hi, u_lo):
    C = cols
    with ExitStack() as ctx:
        sq = ctx.enter_context(nc.sbuf_tensor(name + "_sq", [P, 2, C], F32))
        rs = ctx.enter_context(nc.sbuf_tensor(name + "_rs", [P, C], F32))
        rt = ctx.enter_context(nc.sbuf_tensor(name + "_rt", [P, C], F32))
        un = ctx.enter_context(nc.sbuf_tensor(name + "_un", [P, 2, C], F32))
        s = lambda n: semaphore(nc, ctx, name + n)
        squared, summed, rooted, inverted = s("_squared"), s("_summed"), s("_rooted"), s("_inverted")
        scaled, hi_ok, lo_ok = s("_scaled"), s("_hi"), s("_lo")
        block = ctx.enter_context(nc.Block())
        ps = K.psum

        @block.scalar
        def _(act):
            for k in range(KT):
                if k >= 2:
                    act.wait_ge(summed, k - 1)
                nc.scalar.activation(sq[:, k % 2], xT[:, k], ACT.Square).then_inc(squared, 1)
            act.wait_ge(summed, KT)
            for j, (a, b) in enumerate(pieces):
                nc.scalar.activation(rt[:, a:b], ps[:, 512 * j:512 * j + b - a], ACT.Sqrt, scale=1.0 / D,
                                     bias=K.eps[:, 0:1]).then_inc(rooted, 1)
            for k in range(KT):
                act.wait_ge(scaled, k + 1)
                nc.scalar.activation(u_hi[:, k], un[:, k % 2], ACT.Copy).then_inc(hi_ok, 1)

        @block.tensor
        def _(pe):
            for k in range(KT):
                pe.wait_ge(squared, k + 1)
                for j, (a, b) in enumerate(pieces):
                    last = nc.tensor.matmul(ps[:, 512 * j:512 * j + b - a], K.ones[:, :], sq[:, k % 2, a:b],
                                            start=(k == 0), stop=(k == KT - 1))
                last.then_inc(summed, 1)

        @block.vector
        def _(dve):
            dve.wait_ge(rooted, len(pieces))
            nc.vector.reciprocal(rs[:, :], rt[:, :]).then_inc(inverted, 1)
            dve.wait_ge(inverted, 1)
            for k in range(KT):
                if k >= 2:
                    dve.wait_ge(lo_ok, k - 1)
                nc.vector.scalar_tensor_tensor(un[:, k % 2], xT[:, k], gain[:, k:k + 1], rs[:, :],
                                               ALU.mult, ALU.mult).then_inc(scaled, 1)

        @block.gpsimd
        def _(pool):
            for k in range(KT):
                pool.wait_ge(hi_ok, k + 1)
                nc.gpsimd.tensor_tensor(u_lo[:, k], un[:, k % 2], u_hi[:, k].bitcast(F32),
                                        ALU.subtract).then_inc(lo_ok, 1)


def load_phase(nc, K, xT):
    with ExitStack() as ctx:
        xt = ctx.enter_context(nc.sbuf_tensor("x_tok", [P, CH + 1, D], F32))
        s = lambda n: semaphore(nc, ctx, n)
        const_in, out_xT = s("const_in"), s("xT_stored")
        x_in = [s(f"x_in{c}") for c in range(CH + 1)]
        turned, copied = s("x_turned"), s("x_copied")
        ms = s("eps_set")
        block = ctx.enter_context(nc.Block())
        ps = K.psum
        consts = [(K.ident, K.d["ident"]), (K.tri, K.d["tri"]), (K.gains, K.d["gains"]), (K.mask, K.d["mask"]), (K.pairs, K.d["pairs"])]

        @block.sync
        def _(sp):
            for dst, src in consts:
                sp.dma_start(dst[:, :], src).then_inc(const_in, 16)
            for c in range(CH + 1):
                n = META if c == 0 else P
                src = K.d["meta"] if c == 0 else K.d["x"][0, P * (c - 1):P * c, :]
                sp.dma_start(xt[0:n, c, :], src).then_inc(x_in[c], 16)
            for k in range(KT):
                sp.wait_ge(copied, 2 * (CH + 1))
                sp.dma_start(K.s["xT"][k], xT[:, k, META:L]).then_inc(out_xT, 16)
            sp.wait_ge(out_xT, 16 * KT)

        @block.vector
        def _(dve):
            dve.wait_ge(const_in, 16 * len(consts))
            nc.vector.tensor_copy(K.identb[:, :], K.ident[:, :])
            nc.vector.tensor_scalar(K.maskb[:, :], K.mask[:, :], NEG, None, ALU.mult)
            nc.vector.memset(K.eps[:, :], EPS)
            nc.vector.memset(K.ones[:, :], 1.0).then_inc(ms, 1)
            dve.wait_ge(ms, 1)

        @block.tensor
        def _(pe):
            pe.wait_ge(const_in, 16 * len(consts))
            for c in range(CH + 1):
                n = META if c == 0 else P
                pe.wait_ge(x_in[c], 16)
                for h in range(2):
                    u = 2 * c + h
                    if u >= 4:
                        pe.wait_ge(copied, u - 3)
                    for f in range(4):
                        last = nc.tensor.transpose(ps[:, 512 * (u % 4) + P * f:512 * (u % 4) + P * f + n],
                                                   xt[0:n, c, P * (4 * h + f):P * (4 * h + f + 1)], K.ident[0:n, 0:n])
                    last.then_inc(turned, 1)

        @block.scalar
        def _(act):
            for c in range(CH + 1):
                a, b = chunk_cols(c)
                for h in range(2):
                    u = 2 * c + h
                    act.wait_ge(turned, u + 1)
                    bank = ps[:, 512 * (u % 4):512 * (u % 4) + 512].rearrange("p (f n) -> p f n", f=4)
                    nc.scalar.activation(xT[:, 4 * h:4 * h + 4, a:b], bank[:, :, 0:b - a], ACT.Copy).then_inc(copied, 1)


def small_phase(nc, K, u_hi, u_lo, sm):
    NCH = CH + 1
    with ExitStack() as ctx:
        sb = lambda n, sh, dt=F32: ctx.enter_context(nc.sbuf_tensor(n, sh, dt))
        wraw, whi, wlo = sb("wdf_raw", [P, KT, SM]), sb("wdf_hi", [P, KT, SM], F32R), sb("wdf_lo", [P, KT, SM], F32R)
        brow = sb("dtf_bias", [P, SM])
        arow = sb("a_row", [P, SSD_H])
        aneg = sb("a_neg", [P, SSD_H])
        sgn = sb("dtf_sign", [P, SM])
        names = ["raw", "v", "e", "w", "l", "q", "t", "z", "sp"]
        B = {n: sb("dtf_" + n, [P, NCH, SM]) for n in names}
        adt = sb("adt", [P, NCH, SSD_H])
        acs = sb("acs", [P, NCH, SSD_H])
        alast = sb("alast", [P, NCH, SSD_H])
        fT = sb("fT", [ATT_H, L])
        ncT = sb("ncT", [ATT_H, L])
        onesL = sb("onesL", [ATT_H, L])
        s = lambda n: semaphore(nc, ctx, n)
        w_in, w_split, proj, V, A, G, X, pemm, st = (s("dtf_" + n) for n in
            ["loaded", "wsplit", "projected", "dve", "act", "pool", "x", "pe", "stored"])
        block = ctx.enter_context(nc.Block())
        ps = K.psum

        @block.sync
        def _(sp):
            sp.dma_start(wraw[:, :, :], K.d["wdf"]).then_inc(w_in, 16)
            sp.dma_start(brow[:, :], K.d["dtf_bias"].to_broadcast([P, SM])).then_inc(w_in, 16)
            sp.dma_start(arow[:, :], K.d["a_log"].to_broadcast([P, SSD_H])).then_inc(w_in, 16)
            sp.wait_ge(X, 1)
            sp.dma_start(K.s["nc"], ncT[:, :]).then_inc(st, 16)
            sp.wait_ge(st, 16)

        @block.gpsimd
        def _(pool):
            pool.wait_ge(w_in, 48)
            nc.gpsimd.tensor_copy(whi[:, :, :], wraw[:, :, :]).then_inc(G, 1)
            pool.wait_ge(G, 1)
            nc.gpsimd.tensor_tensor(wlo[:, :, :], wraw[:, :, :], whi[:, :, :].bitcast(F32), ALU.subtract).then_inc(w_split, 1)

        @block.tensor
        def _(pe):
            pe.wait_ge(w_split, 1)
            for c in range(NCH):
                a, b = chunk_cols(c)
                out = ps[0:b - a, SM * c:SM * (c + 1)]
                for k in range(KT):
                    nc.tensor.matmul(out, u_hi[:, k, a:b], whi[:, k], start=(k == 0), stop=False)
                    nc.tensor.matmul(out, u_hi[:, k, a:b], wlo[:, k], start=False, stop=False)
                    last = nc.tensor.matmul(out, u_lo[:, k, a:b], whi[:, k], start=False, stop=(k == KT - 1))
            last.then_inc(pemm, 1)
            pe.wait_ge(proj, 1)
            nc.tensor.matmul(ps[:, 512:768], K.tri[:, :], adt[:, 1:, :], start=True, stop=True)
            nc.tensor.matmul(ps[0:META, 768:800], K.tri[0:META, 0:META], adt[0:META, 0, :], start=True, stop=True)
            nc.tensor.matmul(ps[:, 1024:1280], K.ones[:, :], adt[:, 1:, :], start=True, stop=True)
            nc.tensor.matmul(ps[:, 1280:1312], K.ones[0:META, :], adt[0:META, 0, :], start=True, stop=True)
            for c in range(NCH):
                a, b = chunk_cols(c)
                last = nc.tensor.transpose(ps[0:ATT_H, 1536 + 512 * (c // 3) + P * (c % 3):1536 + 512 * (c // 3) + P * (c % 3) + b - a],
                                           B["sp"][0:b - a, c, SSD_H:SM], K.ident[0:b - a, 0:b - a])
            last.then_inc(pemm, 1)

        @block.scalar
        def _(act):
            act.wait_ge(w_in, 48)
            nc.scalar.activation(aneg[:, :], arow[:, :], ACT.Exp).then_inc(A, 1)
            act.wait_ge(V, 5)
            nc.scalar.activation(B["e"][:, :, :], B["e"][:, :, :], ACT.Exp, scale=-1.0).then_inc(A, 1)
            act.wait_ge(V, 6)
            nc.scalar.activation(B["l"][:, :, :], B["w"][:, :, :], ACT.Ln).then_inc(A, 1)
            act.wait_ge(V, 21)
            for g in range(GROUPS):
                nc.scalar.activation(sm[:, g, 3], sm[:, g, 3], ACT.Exp).then_inc(A, 1)
                nc.scalar.activation(sm[:, g, 4], alast[:, :, HG * g:HG * (g + 1)], ACT.Exp).then_inc(A, 1)
                nc.scalar.activation(sm[:, g, 5], acs[:, :, HG * g:HG * (g + 1)], ACT.Exp).then_inc(A, 1)

        @block.vector
        def _(dve):
            ch = Chain(dve, V)
            raw, v, e, w, l, q, t, z, sp = (B[n][:, :, :] for n in names)
            nc.vector.memset(sgn[:, 0:SSD_H], 1.0)
            nc.vector.memset(sgn[:, SSD_H:SM], -1.0)
            nc.vector.memset(onesL[:, :], 1.0)
            nc.vector.memset(acs[:, :, :], 0.0)
            ch.link(nc.vector.memset(raw, 0.0))
            dve.wait_ge(pemm, 1)
            nc.vector.tensor_copy(B["raw"][0:META, 0, :], ps[0:META, 0:SM])
            ch.link(nc.vector.tensor_copy(B["raw"][:, 1:, :], ps[:, SM:SM * NCH].rearrange("p (c n) -> p c n", n=SM)))
            dve.wait_ge(w_in, 48)
            bb = brow[:, :].unsqueeze(1).to_broadcast([P, NCH, SM])
            sg = sgn[:, :].unsqueeze(1).to_broadcast([P, NCH, SM])
            tt, ts = nc.vector.tensor_tensor, nc.vector.tensor_scalar
            ch.link(tt(v, raw, bb, ALU.add))
            ch.link(tt(v, v, sg, ALU.mult))
            ch.link(nc.vector.scalar_tensor_tensor(e, v, -1.0, v, ALU.mult, ALU.max))
            dve.wait_ge(A, 2)
            ch.link(ts(w, e, 1.0, None, ALU.add))
            ch.link(ts(t, w, -1.0, 1e-30, ALU.add, ALU.max))
            ch.link(nc.vector.reciprocal(q, t))
            ch.link(tt(q, q, e, ALU.mult))
            ch.link(ts(t, w, 1.0, None, ALU.is_equal))
            ch.link(tt(t, t, e, ALU.mult))
            dve.wait_ge(A, 3)
            ch.link(tt(q, q, l, ALU.mult))
            ch.link(tt(t, t, q, ALU.add))
            ch.link(nc.vector.scalar_tensor_tensor(sp, v, 0.0, t, ALU.max, ALU.add))
            dve.wait_ge(A, 1)
            ch.link(ts(aneg[:, :], aneg[:, :], -1.0, None, ALU.mult))
            tt(adt[:, :, :], B["sp"][:, :, 0:SSD_H], aneg[:, :].unsqueeze(1).to_broadcast([P, NCH, SSD_H]), ALU.mult).then_inc(proj, 1)
            dve.wait_ge(pemm, 2)
            nc.vector.tensor_copy(acs[:, 1:, :], ps[:, 512:768].rearrange("p (c h) -> p c h", h=SSD_H))
            nc.vector.tensor_copy(acs[0:META, 0, :], ps[0:META, 768:800])
            nc.vector.tensor_copy(alast[:, 1:, :], ps[:, 1024:1280].rearrange("p (c h) -> p c h", h=SSD_H))
            nc.vector.tensor_copy(alast[:, 0, :], ps[:, 1280:1312])
            for c in range(NCH):
                a, b = chunk_cols(c)
                o = 1536 + 512 * (c // 3) + P * (c % 3)
                m = nc.vector.tensor_scalar(fT[:, a:b], ps[0:ATT_H, o:o + b - a], 8.0, None, ALU.mult)
            ch.link(m)
            nc.vector.tensor_tensor_scan(ncT[:, :], onesL[:, :], fT[:, :], 0.0, ALU.mult, ALU.add).then_inc(X, 1)
            for g in range(GROUPS):
                h = slice(HG * g, HG * (g + 1))
                nc.vector.tensor_copy(sm[:, g, 0], adt[:, :, h])
                nc.vector.tensor_copy(sm[:, g, 1], acs[:, :, h])
                nc.vector.tensor_copy(sm[:, g, 2], B["sp"][:, :, h])
                ch.link(tt(sm[:, g, 3], alast[:, :, h], acs[:, :, h], ALU.subtract))
            ch.link(nc.vector.memset(onesL[:, 0:1], 1.0))


def ssd_phase(nc, K, u_hi, u_lo, sm):
    NCH, NP = CH + 1, 6 * 3
    with ExitStack() as ctx:
        sb = lambda n, sh, dt=F32: ctx.enter_context(nc.sbuf_tensor(n, sh, dt))
        W = Weights(nc, ctx, "ws", 2)
        raw = sb("conv_in", [P, 2, 3 + L])
        feats = sb("conv_out", [P, 6, L])
        z = sb("z_gate", [P, 4, T])
        seg = sb("decay", [P, 2, HG, P])
        xdt, xst = sb("x_dt", [P, 2, 512]), sb("x_dt_decay", [P, 2, 512])
        ytok, yoff = sb("y_tok", [P, 2, 512]), sb("y_off", [P, 512])
        state = sb("state", [P, 512])
        btok, cb = sb("b_tok", [P, 2, P]), sb("cb", [P, 2, P])
        rms = sb("ssd_rms", [P, T])
        smg = sb("small_g", [P, 6, NCH, HG])
        cpg = sb("conv_par_g", [P, 38])
        par = sb("conv_par", [P, GROUPS, 38])
        s = lambda n: semaphore(nc, ctx, "s1_" + n)
        par_in, small_ok = s("par_in"), s("small_ok")
        proj_ok, raw_ok, conv_ok, silu_ok = s("proj"), s("raw"), s("conv"), s("silu")
        xturn, bturn, sums_ok = s("xturn"), s("bturn"), s("sums")
        zproj, zcopy, zsilu = s("zproj"), s("zcopy"), s("zsilu")
        ydiag_ok, yoff_ok, st_ok, yturn = s("ydiag"), s("yoff"), s("states"), s("yturn")
        xdt_ok, cb_ok, seg_ok, m_ok = s("xdt"), s("cb"), s("seg"), s("m")
        h_ok, t_ok, y_ok, y1_ok = s("h"), s("t"), s("y"), s("y1")
        b_ok, exp_ok, xst_ok = s("btok"), s("exp"), s("xst")
        u_ok, sq_ok, norm_sum, rooted, yf_ok, stored = s("u"), s("sq"), s("normsum"), s("rooted"), s("yf"), s("stored")
        dchain = s("dve_chain")
        block = ctx.enter_context(nc.Block())
        ps = K.psum
        bank = lambda n, w=512: ps[:, 512 * n:512 * n + w]
        w_src = K.d["w_ssd"].rearrange("(g n) p k -> g n p k", g=GROUPS)
        y_dst = K.s["y"].rearrange("(g f) p t -> g f p t", g=GROUPS)

        @block.sync
        def _(sp):
            sp.dma_start(par[:, :, :], K.d["conv_par"]).then_inc(par_in, 16)
            sp.sem_inc(stored, 16)
            W.credits_raw(sp)
            with sp.Fori(0, GROUPS) as g:
                for n in range(10):
                    W.load(sp, g, 10, n, w_src[g, n])
            sp.wait_ge(stored, 64 * GROUPS + 16)

        @block.gpsimd
        def _(pool):
            with pool.Fori(0, GROUPS) as g:
                for n in range(8):
                    W.split(pool, g, 10, n)
                for c in range(8):
                    Lc = META if c == 0 else P
                    pool.wait_ge(xdt_ok, g * 9 + c + 1)
                    if c >= 2:
                        pool.wait_ge(st_ok, g * 8 + c - 1)
                    nc.gpsimd.tensor_tensor(xst[0:Lc, c % 2].rearrange("p (h d) -> p h d", h=HG),
                                            xdt[0:Lc, c % 2].rearrange("p (h d) -> p h d", h=HG),
                                            smg[0:Lc, 3, c].unsqueeze(2).to_broadcast([Lc, HG, 64]), ALU.mult).then_inc(xst_ok, 1)
                    if c == 2:
                        W.split(pool, g, 10, 8)
                    if c == 4:
                        W.split(pool, g, 10, 9)

        @block.tensor
        def _(pe):
            W.credits_used(pe)
            with pe.Fori(0, GROUPS) as g:
                pe.wait_ge(rooted, g * 2 + 2)
                for t in range(6):
                    W.wait(pe, g, 10, t)
                    for j, (a, b) in enumerate(THIRDS):
                        if t >= 2:
                            pe.wait_ge(raw_ok, g * NP + 3 * (t - 2) + j + 1)
                        gemm(nc, bank(3 * (t % 2) + j, b - a), W.hi[:, t % 2], W.lo[:, t % 2],
                             lambda k: u_hi[:, k, a:b], lambda k: u_lo[:, k, a:b]).then_inc(proj_ok, 1)
                    pe.wait_ge(proj_ok, g * NP + 3 * t + 3)
                    pe.sem_inc(W.used, 1)

                def front(c):
                    a, b = chunk_cols(c)
                    n = b - a
                    if c >= 1:
                        pe.wait_ge(xdt_ok, g * 9 + c)
                    for f in range(4):
                        last = nc.tensor.transpose(ps[0:n, 1024 + P * f:1024 + P * f + P], feats[:, f, a:b], K.ident[:, :])
                    last.then_inc(xturn, 1)
                    if c >= 1:
                        pe.wait_ge(b_ok, g * 8 + c)
                    if c >= 2:
                        pe.wait_ge(cb_ok, g * 8 + c - 1)
                    if c <= 7:
                        last = nc.tensor.transpose(ps[0:n, 1536:1536 + P], feats[:, 4, a:b], K.ident[:, :])
                    if c >= 1:
                        last = nc.tensor.matmul(ps[:, 1664:1664 + P], feats[:, 4, a:b], feats[:, 5, a:b], start=True, stop=True)
                    last.then_inc(bturn, 1)
                    if c >= 1:
                        if c >= 2:
                            pe.wait_ge(seg_ok, g * 8 + c - 1)
                        for r in range(HG):
                            last = nc.tensor.matmul(ps[:, 2048 + P * r:2048 + P * (r + 1)],
                                                    smg[:, 0, c, r:r + 1].to_broadcast([P, P]), K.tri[:, :], start=True, stop=True)
                        last.then_inc(sums_ok, 1)

                def zunit(u):
                    t, h = 6 + u // 2, u % 2
                    if h == 0:
                        W.wait(pe, g, 10, t)
                    if u >= 1:
                        pe.wait_ge(zcopy, g * 8 + u)
                    a, b = HALVES[h]
                    gemm(nc, bank(0), W.hi[:, t % 2], W.lo[:, t % 2],
                         lambda k: u_hi[:, k, a:b], lambda k: u_lo[:, k, a:b]).then_inc(zproj, 1)
                    if h == 1:
                        pe.wait_ge(zproj, g * 8 + u + 1)
                        pe.sem_inc(W.used, 1)

                def turn_back(c):
                    pe.wait_ge(y_ok, g * 8 + c)
                    if c >= 2:
                        pe.wait_ge(y1_ok, g * 8 + c - 1)
                    for f in range(4):
                        last = nc.tensor.transpose(ps[:, 512 + P * f:512 + P * (f + 1)], ytok[:, c % 2, P * f:P * (f + 1)], K.ident[:, :])
                    last.then_inc(yturn, 1)

                pe.wait_ge(silu_ok, g * 6 + 6)
                pe.wait_ge(small_ok, g + 1)
                front(0)
                for c in range(NCH):
                    a, b = chunk_cols(c)
                    n = b - a
                    if c < 8:
                        front(c + 1)
                        zunit(c)
                    if c >= 1:
                        pe.wait_ge(m_ok, g * 8 + c)
                        if c >= 2:
                            pe.wait_ge(y_ok, g * 8 + c - 1)
                        for r in range(HG):
                            last = nc.tensor.matmul(ps[:, 3072 + 64 * r:3072 + 64 * (r + 1)], seg[:, c % 2, r],
                                                    xdt[:, c % 2, 64 * r:64 * (r + 1)], start=True, stop=True)
                        last.then_inc(ydiag_ok, 1)
                        pe.wait_ge(h_ok, g * 8 + c)
                        nc.tensor.matmul(bank(7), feats[:, 5, a:b], state[:, :], start=True, stop=True).then_inc(yoff_ok, 1)
                    if c >= 2:
                        turn_back(c - 1)
                    if c <= 7:
                        pe.wait_ge(xst_ok, g * 8 + c + 1)
                        pe.wait_ge(b_ok, g * 8 + c + 1)
                        if c >= 1:
                            pe.wait_ge(t_ok, g * 8 + c)
                        nc.tensor.matmul(bank(7), btok[0:n, c % 2], xst[0:n, c % 2], start=True, stop=True).then_inc(st_ok, 1)
                turn_back(8)
                for f in range(4):
                    pe.wait_ge(sq_ok, g * 4 + f + 1)
                    for h in range(2):
                        last = nc.tensor.matmul(bank(2 + h), K.ones[:, :], raw[:, f % 2, 3 + 512 * h:3 + 512 * (h + 1)],
                                                start=(f == 0), stop=(f == 3))
                    last.then_inc(norm_sum, 1)

        @block.scalar
        def _(act):
            act.sem_inc(rooted, 2)
            with act.Fori(0, GROUPS) as g:
                for t in range(6):
                    act.wait_ge(conv_ok, g * 6 + t + 1)
                    for j, (a, b) in enumerate(THIRDS):
                        act.wait_ge(proj_ok, g * NP + 3 * t + j + 1)
                        nc.scalar.activation(raw[:, t % 2, 3 + a:3 + b], bank(3 * (t % 2) + j, b - a), ACT.Copy).then_inc(raw_ok, 1)
                    if t >= 1:
                        act.wait_ge(conv_ok, g * 6 + t + 2)
                        nc.scalar.activation(feats[:, t - 1], feats[:, t - 1], ACT.Silu).then_inc(silu_ok, 1)
                act.wait_ge(conv_ok, g * 6 + 8)
                nc.scalar.activation(feats[:, 5], feats[:, 5], ACT.Silu).then_inc(silu_ok, 1)
                for c in range(8):
                    act.wait_ge(seg_ok, g * 8 + c + 1)
                    nc.scalar.activation(seg[:, (c + 1) % 2], seg[:, (c + 1) % 2], ACT.Exp).then_inc(exp_ok, 1)
                    act.wait_ge(zproj, g * 8 + c + 1)
                    nc.scalar.activation(z[:, c // 2, 512 * (c % 2):512 * (c % 2 + 1)], bank(0), ACT.Copy).then_inc(zcopy, 1)
                act.wait_ge(zcopy, g * 8 + 8)
                for f in range(4):
                    nc.scalar.activation(z[:, f], z[:, f], ACT.Silu).then_inc(zsilu, 1)
                for f in range(4):
                    act.wait_ge(u_ok, g * 4 + f + 1)
                    if f >= 2:
                        act.wait_ge(norm_sum, g * 4 + f - 1)
                    nc.scalar.activation(raw[:, f % 2, 3:3 + T], feats[:, f, META:L], ACT.Square).then_inc(sq_ok, 1)
                act.wait_ge(norm_sum, g * 4 + 4)
                for h in range(2):
                    nc.scalar.activation(rms[:, 512 * h:512 * (h + 1)], bank(2 + h), ACT.Sqrt, scale=1.0 / 512,
                                         bias=K.eps[:, 0:1]).then_inc(rooted, 1)
                for f in range(4):
                    act.wait_ge(yf_ok, g * 4 + f + 1)
                    act.dma_start(y_dst[g, f], feats[:, f, META:L]).then_inc(stored, 16)

        @block.vector
        def _(dve):
            dve.sem_inc(conv_ok, 2)
            nc.vector.memset(raw[:, :, 0:3], 0.0).then_inc(par_in, 16)
            dve.wait_ge(par_in, 32)
            with dve.Fori(0, GROUPS) as g:
                ch = Chain(dve, dchain, 1 + 6 * 3 + 7 + 1, g)
                tt, stt = nc.vector.tensor_tensor, nc.vector.scalar_tensor_tensor
                nc.vector.tensor_copy(smg[:, :, :, :], sm[:, g])
                ch.link(nc.vector.tensor_copy(cpg[:, :], par[:, g]))
                dve.sem_inc(small_ok, 1)
                dve.wait_ge(stored, g * 64 + 16)
                for t in range(6):
                    w = lambda k: cpg[:, 5 * t + k:5 * t + k + 1]
                    r, o = raw[:, t % 2], feats[:, t]
                    dve.wait_ge(raw_ok, g * NP + 3 * t + 3)
                    ch.link(nc.vector.tensor_scalar(o, r[:, 3:3 + L], w(3), w(4), ALU.mult, ALU.add))
                    ch.link(stt(o, r[:, 2:2 + L], w(2), o, ALU.mult, ALU.add))
                    ch.link(stt(o, r[:, 1:1 + L], w(1), o, ALU.mult, ALU.add))
                    stt(o, r[:, 0:L], w(0), o, ALU.mult, ALU.add).then_inc(conv_ok, 1)

                def make_xdt(c):
                    n = META if c == 0 else P
                    dve.wait_ge(xturn, g * 9 + c + 1)
                    if c >= 2:
                        dve.wait_ge(xst_ok, g * 8 + c - 1)
                    if c >= 3:
                        dve.wait_ge(ydiag_ok, g * 8 + c - 2)
                    tt(xdt[0:n, c % 2].rearrange("p (h d) -> p h d", h=HG), ps[0:n, 1024:1536].rearrange("p (h d) -> p h d", h=HG),
                       smg[0:n, 2, c].unsqueeze(2).to_broadcast([n, HG, 64]), ALU.mult).then_inc(xdt_ok, 1)

                def copy_b(c):
                    n = META if c == 0 else P
                    dve.wait_ge(bturn, g * 9 + c + 1)
                    if c >= 2:
                        dve.wait_ge(st_ok, g * 8 + c - 1)
                    nc.vector.tensor_copy(btok[0:n, c % 2], ps[0:n, 1536:1536 + P]).then_inc(b_ok, 1)

                make_xdt(0)
                copy_b(0)
                for c in range(NCH):
                    a, b = chunk_cols(c)
                    if c < 8:
                        d = c + 1
                        make_xdt(d)
                        if d < 8:
                            copy_b(d)
                        dve.wait_ge(bturn, g * 9 + d + 1)
                        tt(cb[:, d % 2], ps[:, 1664:1664 + P], K.tri[:, :], ALU.mult).then_inc(cb_ok, 1)
                        dve.wait_ge(sums_ok, g * 8 + d)
                        if d >= 3:
                            dve.wait_ge(ydiag_ok, g * 8 + d - 2)
                        for r in range(HG):
                            last = nc.vector.tensor_scalar(seg[:, d % 2, r], ps[:, 2048 + P * r:2048 + P * (r + 1)],
                                                           smg[:, 1, d, r:r + 1], smg[:, 1, d, r:r + 1], ALU.min, ALU.subtract)
                        last.then_inc(seg_ok, 1)
                    if c >= 1:
                        dve.wait_ge(yoff_ok, g * 8 + c)
                        tt(yoff[:, :].rearrange("p (h d) -> p h d", h=HG), bank(7).rearrange("p (h d) -> p h d", h=HG),
                           smg[:, 5, c].unsqueeze(2).to_broadcast([P, HG, 64]), ALU.mult).then_inc(t_ok, 1)
                        dve.wait_ge(t_ok, g * 8 + c)
                        dve.wait_ge(ydiag_ok, g * 8 + c)
                        if c >= 3:
                            dve.wait_ge(yturn, g * 8 + c - 2)
                        tt(ytok[:, c % 2], bank(6), yoff[:, :], ALU.add).then_inc(y_ok, 1)
                    if c <= 7:
                        if c == 0:
                            dve.wait_ge(st_ok, g * 8 + 1)
                            nc.vector.tensor_copy(state[:, :], bank(7)).then_inc(h_ok, 1)
                        else:
                            ch.link(tt(state[:, :].rearrange("p (h d) -> p h d", h=HG), state[:, :].rearrange("p (h d) -> p h d", h=HG),
                                       smg[:, 4, c].unsqueeze(2).to_broadcast([P, HG, 64]), ALU.mult))
                            dve.wait_ge(st_ok, g * 8 + c + 1)
                            tt(state[:, :], state[:, :], bank(7), ALU.add).then_inc(h_ok, 1)
                    if c < 8:
                        dve.wait_ge(exp_ok, g * 8 + c + 1)
                        dve.wait_ge(cb_ok, g * 8 + c + 1)
                        tt(seg[:, (c + 1) % 2], seg[:, (c + 1) % 2], cb[:, (c + 1) % 2].unsqueeze(1).to_broadcast([P, HG, P]),
                           ALU.mult).then_inc(m_ok, 1)
                    for e in ([c - 1] if 2 <= c < 8 else [7, 8] if c == 8 else []):
                        a, b = chunk_cols(e)
                        dve.wait_ge(yturn, g * 8 + e)
                        for f in range(4):
                            last = stt(feats[:, f, a:b], feats[:, f, a:b], cpg[:, 30 + f:31 + f], ps[:, 512 + P * f:512 + P * (f + 1)],
                                       ALU.mult, ALU.add)
                        last.then_inc(y1_ok, 1)
                dve.wait_ge(y1_ok, g * 8 + 8)
                for f in range(4):
                    dve.wait_ge(zsilu, g * 4 + f + 1)
                    tt(feats[:, f, META:L], feats[:, f, META:L], z[:, f], ALU.mult).then_inc(u_ok, 1)
                dve.wait_ge(rooted, g * 2 + 4)
                ch.link(nc.vector.reciprocal(rms[:, :], rms[:, :]))
                dve.wait_ge(sq_ok, g * 4 + 4)
                for f in range(4):
                    stt(feats[:, f, META:L], feats[:, f, META:L], cpg[:, 34 + f:35 + f], rms[:, :], ALU.mult, ALU.mult).then_inc(yf_ok, 1)
                dve.wait_ge(yf_ok, g * 4 + 4)
                assert ch.n == ch.per, ch.n


def ssd_out_phase(nc, K):
    with ExitStack() as ctx:
        sb = lambda n, sh, dt=F32: ctx.enter_context(nc.sbuf_tensor(n, sh, dt))
        W = Weights(nc, ctx, "wo1", 4)
        yraw = sb("yo_raw", [P, 4, 512])
        y_hi, y_lo = sb("yo_hi", [P, 16, 512], F32R), sb("yo_lo", [P, 16, 512], F32R)
        res = sb("yo_out", [P, 2, 512])
        s = lambda n: semaphore(nc, ctx, "so_" + n)
        y_in = [s(f"yin{r}") for r in range(4)]
        hi_ok, lo_ok, done, copied, stored = s("hi"), s("lo"), s("done"), s("copied"), [s("stored0"), s("stored1")]
        block = ctx.enter_context(nc.Block())
        ps = K.psum
        y_src = K.s["y"].rearrange("t p (h c) -> h t p c", h=2)
        out = K.s["pssd"].rearrange("f p (h c) -> h f p c", h=2)

        @block.sync
        def _(sp):
            W.credits_raw(sp)
            with sp.Fori(0, 2) as h:
                for k in range(16):
                    W.load(sp, h, 16, k, K.d["w_proj_ssd"][k])
            for r in range(2):
                sp.wait_ge(stored[r], 16 * 8 + 16)

        @block.gpsimd
        def _(pool):
            with pool.Fori(0, 2) as h:
                for n in range(16):
                    W.split(pool, h, 16, n)

        @block.tensor
        def _(pe):
            W.credits_used(pe)
            with pe.Fori(0, 2) as h:
                for f in range(8):
                    pe.wait_ge(copied, h * 8 + f + 1)
                    for p in range(2):
                        W.wait(pe, h, 16, 2 * f + p)
                        if f == 0:
                            pe.wait_ge(lo_ok, h * 16 + 8 * p + 8 + 4)
                        last = gemm(nc, ps[:, 512 * (f % 4):512 * (f % 4 + 1)], W.hi[:, p], W.lo[:, p],
                                    lambda k: y_hi[:, 8 * p + k], lambda k: y_lo[:, 8 * p + k], first=(p == 0), final=(p == 1))
                        last.then_inc(done, 1)
                        pe.wait_ge(done, h * 16 + 2 * f + p + 1)
                        pe.sem_inc(W.used, 1)

        @block.scalar
        def _(act):
            act.sem_inc(copied, 4)
            for r in range(2):
                act.sem_inc(stored[r], 16)
            with act.Fori(0, 2) as h:
                for k in range(-4, 16):
                    if k >= 0:
                        act.wait_ge(y_in[k % 4], h * 64 + 16 * (k // 4 + 1))
                        nc.scalar.activation(y_hi[:, k], yraw[:, k % 4], ACT.Copy).then_inc(hi_ok, 1)
                    if k + 4 < 16:
                        act.wait_ge(lo_ok, h * 16 + k + 5)
                        act.dma_start(yraw[:, k % 4], y_src[h, k + 4]).then_inc(y_in[k % 4], 16)
                for f in range(8):
                    act.wait_ge(done, h * 16 + 2 * f + 2)
                    act.wait_ge(stored[f % 2], h * 64 + 16 * (f // 2 + 1))
                    nc.scalar.activation(res[:, f % 2], ps[:, 512 * (f % 4):512 * (f % 4 + 1)], ACT.Copy).then_inc(copied, 1)
                    act.wait_ge(copied, h * 8 + f + 5)
                    act.dma_start(out[h, f], res[:, f % 2]).then_inc(stored[f % 2], 16)

        @block.vector
        def _(dve):
            dve.sem_inc(lo_ok, 4)
            with dve.Fori(0, 2) as h:
                for k in range(16):
                    dve.wait_ge(hi_ok, h * 16 + k + 1)
                    nc.vector.tensor_tensor(y_lo[:, k], yraw[:, k % 4], y_hi[:, k].bitcast(F32), ALU.subtract).then_inc(lo_ok, 1)


def pieces_of(n):
    return [(a, min(a + 512, n)) for a in range(0, n, 512)]


def run_passes(eng, n, one):
    with eng.Fori(0, n // 2 - 1) as i:
        one(i * 2, 0, True)
        one(i * 2 + 1, 1, True)
    one(n - 2, 0, True)
    one(n - 1, 1, False)


def fox_phase(nc, K, u_hi, u_lo):
    PAIRS = ATT_H // 2
    NB = 16
    step = [(b // 8, b % 8) for b in range(NB)]
    keys = lambda i: META + P * (i + 1)
    groups = [(b, k0, min(4, step[b][1] + 2 - k0)) for b in range(NB) for k0 in range(0, step[b][1] + 2, 4)]
    NG = len(groups)
    last_of = [max(x for x in range(NG) if groups[x][0] == b) for b in range(NB)]
    by_act = [x % 2 == 1 for x in range(NG)]
    n_act, n_dve = sum(by_act), NG - sum(by_act)
    units = [(0, a, b) for a, b in HALVES] + [(1, a, b) for a, b in THIRDS] + [(2, a, b) for a, b in THIRDS] + \
            [(3, a, b) for a, b in HALVES]
    NU, USES, PER = len(units), len(units) + 3, len(units) + 5
    items = [(u, k) for u in range(NU) for k in range(KT)] + [(NU + m, 0) for m in range(3)]
    share = lambda x: items[len(items) * x // NG:len(items) * (x + 1) // NG]
    with ExitStack() as ctx:
        sb = lambda n, sh, dt=F32: ctx.enter_context(nc.sbuf_tensor(n, sh, dt))
        W = Weights(nc, ctx, "wf", 2)
        qT, kT, vT, zT = sb("f_qT", [P, 2, T]), sb("f_kT", [P, 2, L]), sb("f_vT", [P, L]), sb("f_zT", [P, 2, T])
        vtok = sb("f_v", [P, 2, CH + 1, P])
        ncb = sb("f_decay", [P, 2, 2, L])
        S = sb("f_scores", [P, 3, L])
        pt = sb("f_pT", [P, 2, 4, P])
        otok = sb("f_o", [P, CH, P])
        yt = sb("f_y", [P, T])
        mx, nm, ls, rl = (sb(n, [P, 2, NB]) for n in ("f_max", "f_negmax", "f_sum", "f_rsum"))
        s = lambda n: semaphore(nc, ctx, "f_" + n)
        nc_in = [s("decay_in0"), s("decay_in1")]
        mm6, free6, carried = s("bank6_full"), s("bank6_free"), s("carried")
        qk_ok, ttr_ok, neg_ok, exp_ok = s("qk"), s("biased"), s("negmax"), s("exp")
        turned, copy_dve, copy_act, pv_ok = s("turned"), s("copy_dve"), s("copy_act"), s("pv")
        rl_ok, o_ok, z_ok, stored = s("rl"), s("o"), s("z"), s("stored")
        block = ctx.enter_context(nc.Block())
        ps = K.psum
        sbase = lambda i: 0 if i % 2 else 1536
        TB, FB, OB = 2560, 3072, 3584
        w_src = K.d["w_fox"].rearrange("(g n) p k -> g n p k", n=8)
        nc_src = K.s["nc"].rearrange("(g j) l -> g j l", j=4)

        def wait_copy(eng, p, x):
            if by_act[x]:
                eng.wait_ge(copy_act, p * n_act + x // 2 + 1)
            else:
                eng.wait_ge(copy_dve, p * n_dve + x // 2 + 1)

        @block.sync
        def _(sp):
            W.credits_raw(sp)
            with sp.Fori(0, PAIRS // 2) as i:
                for q in range(2):
                    for n in range(4):
                        W.load(sp, i, 8, 4 * q + n, w_src[i, 4 * q + n])
                    sp.wait_ge(ttr_ok, i * 2 * NB + q * NB + NB)
                    for j in range(2):
                        sp.dma_start(ncb[:, q, j], nc_src[i, 2 * q + j:2 * q + j + 1].to_broadcast([P, L])).then_inc(nc_in[q], 16)
            sp.wait_ge(stored, 16 * PAIRS + 16)

        @block.gpsimd
        def _(pool):
            with pool.Fori(0, PAIRS) as h:
                for n in range(4):
                    W.split(pool, h, 4, n)

        @block.tensor
        def _(pe):
            W.credits_used(pe)

            def project(p, r, item):
                u, k = item
                if k == 0:
                    pe.wait_ge(free6, p * PER + u + 1)
                if u < NU:
                    t, a, b = units[u]
                    if k == 0 and (u == 0 or units[u - 1][0] != t):
                        W.wait(pe, p, 4, t)
                    last = gemm_k(nc, ps[:, FB:FB + b - a], W.hi[:, t % 2], W.lo[:, t % 2], u_hi[:, k, a:b], u_lo[:, k, a:b], k)
                    if k == KT - 1:
                        last.then_inc(mm6, 1)
                else:
                    for c in range(4 * (u - NU), min(4 * (u - NU) + 4, CH + 1)):
                        a, b = (META + P * c, META + P * (c + 1)) if c < CH else (0, META)
                        last = nc.tensor.transpose(ps[0:b - a, FB + P * (c % 4):FB + P * (c % 4 + 1)], vT[:, a:b], K.ident[:, :])
                    last.then_inc(mm6, 1)

            def scores(p, r, b):
                j, i = step[b]
                pe.wait_ge(ttr_ok, p * NB + 2 * NB + b - 1)
                if b == 0:
                    pe.wait_ge(free6, p * PER + USES + 1)
                d0, d1 = META + P * i, META + P * (i + 1)
                for a, e in pieces_of(keys(i)):
                    masked = d0 < e and d1 > a
                    last = nc.tensor.matmul(ps[:, sbase(i) + a:sbase(i) + e], qT[64 * j:64 * j + 64, r, P * i:P * (i + 1)],
                                            kT[64 * j:64 * j + 64, r, a:e], start=True, stop=not masked)
                    if masked:
                        x, y = max(a, d0), min(e, d1)
                        last = nc.tensor.matmul(ps[:, sbase(i) + x:sbase(i) + y], K.identb[:, :],
                                                K.maskb[:, x - d0:y - d0], start=False, stop=True)
                last.then_inc(qk_ok, 1)

            def turn(p, x):
                b, k0, n = groups[x]
                if k0 == 0:
                    pe.wait_ge(exp_ok, p * NB + b + 1)
                if x >= 1:
                    wait_copy(pe, p, x - 1)
                for m in range(n):
                    c = 0 if k0 + m == 0 else META + P * (k0 + m - 1)
                    last = nc.tensor.transpose(ps[:, TB + P * m:TB + P * (m + 1)], S[:, b % 3, c:c + P], K.ident[:, :])
                last.then_inc(turned, 1)

            def values(p, r, x):
                b, k0, n = groups[x]
                j, i = step[b]
                if k0 == 0:
                    pe.wait_ge(o_ok, p * NB + b + 1)
                wait_copy(pe, p, x)
                for m in range(n):
                    kb = k0 + m
                    rows, c = (META, CH) if kb == 0 else (P, kb - 1)
                    last = nc.tensor.matmul(ps[:, OB:OB + 64], pt[0:rows, x % 2, m], vtok[0:rows, r, c, 64 * j:64 * j + 64],
                                            start=(kb == 0), stop=(kb == i + 1))
                last.then_inc(pv_ok, 1)

            def one(p, r, more):
                for x in range(NG):
                    b, k0, n = groups[x]
                    turn(p, x)
                    if k0 == 0 and b + 2 < NB:
                        scores(p, r, b + 2)
                    if more:
                        for item in share(x):
                            project(p + 1, 1 - r, item)
                    if x >= 1:
                        values(p, r, x - 1)
                values(p, r, NG - 1)
                if more:
                    scores(p + 1, 1 - r, 0)
                    scores(p + 1, 1 - r, 1)
                pe.wait_ge(o_ok, p * NB + NB + 1)
                for hf in range(2):
                    pe.wait_ge(free6, p * PER + PER + (USES if more else 0) + hf + 1)
                    for m in range(4):
                        last = nc.tensor.transpose(ps[:, FB + P * m:FB + P * (m + 1)], otok[:, 4 * hf + m], K.ident[:, :])
                    last.then_inc(mm6, 1)

            for item in items:
                project(0, 0, item)
            scores(0, 0, 0)
            pe.sem_inc(mm6, 2)
            scores(0, 0, 1)
            run_passes(pe, PAIRS, one)

        @block.scalar
        def _(act):
            act.sem_inc(free6, 1)

            def empty6(p, r, u):
                act.wait_ge(mm6, p * PER + u + 1)
                if u < NU:
                    t, a, b = units[u]
                    if u + 1 == NU or units[u + 1][0] != t:
                        act.sem_inc(W.used, 1)
                    dst = [qT[:, r, a - META:b - META], kT[:, r, a:b], vT[:, a:b], zT[:, r, a - META:b - META]][t]
                    nc.scalar.activation(dst, ps[:, FB:FB + b - a], ACT.Copy).then_inc(free6, 1)
                elif u < NU + 2:
                    m = u - NU
                    nc.scalar.activation(vtok[:, r, 4 * m:4 * m + 4].rearrange("p c n -> p (c n)"), ps[:, FB:FB + 512], ACT.Copy).then_inc(free6, 1)
                else:
                    nc.scalar.activation(vtok[0:META, r, CH], ps[0:META, FB:FB + P], ACT.Copy).then_inc(free6, 1)

            def exps(p, r, b):
                n = keys(step[b][1])
                act.wait_ge(neg_ok, p * NB + b + 1)
                nc.scalar.activation(S[:, b % 3, 0:n], S[:, b % 3, 0:n], ACT.Exp, bias=nm[:, r, b:b + 1],
                                     accum_out=ls[:, r, b:b + 1]).then_inc(exp_ok, 1)

            def one(p, r, more):
                for x in range(NG):
                    b, k0, n = groups[x]
                    if by_act[x]:
                        act.wait_ge(turned, p * NG + x + 1 + NG)
                        if x >= 2:
                            act.wait_ge(pv_ok, p * NG + x - 1)
                        nc.scalar.activation(pt[:, x % 2, 0:n].rearrange("p m n -> p (m n)"), ps[:, TB:TB + P * n], ACT.Copy).then_inc(copy_act, 1)
                    if k0 == 0 and b + 2 < NB:
                        exps(p, r, b + 2)
                    if more:
                        for u, k in share(x):
                            if k == KT - 1 or u >= NU:
                                empty6(p + 1, 1 - r, u)
                if more:
                    exps(p + 1, 1 - r, 0)
                    exps(p + 1, 1 - r, 1)
                nc.scalar.activation(zT[:, r], zT[:, r], ACT.Silu).then_inc(z_ok, 1)
                act.wait_ge(free6, p * PER + PER + (USES if more else 0) + 3)
                act.dma_start(y_dst(p), yt[:, :]).then_inc(stored, 16)

            def y_dst(p):
                return K.s["yatt"][bass.ds(p, 1)].rearrange("a p t -> (a p) t")

            for u in range(USES):
                empty6(0, 0, u)
            act.wait_ge(free6, USES + 1)
            act.sem_inc(free6, 2)
            exps(0, 0, 0)
            exps(0, 0, 1)
            run_passes(act, PAIRS, one)

        @block.vector
        def _(dve):
            dve.sem_inc(ttr_ok, 2 * NB)
            dve.sem_inc(turned, NG)
            dve.sem_inc(o_ok, 1)
            dve.sem_inc(stored, 16)

            def biased(p, r, b):
                j, i = step[b]
                n = keys(i)
                if b == 0:
                    dve.wait_ge(nc_in[r], p * 16 + 32 - 16 * r)
                dve.wait_ge(qk_ok, p * NB + b + 1)
                dve.wait_ge(turned, p * NG + last_of[b - 3] + 1 - (NG if b < 3 else 0) + NG)
                dve.sem_inc(carried, 1)
                nc.vector.tensor_tensor_reduce(out=S[:, b % 3, 0:n], in0=ps[:, sbase(i):sbase(i) + n], in1=ncb[:, r, j, 0:n],
                                               scale=0.125, scalar=-3e38, op0=ALU.add, op1=ALU.max,
                                               accum_out=mx[:, r, b:b + 1]).then_inc(ttr_ok, 1)
                dve.wait_ge(ttr_ok, p * NB + 2 * NB + b + 1)
                nc.vector.tensor_scalar(nm[:, r, b:b + 1], mx[:, r, b:b + 1], -1.0, None, ALU.mult).then_inc(neg_ok, 1)

            def one(p, r, more):
                for x in range(NG):
                    b, k0, n = groups[x]
                    if not by_act[x]:
                        dve.wait_ge(turned, p * NG + x + 1 + NG)
                        if x >= 2:
                            dve.wait_ge(pv_ok, p * NG + x - 1)
                        nc.vector.tensor_copy(pt[:, x % 2, 0:n].rearrange("p m n -> p (m n)"), ps[:, TB:TB + P * n]).then_inc(copy_dve, 1)
                    if k0 == 0 and b + 2 < NB:
                        biased(p, r, b + 2)
                    if x >= 1 and x - 1 == last_of[groups[x - 1][0]]:
                        output(p, r, groups[x - 1][0])
                output(p, r, NB - 1)
                if more:
                    biased(p + 1, 1 - r, 0)
                    biased(p + 1, 1 - r, 1)
                dve.wait_ge(stored, p * 16 + 16)
                dve.wait_ge(z_ok, p + 1)
                for hf in range(2):
                    dve.wait_ge(mm6, p * PER + PER + (USES if more else 0) + hf + 1)
                    nc.vector.tensor_tensor(yt[:, 512 * hf:512 * (hf + 1)], ps[:, FB:FB + 512],
                                            zT[:, r, 512 * hf:512 * (hf + 1)], ALU.mult).then_inc(free6, 1)

            def output(p, r, b):
                j, i = step[b]
                dve.wait_ge(exp_ok, p * NB + b + 1)
                nc.vector.reciprocal(rl[:, r, b:b + 1], ls[:, r, b:b + 1]).then_inc(rl_ok, 1)
                dve.wait_ge(rl_ok, p * NB + b + 1)
                dve.wait_ge(pv_ok, p * NG + last_of[b] + 1)
                nc.vector.tensor_scalar(otok[:, i, 64 * j:64 * j + 64], ps[:, OB:OB + 64], rl[:, r, b:b + 1], None,
                                        ALU.mult).then_inc(o_ok, 1)

            biased(0, 0, 0)
            biased(0, 0, 1)
            run_passes(dve, PAIRS, one)


def merge_phase(nc, K, u_hi, u_lo):
    with ExitStack() as ctx:
        sb = lambda n, sh, dt=F32: ctx.enter_context(nc.sbuf_tensor(n, sh, dt))
        W = Weights(nc, ctx, "wm", 3)
        raw = sb("m_raw", [P, 2, T])
        y_hi, y_lo = sb("m_yhi", [P, KT, T], F32R), sb("m_ylo", [P, KT, T], F32R)
        pssd = sb("m_pssd", [P, 2, T])
        sg, sa = sb("m_sg", [P, T]), sb("m_sa", [P, T])
        bias = sb("m_bias", [P, 2 * KT])
        s = lambda n: semaphore(nc, ctx, "m_" + n)
        y_in, hi_ok, lo_ok, p_in = [s("yin0"), s("yin1")], s("hi"), s("lo"), [s("pin0"), s("pin1")]
        b_in, unit, sig_ok, g1_ok, g2_ok, gm, m_ok = s("bin"), s("unit"), s("sig"), s("g1"), s("g2"), s("gm"), s("m")
        stored = [s("stored0"), s("stored1")]
        block = ctx.enter_context(nc.Block())
        ps = K.psum
        w_src = K.d["w_merge"].rearrange("(g n) p k -> g n p k", n=6)

        def store(act, f):
            act.wait_ge(m_ok, f + 1)
            act.dma_start(K.s["merged"][f], pssd[:, f % 2]).then_inc(stored[f % 2], 16)
            if f + 2 < KT:
                act.wait_ge(stored[f % 2], 16 * (f // 2 + 1))
                act.dma_start(pssd[:, f % 2], K.s["pssd"][f + 2]).then_inc(p_in[f % 2], 16)

        @block.sync
        def _(sp):
            W.credits_raw(sp)
            sp.dma_start(bias[:, :], K.d["gate_bias"]).then_inc(b_in, 16)
            with sp.Fori(0, 4) as g:
                for n in range(6):
                    W.load(sp, g, 6, n, w_src[g, n])

        @block.gpsimd
        def _(pool):
            with pool.Fori(0, 4) as g:
                for n in range(6):
                    W.split(pool, g, 6, n)

        @block.tensor
        def _(pe):
            W.credits_used(pe)
            with pe.Fori(0, 4) as g:
                for q in range(2):
                    for n in range(3):
                        W.wait(pe, g, 6, 3 * q + n)
                        if n < 2:
                            pe.wait_ge(sig_ok, g * 8 + 4 * q + 2 * n + 2)
                        else:
                            pe.wait_ge(g2_ok, g * 4 + 2 * q + 2)
                            if q == 0:
                                pe.wait_ge(lo_ok, KT)
                        wl, wh = W.lo[:, (3 * q + n) % 2], W.hi[:, (3 * q + n) % 2]
                        for h in range(2):
                            if n < 2:
                                act_hi = lambda k: u_hi[:, k, META + 512 * h:META + 512 * (h + 1)]
                                act_lo = lambda k: u_lo[:, k, META + 512 * h:META + 512 * (h + 1)]
                            else:
                                act_hi = lambda k: y_hi[:, k, 512 * h:512 * (h + 1)]
                                act_lo = lambda k: y_lo[:, k, 512 * h:512 * (h + 1)]
                            gemm(nc, ps[:, 1024 * n + 512 * h:1024 * n + 512 * (h + 1)], wh, wl, act_hi, act_lo).then_inc(unit, 1)
                        pe.wait_ge(unit, g * 12 + 6 * q + 2 * n + 2)
                        pe.sem_inc(W.used, 1)

        @block.scalar
        def _(act):
            act.sem_inc(sig_ok, 4)
            for k in range(2):
                act.dma_start(raw[:, k], K.s["yatt"][k]).then_inc(y_in[k], 16)
                act.dma_start(pssd[:, k], K.s["pssd"][k]).then_inc(p_in[k], 16)
            for k in range(KT):
                act.wait_ge(y_in[k % 2], 16 * (k // 2 + 1))
                nc.scalar.activation(y_hi[:, k], raw[:, k % 2], ACT.Copy).then_inc(hi_ok, 1)
                if k + 2 < KT:
                    act.wait_ge(lo_ok, k + 1)
                    act.dma_start(raw[:, k % 2], K.s["yatt"][k + 2]).then_inc(y_in[k % 2], 16)
            act.wait_ge(b_in, 16)
            for f in range(KT):
                for n in range(2):
                    for h in range(2):
                        act.wait_ge(unit, 6 * f + 2 * n + h + 1)
                        if f >= 1:
                            act.wait_ge(g1_ok if n == 0 else g2_ok, 2 * f if n == 0 else 2 * f + 2)
                        nc.scalar.activation((sa if n else sg)[:, 512 * h:512 * (h + 1)], ps[:, 1024 * n + 512 * h:1024 * n + 512 * (h + 1)],
                                             ACT.Sigmoid, bias=bias[:, KT * n + f:KT * n + f + 1]).then_inc(sig_ok, 1)
                if f >= 1:
                    store(act, f - 1)
            store(act, KT - 1)
            for f in (KT - 2, KT - 1):
                act.wait_ge(stored[f % 2], 64)

        @block.vector
        def _(dve):
            dve.sem_inc(g2_ok, 2)
            for k in range(KT):
                dve.wait_ge(hi_ok, k + 1)
                nc.vector.tensor_tensor(y_lo[:, k], raw[:, k % 2], y_hi[:, k].bitcast(F32), ALU.subtract).then_inc(lo_ok, 1)
            for f in range(KT):
                dve.wait_ge(p_in[f % 2], 16 * (f // 2 + 1))
                p = pssd[:, f % 2]
                for h in range(2):
                    c = slice(512 * h, 512 * (h + 1))
                    dve.wait_ge(sig_ok, 4 + 4 * f + h + 1)
                    nc.vector.tensor_tensor(p[:, c], p[:, c], sg[:, c], ALU.mult).then_inc(g1_ok, 1)
                for h in range(2):
                    c = slice(512 * h, 512 * (h + 1))
                    dve.wait_ge(unit, 6 * f + 4 + h + 1)
                    dve.wait_ge(sig_ok, 4 + 4 * f + 2 + h + 1)
                    nc.vector.tensor_tensor(sa[:, c], sa[:, c], ps[:, 2048 + 512 * h:2048 + 512 * (h + 1)], ALU.mult).then_inc(gm, 1)
                    dve.wait_ge(gm, 2 * f + h + 1)
                    dve.wait_ge(g1_ok, 2 * f + h + 1)
                    last = nc.vector.tensor_tensor(p[:, c], p[:, c], sa[:, c], ALU.add)
                    last.then_inc(g2_ok, 1)
                dve.wait_ge(g2_ok, 2 * f + 4)
                dve.sem_inc(m_ok, 1)


def linear_phase(nc, K, name, src, w_src, dst, raw_slots=4):
    with ExitStack() as ctx:
        sb = lambda n, sh, dt=F32: ctx.enter_context(nc.sbuf_tensor(name + n, sh, dt))
        W = Weights(nc, ctx, name + "w", raw_slots)
        raw = sb("_raw", [P, 4, T])
        a_hi, a_lo = sb("_hi", [P, KT, T], F32R), sb("_lo", [P, KT, T], F32R)
        s = lambda n: semaphore(nc, ctx, name + n)
        a_in, hi_ok, lo_ok, unit, copied = [s(f"_in{r}") for r in range(4)], s("_hi_ok"), s("_lo_ok"), s("_unit"), s("_copied")
        block = ctx.enter_context(nc.Block())
        ps = K.psum

        @block.sync
        def _(sp):
            W.credits_raw(sp)
            for k in range(2):
                W.load(sp, 0, 8, k, w_src[k])
            for k in range(KT):
                if k >= 4:
                    sp.wait_ge(lo_ok, k - 3)
                sp.dma_start(raw[:, k % 4], src[k]).then_inc(a_in[k % 4], 16)
            for k in range(2, KT):
                W.load(sp, 0, 8, k, w_src[k])

        @block.gpsimd
        def _(pool):
            for n in range(KT):
                W.split(pool, 0, 8, n)

        @block.tensor
        def _(pe):
            W.credits_used(pe)
            pe.wait_ge(lo_ok, KT)
            for f in range(KT):
                W.wait(pe, 0, 8, f)
                for h in range(2):
                    u = 2 * f + h
                    if u >= 8:
                        pe.wait_ge(copied, u - 7)
                    gemm(nc, ps[:, 512 * (u % 8):512 * (u % 8 + 1)], W.hi[:, f % 2], W.lo[:, f % 2],
                         lambda k: a_hi[:, k, 512 * h:512 * (h + 1)], lambda k: a_lo[:, k, 512 * h:512 * (h + 1)]).then_inc(unit, 1)
                pe.wait_ge(unit, 2 * f + 2)
                pe.sem_inc(W.used, 1)

        @block.scalar
        def _(act):
            for k in range(KT):
                act.wait_ge(a_in[k % 4], 16 * (k // 4 + 1))
                nc.scalar.activation(a_hi[:, k], raw[:, k % 4], ACT.Copy).then_inc(hi_ok, 1)
            for u in range(2 * KT):
                act.wait_ge(unit, u + 1)
                nc.scalar.activation(dst[:, u // 2, 512 * (u % 2):512 * (u % 2 + 1)], ps[:, 512 * (u % 8):512 * (u % 8 + 1)],
                                     ACT.Copy).then_inc(copied, 1)

        @block.vector
        def _(dve):
            for k in range(KT):
                dve.wait_ge(hi_ok, k + 1)
                nc.vector.tensor_tensor(a_lo[:, k], raw[:, k % 4], a_hi[:, k].bitcast(F32), ALU.subtract).then_inc(lo_ok, 1)


def residual_phase(nc, K, o, gain, xr):
    with ExitStack() as ctx:
        sb = lambda n, sh, dt=F32: ctx.enter_context(nc.sbuf_tensor(n, sh, dt))
        sq, rs = sb("r_sq", [P, 2, T]), sb("r_rs", [P, T])
        s = lambda n: semaphore(nc, ctx, "r_" + n)
        x_in, squared, summed, rooted, inv, scaled, added = (s(n) for n in ["xin", "squared", "summed", "rooted", "inv", "scaled", "added"])
        block = ctx.enter_context(nc.Block())
        ps = K.psum

        @block.sync
        def _(sp):
            sp.dma_start(xr[:, :, :], K.s["xT"].rearrange("k p t -> p k t")).then_inc(x_in, 16)

        @block.scalar
        def _(act):
            for k in range(KT):
                if k >= 2:
                    act.wait_ge(summed, k - 1)
                nc.scalar.activation(sq[:, k % 2], o[:, k], ACT.Square).then_inc(squared, 1)
            act.wait_ge(summed, KT)
            for h in range(2):
                nc.scalar.activation(rs[:, 512 * h:512 * (h + 1)], ps[:, 512 * h:512 * (h + 1)], ACT.Sqrt, scale=1.0 / D,
                                     bias=K.eps[:, 0:1]).then_inc(rooted, 1)

        @block.tensor
        def _(pe):
            for k in range(KT):
                pe.wait_ge(squared, k + 1)
                for h in range(2):
                    last = nc.tensor.matmul(ps[:, 512 * h:512 * (h + 1)], K.ones[:, :], sq[:, k % 2, 512 * h:512 * (h + 1)],
                                            start=(k == 0), stop=(k == KT - 1))
                last.then_inc(summed, 1)

        @block.vector
        def _(dve):
            dve.wait_ge(rooted, 2)
            nc.vector.reciprocal(rs[:, :], rs[:, :]).then_inc(inv, 1)
            dve.wait_ge(inv, 1)
            for k in range(KT):
                nc.vector.scalar_tensor_tensor(o[:, k], o[:, k], gain[:, k:k + 1], rs[:, :], ALU.mult, ALU.mult).then_inc(scaled, 1)
            dve.wait_ge(x_in, 16)
            for k in range(KT):
                dve.wait_ge(scaled, k + 1)
                nc.vector.tensor_tensor(xr[:, k], xr[:, k], o[:, k], ALU.add).then_inc(added, 1)


def mixer_phase(nc, K, name, dil, u_hi, u_lo):
    NPASS, NB, NI = 4, 16, 8
    step = [(b // 8, b % 8) for b in range(NB)] if dil else [(b % 2, b // 2) for b in range(NB)]
    LEN = 2 * T - P
    NT = NB if dil else NI
    VW = 64 if dil else P
    with ExitStack() as ctx:
        sb = lambda n, sh, dt=F32: ctx.enter_context(nc.sbuf_tensor(name + n, sh, dt))
        W = Weights(nc, ctx, name + "w", 2)
        qk, vT, zT = sb("_qk", [P, 2, T]), sb("_vT", [P, T]), sb("_zT", [P, T])
        vtok = sb("_v", [P, CH, P])
        dist = sb("_dist", [P, LEN])
        count = sb("_count", [P, LEN]) if dil else None
        bias = sb("_bias", [P, 2 if dil else 1, LEN])
        slopes = sb("_slopes", [P, 8])
        par = sb("_par", [P, 3])
        S = sb("_scores", [P, 4, T])
        sq, rs = S[:, 0:2], S[:, 2:4]
        pt = sb("_pT", [P, 2, 4, P])
        otok = sb("_o", [P, CH, P])
        osq = sb("_osq", [P, P])
        yt = vT
        mx, nm, ls, rl = (sb(n, [P, NB]) for n in ("_max", "_negmax", "_sum", "_rsum"))
        oss, ors = sb("_oss", [P, NI]), sb("_ors", [P, NI])
        s = lambda n: semaphore(nc, ctx, name + n)
        par_in, proj, proj_ok, squared, summed, rooted, inv, qk_ready = (s("_" + n) for n in
            ["par", "proj", "proj_ok", "squared", "summed", "rooted", "inv", "qk_ready"])
        vturn, v_ok, bias_ok, qk_ok, ttr_ok, neg_ok, exp_ok, carried = (s("_" + n) for n in
            ["vturn", "v_ok", "bias_ok", "qk_ok", "ttr", "neg", "exp", "carried"])
        turned, pt0, pt1, pv_ok, rl_ok, part_ok, w_ok, o_ok, ss_ok, or_ok, on_ok, oturn, y_ok, stored = (s("_" + n) for n in
            ["turned", "pt0", "pt1", "pv", "rl", "part", "w", "o", "ss", "or", "on", "oturn", "y", "stored"])
        block = ctx.enter_context(nc.Block())
        ps = K.psum
        w_src = (K.d["w_dil"] if dil else K.d["w_diff"]).rearrange("(g n) p k -> g n p k", g=NPASS)
        tile0 = 4 if dil else 0
        y_dst = K.s["mix"]
        units = [(t, 512 * h, 512 * (h + 1)) for t in range(4) for h in range(2)]
        n_par = 4 if dil else 3

        @block.sync
        def _(sp):
            W.credits_raw(sp)
            sp.dma_start(dist[:, :], K.d["dist"]).then_inc(par_in, 16)
            if dil:
                sp.dma_start(count[:, :], K.d["count"]).then_inc(par_in, 16)
            sp.dma_start(slopes[:, :], K.d["slopes_dil"] if dil else K.d["slopes_diff"]).then_inc(par_in, 16)
            sp.dma_start(par[:, :], K.d["par_dil"] if dil else K.d["par_diff"]).then_inc(par_in, 16)
            with sp.Fori(0, NPASS) as h:
                for n in range(4):
                    W.load(sp, h, 4, n, w_src[h, n])

        @block.gpsimd
        def _(pool):
            with pool.Fori(0, NPASS) as h:
                for n in range(4):
                    W.split(pool, h, 4, n)

        @block.tensor
        def _(pe):
            W.credits_used(pe)
            with pe.Fori(0, NPASS) as h:
                pe.wait_ge(y_ok, h * 2 + 2)
                for u, (t, a, b) in enumerate(units):
                    if u % 2 == 0:
                        W.wait(pe, h, 4, t)
                    if u >= 4:
                        pe.wait_ge(proj_ok, h * 8 + u - 3)
                    gemm(nc, ps[:, 512 * (u % 4):512 * (u % 4 + 1)], W.hi[:, t % 2], W.lo[:, t % 2],
                         lambda k: u_hi[:, k, a:b], lambda k: u_lo[:, k, a:b]).then_inc(proj, 1)
                    if u % 2 == 1:
                        pe.wait_ge(proj, h * 8 + u + 1)
                        pe.sem_inc(W.used, 1)
                    if u in (3, 5):
                        m = (u - 3) // 2
                        pe.wait_ge(squared, h * 2 + m + 1)
                        for f in range(2):
                            last = nc.tensor.matmul(ps[:, 2048 + 1024 * m + 512 * f:2048 + 1024 * m + 512 * (f + 1)], K.pairs[:, :],
                                                    sq[:, m, 512 * f:512 * (f + 1)], start=True, stop=True)
                        last.then_inc(summed, 1)
                pe.wait_ge(proj_ok, h * 8 + 6)
                pe.wait_ge(rooted, h * 2 + 2)
                for c in range(CH):
                    last = nc.tensor.transpose(ps[:, 2048 + P * c:2048 + P * (c + 1)], vT[:, P * c:P * (c + 1)], K.ident[:, :])
                last.then_inc(vturn, 1)
                pe.wait_ge(proj_ok, h * 8 + 8)
                pe.wait_ge(qk_ready, h * 2 + 2)

                def scores(b):
                    j, i = step[b]
                    if b >= 2:
                        pe.wait_ge(ttr_ok, h * NB + b - 1)
                    for f in range(2):
                        last = nc.tensor.matmul(ps[:, 1024 * (b % 2) + 512 * f:1024 * (b % 2) + 512 * (f + 1)],
                                                qk[64 * j:64 * j + 64, 0, P * i:P * (i + 1)],
                                                qk[64 * j:64 * j + 64, 1, 512 * f:512 * (f + 1)], start=True, stop=True)
                    last.then_inc(qk_ok, 1)

                def turn(r, g):
                    x = 2 * r + g
                    slot = r % 4 if dil else 2 * r % 4
                    if g == 0:
                        pe.wait_ge(exp_ok if dil else w_ok, h * NT + r + 1)
                    if r >= 1:
                        pe.wait_ge(pt1 if g else pt0, h * NT + r)
                    for m in range(4):
                        last = nc.tensor.transpose(ps[:, 2048 + 512 * g + P * m:2048 + 512 * g + P * (m + 1)],
                                                   S[:, slot, 512 * g + P * m:512 * g + P * (m + 1)], K.ident[:, :])
                    last.then_inc(turned, 1)

                def values(r, g):
                    j = step[r][0] if dil else 0
                    if g == 0 and r >= 1:
                        pe.wait_ge(o_ok, h * NT + r)
                    pe.wait_ge(pt1 if g else pt0, h * NT + r + 1)
                    for m in range(4):
                        last = nc.tensor.matmul(ps[:, 3072:3072 + VW], pt[:, g, m], vtok[:, 4 * g + m, 64 * j:64 * j + VW],
                                                start=(g == 0 and m == 0), stop=(g == 1 and m == 3))
                    last.then_inc(pv_ok, 1)

                scores(0)
                scores(1)
                pe.wait_ge(v_ok, h + 1)
                for r in range(NT):
                    nxt = [r + 2] if dil else [2 * r + 2, 2 * r + 3]
                    turn(r, 0)
                    turn(r, 1)
                    if nxt[0] < NB:
                        scores(nxt[0])
                    values(r, 0)
                    if len(nxt) > 1 and nxt[1] < NB:
                        scores(nxt[1])
                    values(r, 1)
                for hf in range(2):
                    pe.wait_ge(o_ok if dil else on_ok, h * NT + NT if dil else h + 1)
                    for m in range(4):
                        last = nc.tensor.transpose(ps[:, 512 * hf + P * m:512 * hf + P * (m + 1)], otok[:, 4 * hf + m], K.ident[:, :])
                    last.then_inc(oturn, 1)

        @block.scalar
        def _(act):
            with act.Fori(0, NPASS) as h:
                for u, (t, a, b) in enumerate(units):
                    if u == 4:
                        act.wait_ge(stored, h * 16 + 16)
                    act.wait_ge(proj, h * 8 + u + 1)
                    dst = [qk[:, 0, a:b], qk[:, 1, a:b], vT[:, a:b], zT[:, a:b]][t]
                    nc.scalar.activation(dst, ps[:, 512 * (u % 4):512 * (u % 4 + 1)], ACT.Silu if t == 3 else ACT.Copy).then_inc(proj_ok, 1)
                    if u in (1, 3):
                        m = u // 2
                        act.wait_ge(proj_ok, h * 8 + u + 1)
                        nc.scalar.activation(sq[:, m], qk[:, m], ACT.Square).then_inc(squared, 1)
                    if u == 5:
                        for m in range(2):
                            act.wait_ge(summed, h * 2 + m + 1)
                            nc.scalar.activation(rs[:, m], ps[:, 2048 + 1024 * m:3072 + 1024 * m], ACT.Sqrt, scale=1.0 / 64,
                                                 bias=K.eps[:, 0:1]).then_inc(rooted, 1)
                act.wait_ge(vturn, h + 1)
                nc.scalar.activation(vtok[:, :, :].rearrange("p c n -> p (c n)"), ps[:, 2048:3072], ACT.Copy).then_inc(v_ok, 1)

                def exps(b):
                    act.wait_ge(neg_ok, h * NB + b + 1)
                    nc.scalar.activation(S[:, b % 4], S[:, b % 4], ACT.Exp, bias=nm[:, b:b + 1],
                                         accum_out=ls[:, b:b + 1]).then_inc(exp_ok, 1)

                def copy(r, g):
                    act.wait_ge(turned, h * 2 * NT + 2 * r + g + 1)
                    if r >= 1:
                        act.wait_ge(pv_ok, h * 2 * NT + 2 * r - 1 + g)
                    nc.scalar.activation(pt[:, g].rearrange("p m n -> p (m n)"), ps[:, 2048 + 512 * g:2048 + 512 * (g + 1)],
                                         ACT.Copy).then_inc(pt1 if g else pt0, 1)

                exps(0)
                exps(1)
                for r in range(NT):
                    if not dil:
                        copy(r, 0)
                    copy(r, 1)
                    for b in ([r + 2] if dil else [2 * r + 2, 2 * r + 3]):
                        if b < NB:
                            exps(b)
                    if not dil:
                        act.wait_ge(o_ok, h * NT + r + 1)
                        nc.scalar.activation(osq[:, :], otok[:, r], ACT.Square, accum_out=oss[:, r:r + 1]).then_inc(ss_ok, 1)
                        act.wait_ge(ss_ok, h * (NT + 1) + r + 1)
                if not dil:
                    nc.scalar.activation(oss[:, :], oss[:, :], ACT.Sqrt, scale=1.0 / P, bias=K.eps[:, 0:1]).then_inc(ss_ok, 1)
                act.wait_ge(y_ok, h * 2 + 4)
                act.dma_start(y_dst[tile0:tile0 + 4][h], yt[:, :]).then_inc(stored, 16)
            act.wait_ge(stored, 16 * NPASS + 16)

        @block.vector
        def _(dve):
            dve.sem_inc(y_ok, 2)
            dve.sem_inc(stored, 16)
            dve.wait_ge(par_in, 16 * n_par)
            stt, tt = nc.vector.scalar_tensor_tensor, nc.vector.tensor_tensor
            with dve.Fori(0, NPASS) as h:
                for m in range(2 if dil else 1):
                    if dil:
                        stt(bias[:, m], dist[:, :], slopes.rearrange("p (h m) -> p h m", m=2)[:, h, m:m + 1], count[:, :],
                            ALU.mult, ALU.add).then_inc(bias_ok, 1)
                    else:
                        nc.vector.tensor_scalar(bias[:, m], dist[:, :], slopes[:, bass.ds(h, 1)], None, ALU.mult).then_inc(bias_ok, 1)
                for m in range(2):
                    dve.wait_ge(rooted, h * 2 + m + 1)
                    nc.vector.reciprocal(rs[:, m], rs[:, m]).then_inc(inv, 1)
                    dve.wait_ge(inv, h * 2 + m + 1)
                    dve.wait_ge(squared, h * 2 + m + 1)
                    stt(qk[:, m], qk[:, m], par[:, m:m + 1], rs[:, m], ALU.mult, ALU.mult).then_inc(qk_ready, 1)
                dve.wait_ge(bias_ok, h + 1 if not dil else h * 2 + 2)

                def biased(b):
                    j, i = step[b]
                    dve.wait_ge(qk_ok, h * NB + b + 1)
                    if b >= 4:
                        r = b - 4 if dil else b // 2 - 2
                        dve.wait_ge(turned, h * 2 * NT + 2 * r + 2)
                    dve.sem_inc(carried, 1)
                    o = T - P - P * i
                    nc.vector.tensor_tensor_reduce(out=S[:, b % 4], in0=ps[:, 1024 * (b % 2):1024 * (b % 2 + 1)],
                                                   in1=bias[:, j if dil else 0, o:o + T], scale=0.125, scalar=-3e38,
                                                   op0=ALU.add, op1=ALU.max, accum_out=mx[:, b:b + 1]).then_inc(ttr_ok, 1)
                    dve.wait_ge(ttr_ok, h * NB + b + 1)
                    nc.vector.tensor_scalar(nm[:, b:b + 1], mx[:, b:b + 1], -1.0, None, ALU.mult).then_inc(neg_ok, 1)

                def inverse(b):
                    dve.wait_ge(exp_ok, h * NB + b + 1)
                    nc.vector.reciprocal(rl[:, b:b + 1], ls[:, b:b + 1]).then_inc(rl_ok, 1)

                def mix(r):
                    b = 2 * r
                    inverse(b)
                    inverse(b + 1)
                    dve.wait_ge(rl_ok, h * NB + b + 2)
                    nc.vector.tensor_scalar(S[:, (b + 1) % 4], S[:, (b + 1) % 4], rl[:, b + 1:b + 2], K.neglam[:, 0:1],
                                            ALU.mult, ALU.mult).then_inc(part_ok, 1)
                    dve.wait_ge(part_ok, h * NT + r + 1)
                    stt(S[:, b % 4], S[:, b % 4], rl[:, b:b + 1], S[:, (b + 1) % 4], ALU.mult, ALU.add).then_inc(w_ok, 1)

                biased(0)
                biased(1)
                for r in range(NT):
                    j, i = step[r] if dil else (0, r)
                    if dil:
                        dve.wait_ge(turned, h * 2 * NT + 2 * r + 1)
                        if r >= 1:
                            dve.wait_ge(pv_ok, h * 2 * NT + 2 * r - 1)
                        nc.vector.tensor_copy(pt[:, 0].rearrange("p m n -> p (m n)"), ps[:, 2048:2560]).then_inc(pt0, 1)
                    else:
                        mix(r)
                    for b in ([r + 2] if dil else [2 * r + 2, 2 * r + 3]):
                        if b < NB:
                            biased(b)
                    if dil:
                        inverse(r)
                        dve.wait_ge(rl_ok, h * NB + r + 1)
                        dve.wait_ge(pv_ok, h * 2 * NT + 2 * r + 2)
                        nc.vector.tensor_scalar(otok[:, i, 64 * j:64 * j + 64], ps[:, 3072:3136], rl[:, r:r + 1], None,
                                                ALU.mult).then_inc(o_ok, 1)
                    else:
                        dve.wait_ge(pv_ok, h * 2 * NT + 2 * r + 2)
                        nc.vector.tensor_copy(otok[:, i], ps[:, 3072:3072 + P]).then_inc(o_ok, 1)
                if not dil:
                    dve.wait_ge(ss_ok, h * (NT + 1) + NT + 1)
                    nc.vector.reciprocal(ors[:, :], oss[:, :]).then_inc(or_ok, 1)
                    dve.wait_ge(or_ok, h + 1)
                    tt(otok[:, :, :], otok[:, :, :], ors[:, :].unsqueeze(2).to_broadcast([P, NI, P]), ALU.mult).then_inc(on_ok, 1)
                for hf in range(2):
                    c = slice(512 * hf, 512 * (hf + 1))
                    dve.wait_ge(oturn, h * 2 + hf + 1)
                    if dil:
                        tt(yt[:, c], ps[:, c], zT[:, c], ALU.mult).then_inc(y_ok, 1)
                    else:
                        stt(yt[:, c], ps[:, c], K.outgain[:, 0:1], zT[:, c], ALU.mult, ALU.mult).then_inc(y_ok, 1)


def lambda_phase(nc, K):
    LAM0 = 0.8 - 0.6 * math.exp(0.0)
    with ExitStack() as ctx:
        sb = lambda n, sh: ctx.enter_context(nc.sbuf_tensor("lam_" + n, sh, F32))
        v, pr, e, par = sb("v", [P, 4, 64]), sb("pr", [P, 2, 64]), sb("e", [P, 2]), sb("par", [P, 3])
        s = lambda n: semaphore(nc, ctx, "lam_" + n)
        v_in, V, A = s("in"), s("dve"), s("act")
        block = ctx.enter_context(nc.Block())

        @block.sync
        def _(sp):
            sp.dma_start(v[:, :, :].rearrange("p a b -> p (a b)"), K.d["lambdas"].to_broadcast([P, 256])).then_inc(v_in, 16)
            sp.dma_start(par[:, :], K.d["par_diff"]).then_inc(v_in, 16)

        @block.scalar
        def _(act):
            act.wait_ge(V, 2)
            nc.scalar.activation(e[:, :], e[:, :], ACT.Exp).then_inc(A, 1)

        @block.vector
        def _(dve):
            ch = Chain(dve, V)
            dve.wait_ge(v_in, 32)
            vv = v[:, :, :].rearrange("p (a b) n -> p a b n", b=2)
            ch.link(nc.vector.tensor_tensor(pr[:, :, :], vv[:, :, 0], vv[:, :, 1], ALU.mult))
            ch.link(nc.vector.reduce_sum(e[:, :], pr[:, :, :], axis=mybir.AxisListType.X))
            dve.wait_ge(A, 1)
            ch.link(nc.vector.tensor_tensor(K.neglam[:, :], e[:, 1:2], e[:, 0:1], ALU.subtract))
            ch.link(nc.vector.tensor_scalar(K.neglam[:, :], K.neglam[:, :], -LAM0, None, ALU.add))
            ch.link(nc.vector.tensor_scalar(K.outgain[:, :], par[:, 2:3], 1.0 - LAM0, None, ALU.mult))


def add_phase(nc, K, xr, o):
    with ExitStack() as ctx:
        added = semaphore(nc, ctx, "added2")
        block = ctx.enter_context(nc.Block())

        @block.vector
        def _(dve):
            for k in range(KT):
                nc.vector.tensor_tensor(xr[:, k], xr[:, k], o[:, k], ALU.add).then_inc(added, 1)


def final_phase(nc, K, u_hi, u_lo, xr):
    with ExitStack() as ctx:
        sb = lambda n, sh, dt=F32: ctx.enter_context(nc.sbuf_tensor("g_" + n, sh, dt))
        W = Weights(nc, ctx, "gw", 4)
        p_in = sb("p", [P, CH, 2 * P])
        pT, p_hi, p_lo = sb("pT", [P, 2, T]), sb("p_hi", [P, 2, T], F32R), sb("p_lo", [P, 2, T], F32R)
        pw, pw_hi, pw_lo = sb("pw", [P, KT, 2 * P]), sb("pw_hi", [P, KT, 2, P], F32R), sb("pw_lo", [P, KT, 2, P], F32R)
        gate = sb("gate", [P, T])
        ot = sb("out", [P, 2, CH, P])
        s = lambda n: semaphore(nc, ctx, "g_" + n)
        in_p, in_w, pturn, p_ok, p_hi_ok, p_lo_ok, w_hi_ok, w_lo_ok = (s(n) for n in
            ["in_p", "in_w", "pturn", "p_ok", "p_hi", "p_lo", "w_hi", "w_lo"])
        gate_mm, ple_mm, sig_ok, prod_ok, sum_ok, turned, copied = (s(n) for n in
            ["gate_mm", "ple_mm", "sig", "prod", "sum", "turned", "copied"])
        stored = [s("stored0"), s("stored1")]
        block = ctx.enter_context(nc.Block())
        ps = K.psum
        out = K.d["out"][0].rearrange("(c p) (f n) -> f p c n", p=P, n=P)

        def back(act, f):
            for h in range(2):
                act.wait_ge(turned, 2 * f + h + 1)
                if f >= 2:
                    act.wait_ge(stored[f % 2], 16 * (f // 2))
                nc.scalar.activation(ot[:, f % 2, 4 * h:4 * h + 4].rearrange("p c n -> p (c n)"),
                                     ps[:, 2048 + 512 * h:2048 + 512 * (h + 1)], ACT.Copy).then_inc(copied, 1)

        @block.sync
        def _(sp):
            W.credits_raw(sp)
            sp.dma_start(p_in[:, :, :], K.d["p"][0, 0].rearrange("(c p) n -> p c n", p=P)).then_inc(in_p, 16)
            sp.dma_start(pw[:, :, :], K.d["w_ple"].rearrange("f p k -> p f k")).then_inc(in_w, 16)
            for n in range(KT):
                W.load(sp, 0, 8, n, K.d["w_gate"][n])
            for f in range(KT):
                sp.wait_ge(copied, 2 * f + 2)
                sp.dma_start(out[f], ot[:, f % 2]).then_inc(stored[f % 2], 16)
            for r in range(2):
                sp.wait_ge(stored[r], 64)

        @block.gpsimd
        def _(pool):
            W.split(pool, 0, 8, 0)
            W.split(pool, 0, 8, 1)
            pool.wait_ge(in_w, 16)
            w4 = pw[:, :, :].rearrange("p f (k n) -> p f k n", k=2)
            nc.gpsimd.tensor_copy(pw_hi[:, :, :, :], w4).then_inc(w_hi_ok, 1)
            pool.wait_ge(w_hi_ok, 1)
            nc.gpsimd.tensor_tensor(pw_lo[:, :, :, :].rearrange("p f k n -> p (f k n)"), pw[:, :, :].rearrange("p f k -> p (f k)"),
                                    pw_hi[:, :, :, :].rearrange("p f k n -> p (f k n)").bitcast(F32), ALU.subtract).then_inc(w_lo_ok, 1)
            for n in range(2, KT):
                W.split(pool, 0, 8, n)

        @block.tensor
        def _(pe):
            W.credits_used(pe)
            pe.wait_ge(in_p, 16)
            for c in range(CH):
                if c == 4:
                    pe.wait_ge(p_ok, 2)
                for k in range(2):
                    last = nc.tensor.transpose(ps[:, 3072 + 512 * k + P * (c % 4):3072 + 512 * k + P * (c % 4 + 1)],
                                               p_in[:, c, P * k:P * (k + 1)], K.ident[:, :])
                last.then_inc(pturn, 1)

            def turn(f):
                pe.wait_ge(sum_ok, f + 1)
                for h in range(2):
                    if f >= 1:
                        pe.wait_ge(copied, 2 * f + h - 1)
                    for m in range(4):
                        last = nc.tensor.transpose(ps[:, 2048 + 512 * h + P * m:2048 + 512 * h + P * (m + 1)],
                                                   xr[:, f, 512 * h + P * m:512 * h + P * (m + 1)], K.ident[:, :])
                    last.then_inc(turned, 1)

            for f in range(KT):
                W.wait(pe, 0, 8, f)
                for h in range(2):
                    c = slice(512 * h, 512 * (h + 1))
                    if f >= 1:
                        pe.wait_ge(sig_ok, 2 * (f - 1) + h + 1)
                    gemm(nc, ps[:, c], W.hi[:, f % 2], W.lo[:, f % 2], lambda k: u_hi[:, k, c], lambda k: u_lo[:, k, c]).then_inc(gate_mm, 1)
                pe.wait_ge(gate_mm, 2 * f + 2)
                pe.sem_inc(W.used, 1)
                if f == 0:
                    pe.wait_ge(w_lo_ok, 1)
                    pe.wait_ge(p_lo_ok, 1)
                for h in range(2):
                    c = slice(512 * h, 512 * (h + 1))
                    if f >= 1:
                        pe.wait_ge(prod_ok, f)
                    gemm(nc, ps[:, 1024 + 512 * h:1024 + 512 * (h + 1)], pw_hi[:, f], pw_lo[:, f],
                         lambda k: p_hi[:, k, c], lambda k: p_lo[:, k, c], kk=2).then_inc(ple_mm, 1)
                if f >= 1:
                    turn(f - 1)
            turn(KT - 1)

        @block.scalar
        def _(act):
            for g in range(2):
                act.wait_ge(pturn, 4 * g + 4)
                for k in range(2):
                    nc.scalar.activation(pT[:, k, 512 * g:512 * (g + 1)], ps[:, 3072 + 512 * k:3072 + 512 * (k + 1)], ACT.Copy).then_inc(p_ok, 1)
            act.wait_ge(p_ok, 4)
            nc.scalar.activation(p_hi[:, :, :], pT[:, :, :], ACT.Copy).then_inc(p_hi_ok, 1)
            for f in range(KT):
                for h in range(2):
                    act.wait_ge(gate_mm, 2 * f + h + 1)
                    if f >= 1:
                        act.wait_ge(sum_ok, f)
                    nc.scalar.activation(gate[:, 512 * h:512 * (h + 1)], ps[:, 512 * h:512 * (h + 1)], ACT.Sigmoid).then_inc(sig_ok, 1)
                if f >= 1:
                    back(act, f - 1)
            back(act, KT - 1)

        @block.vector
        def _(dve):
            dve.wait_ge(p_hi_ok, 1)
            nc.vector.tensor_tensor(p_lo[:, :, :], pT[:, :, :], p_hi[:, :, :].bitcast(F32), ALU.subtract).then_inc(p_lo_ok, 1)
            for f in range(KT):
                dve.wait_ge(ple_mm, 2 * f + 2)
                dve.wait_ge(sig_ok, 2 * f + 2)
                nc.vector.tensor_tensor(gate[:, :], gate[:, :], ps[:, 1024:2048], ALU.mult).then_inc(prod_ok, 1)
                dve.wait_ge(prod_ok, f + 1)
                nc.vector.tensor_tensor(xr[:, f], xr[:, f], gate[:, :], ALU.add).then_inc(sum_ok, 1)


def program(nc, d, s):
    K = Kernel(d, s)
    with ExitStack() as top:
        sb = lambda n, sh, dt=F32: top.enter_context(nc.sbuf_tensor(n, sh, dt))
        K.psum = top.enter_context(nc.psum_tensor("psum", [P, 4096], F32))
        K.ident, K.tri, K.ones = sb("ident", [P, P]), sb("tri", [P, P]), sb("ones", [P, P])
        K.identb, K.maskb = sb("identb", [P, P], BF16), sb("maskb", [P, P], BF16)
        K.eps = sb("eps", [P, 1])
        K.mask = sb("mask", [P, P])
        K.pairs = sb("pairs", [P, P])
        K.neglam, K.outgain = sb("neglam", [P, 1]), sb("outgain", [P, 1])
        K.gains = sb("gains", [P, 4 * KT])
        with ExitStack() as one:
            sb1 = lambda n, sh, dt=F32: one.enter_context(nc.sbuf_tensor(n, sh, dt))
            u_hi, u_lo = sb1("u_hi", [P, KT, L], F32R), sb1("u_lo", [P, KT, L], F32R)
            sm = sb1("ssd_small", [P, GROUPS, 6, CH + 1, HG])
            with ExitStack() as c0:
                xT = c0.enter_context(nc.sbuf_tensor("xT", [P, KT, L], F32))
                load_phase(nc, K, xT)
                clear_semaphores(nc)
                norm_phase(nc, K, "n0", xT, L, THIRDS, K.gains[:, 0:KT], u_hi, u_lo)
                clear_semaphores(nc)
            small_phase(nc, K, u_hi, u_lo, sm)
            clear_semaphores(nc)
            ssd_phase(nc, K, u_hi, u_lo, sm)
            clear_semaphores(nc)
            ssd_out_phase(nc, K)
            clear_semaphores(nc)
            fox_phase(nc, K, u_hi, u_lo)
            clear_semaphores(nc)
            merge_phase(nc, K, u_hi, u_lo)
            clear_semaphores(nc)
        with ExitStack() as two:
            sb2 = lambda n, sh, dt=F32: two.enter_context(nc.sbuf_tensor(n, sh, dt))
            xr = sb2("x_res", [P, KT, T])
            with ExitStack() as c1:
                o = c1.enter_context(nc.sbuf_tensor("w_out_o", [P, KT, T], F32))
                linear_phase(nc, K, "l1", K.s["merged"], K.d["w_out"], o)
                clear_semaphores(nc)
                residual_phase(nc, K, o, K.gains[:, KT:2 * KT], xr)
                clear_semaphores(nc)
            lambda_phase(nc, K)
            clear_semaphores(nc)
            with ExitStack() as c2:
                h_hi, h_lo = (c2.enter_context(nc.sbuf_tensor("h_" + n, [P, KT, T], F32R)) for n in ("hi", "lo"))
                norm_phase(nc, K, "n2", xr, T, [(0, 512), (512, 1024)], K.gains[:, 2 * KT:3 * KT], h_hi, h_lo)
                clear_semaphores(nc)
                mixer_phase(nc, K, "md", False, h_hi, h_lo)
                clear_semaphores(nc)
                mixer_phase(nc, K, "ml", True, h_hi, h_lo)
                clear_semaphores(nc)
            with ExitStack() as c3:
                o = c3.enter_context(nc.sbuf_tensor("w_out2_o", [P, KT, T], F32))
                linear_phase(nc, K, "l2", K.s["mix"], K.d["w_out_2"], o)
                clear_semaphores(nc)
                add_phase(nc, K, xr, o)
                clear_semaphores(nc)
            with ExitStack() as c4:
                r_hi, r_lo = (c4.enter_context(nc.sbuf_tensor("r_" + n, [P, KT, T], F32R)) for n in ("hi", "lo"))
                norm_phase(nc, K, "n3", xr, T, [(0, 512), (512, 1024)], K.gains[:, 3 * KT:4 * KT], r_hi, r_lo)
                clear_semaphores(nc)
                final_phase(nc, K, r_hi, r_lo, xr)
                clear_semaphores(nc)


def tiles(np, w):
    k, n = w.shape[0] // P, w.shape[1] // P
    return w.reshape(k, P, n, P).transpose(2, 1, 0, 3).reshape(n, P, k * P)


def cols(v):
    return v.reshape(-1, P).transpose(1, 0)


def kernel(**inputs):
    import numpy as np
    import concourse.bacc as bacc
    from concourse import mybir as mb
    from concourse.bass_utils import run_bass_kernel_spmd as run

    I = {k: np.asarray(v) for k, v in inputs.items()}
    g = lambda n: I[n][0]
    A = {}
    A["x"], A["meta"] = I["x"], I["meta_tokens"]
    w = g("w_in")
    o_x, o_dt, o_za = 2048, 5120, 5152
    o_q, o_k, o_v, o_f, o_g = 6176, 7200, 8224, 9248, 9264
    tz, txs = tiles(np, w[:, 0:2048]), tiles(np, w[:, o_x:o_x + 2048])
    tb, tc = tiles(np, w[:, o_x + 2048:o_x + 2560]), tiles(np, w[:, o_x + 2560:o_x + 3072])
    A["w_ssd"] = np.concatenate([np.concatenate([txs[4 * i:4 * i + 4], tb[i:i + 1], tc[i:i + 1], tz[4 * i:4 * i + 4]]) for i in range(GROUPS)])
    A["wdf"] = np.concatenate([w[:, o_dt:o_dt + 32], w[:, o_f:o_f + 16]], axis=1).reshape(KT, P, SM).transpose(1, 0, 2)
    A["dtf_bias"] = np.concatenate([g("dt_bias"), g("fgate_bias")])[None]
    A["a_log"] = g("a_log")[None]
    A["gains"] = np.concatenate([cols(g("norm_pre")), cols(g("norm_post")), cols(g("mix_norm_g_2")), cols(g("ple_norm_g_2"))], axis=1)
    cw = np.concatenate([g("conv_w"), g("conv_b")[None]])
    cw = cw.reshape(5, 24, P).transpose(2, 1, 0)
    dsk = cols(np.broadcast_to(g("d_skip")[:, None], (SSD_H, 64)).reshape(-1))
    gn = cols(g("ssd_norm"))
    A["conv_par"] = np.stack([np.concatenate([cw[:, 4 * i:4 * i + 4].reshape(P, 20), cw[:, 16 + i], cw[:, 20 + i],
                                              dsk[:, 4 * i:4 * i + 4], gn[:, 4 * i:4 * i + 4]], axis=1) for i in range(GROUPS)], axis=1)
    A["mask"] = np.triu(np.ones((P, P), np.float32), 1)
    A["w_proj_ssd"] = tiles(np, g("w_proj_ssd")).reshape(KT, P, 2, KT * P).transpose(0, 2, 1, 3).reshape(16, P, KT * P)
    tq, tk, tv, tza = (tiles(np, w[:, o:o + 1024]) for o in (o_q, o_k, o_v, o_za))
    A["w_fox"] = np.stack([tq, tk, tv, tza], axis=1).reshape(32, P, KT * P)
    tgs, tga, twa = tiles(np, w[:, o_g:o_g + 1024]), tiles(np, w[:, o_g + 1024:o_g + 2048]), tiles(np, g("w_proj_att"))
    A["w_merge"] = np.stack([tgs, tga, twa], axis=1).reshape(24, P, KT * P)
    A["w_out"] = tiles(np, g("w_out"))
    A["gate_bias"] = cols(g("gate_bias"))
    A["pairs"] = np.kron(np.eye(2, dtype=np.float32), np.ones((64, 64), np.float32))
    w2 = tiles(np, g("w_in_2"))
    A["w_diff"] = np.stack([w2[0:4], w2[4:8], w2[8:12], w2[24:28]], axis=1).reshape(16, P, KT * P)
    A["w_dil"] = np.stack([w2[12:16], w2[16:20], w2[20:24], w2[28:32]], axis=1).reshape(16, P, KT * P)
    A["w_out_2"], A["w_gate"], A["w_ple"] = (tiles(np, g(n)) for n in ("w_out_2", "w_ple_gate_2", "w_ple_proj_2"))
    A["p"] = I["p_2"]
    A["lambdas"] = np.concatenate([g("lambda_q1_2"), g("lambda_k1_2"), g("lambda_q2_2"), g("lambda_k2_2")])[None]
    twice = lambda v: np.concatenate([v, v])
    A["par_diff"] = np.stack([twice(g("diff_q_norm_g_2")), twice(g("diff_k_norm_g_2")), g("diff_sub_norm_g_2")], axis=1)
    A["par_dil"] = np.stack([twice(g("dil_q_norm_g_2")), twice(g("dil_k_norm_g_2")), twice(g("dil_k_norm_g_2"))], axis=1)
    dist = np.abs(np.arange(P)[:, None] + (T - P) - np.arange(2 * T - P)[None, :])
    A["dist"] = dist.astype(np.float32)
    held = (dist <= 64) * 1 + ((dist <= 256) & (dist % 4 == 0)) + (dist % 16 == 0)
    A["count"] = np.where(held > 0, 8.0 * np.log(np.maximum(held, 1)), NEG).astype(np.float32)
    A["slopes_diff"] = np.broadcast_to(np.array([-8.0 * 2.0 ** (-2.0 * (i % 4 + 1)) for i in range(8)], np.float32), (P, 8))
    A["slopes_dil"] = np.broadcast_to(np.array([-8.0 * 2.0 ** (-(i + 1.0)) for i in range(8)], np.float32), (P, 8))
    A["ident"] = np.eye(P, dtype=np.float32)
    A["tri"] = np.triu(np.ones((P, P), np.float32))
    nc = bacc.Bacc("TRN2", target_bir_lowering=False, num_devices=1)
    arrays, ins = {}, {}
    for n, a in A.items():
        a = np.ascontiguousarray(a)
        arrays["in_" + n] = a
        ins[n] = (nc.dram_tensor("in_" + n, a.shape, mb.dt.from_np(a.dtype), kind="ExternalInput").ap())
    ins["out"] = nc.dram_tensor("out_0", (1, T, D), F32, kind="ExternalOutput").ap()
    s = {}
    s["xT"] = nc.dram_tensor("s_xT", (KT, P, T), F32, kind="Internal").ap()
    s["y"] = nc.dram_tensor("s_y", (16, P, T), F32, kind="Internal").ap()
    for n in ("pssd", "yatt", "merged", "mix"):
        s[n] = nc.dram_tensor("s_" + n, (KT, P, T), F32, kind="Internal").ap()
    s["nc"] = nc.dram_tensor("s_nc", (ATT_H, L), F32, kind="Internal").ap()
    program(nc, ins, s)
    r = run(nc, [arrays], core_ids=[0])
    return r.results[0]["out_0"]
```

```python
import concourse.bass as bass
from concourse import mybir
from contextlib import ExitStack
import math

F32 = mybir.dt.float32
F32R = mybir.dt.float32r
BF16 = mybir.dt.bfloat16
ALU = mybir.AluOpType
ACT = mybir.ActivationFunctionType
P = 128
D = 1024
T = 1024
META = 16
L = META + T
KT = D // P
CH = T // P
GROUPS, HG = 4, 8
SSD_H, ATT_H = 32, 16
SM = 48
EPS = 1e-6
NEG = -1e30
THIRDS = [(0, 348), (348, 696), (696, 1040)]
HALVES = [(META, META + 512), (META + 512, L)]


def chunk_cols(c):
    return (0, META) if c == 0 else (META + P * (c - 1), META + P * c)


USED = []
NUMBERS = 85


def semaphore(nc, ctx, name):
    USED.append(ctx.enter_context(nc.semaphore(name)))
    return USED[-1]


def clear_semaphores(nc):
    if len(USED) < NUMBERS:
        return
    with nc.Block() as block:
        @block.gpsimd
        def _(pool):
            for s in USED:
                pool.sem_clear(s)
    USED.clear()


class Chain:

    def __init__(self, eng, sem, per=0, i=0):
        self.eng, self.sem, self.per, self.i, self.n = eng, sem, per, i, 0

    def step(self, ins):
        ins.then_inc(self.sem, 1)
        self.n += 1
        return self.n

    def after(self, n):
        self.eng.wait_ge(self.sem, self.i * self.per + n)

    def link(self, ins):
        self.after(self.step(ins))


def gemm_k(nc, out, w_hi, w_lo, a_hi, a_lo, k, kk=KT, first=True, final=True):
    nc.tensor.matmul(out, w_hi[:, k], a_hi, start=(k == 0 and first), stop=False)
    nc.tensor.matmul(out, w_hi[:, k], a_lo, start=False, stop=False)
    return nc.tensor.matmul(out, w_lo[:, k], a_hi, start=False, stop=(k == kk - 1 and final))


def gemm(nc, out, w_hi, w_lo, a_hi, a_lo, kk=KT):
    for k in range(kk):
        last = gemm_k(nc, out, w_hi, w_lo, a_hi(k), a_lo(k), k, kk)
    return last


class Kernel:

    def __init__(self, d, s):
        self.d, self.s = d, s


class Weights:

    def __init__(self, nc, ctx, src):
        self.nc, self.src, self.base = nc, src, -2
        self.raw = ctx.enter_context(nc.sbuf_tensor("w_raw", [P, 2, KT, P], F32))
        self.hi = ctx.enter_context(nc.sbuf_tensor("w_hi", [P, 2, KT, P], F32R))
        self.lo = ctx.enter_context(nc.sbuf_tensor("w_lo", [P, 2, KT, P], F32R))
        s = lambda n: ctx.enter_context(nc.semaphore("w_" + n))
        self.loaded = [s("loaded0"), s("loaded1")]
        self.raw_free = s("raw_free")
        self.hi_done = s("hi_done")
        self.turns = s("turns")
        self.ready = s("split")
        self.used = s("used")

    def credits(self, eng):
        eng.sem_inc(self.raw_free, 2)
        eng.sem_inc(self.used, 2)

    def load(self, eng, i, per, n):
        m = i * per + (self.base + n + 2)
        eng.wait_ge(self.raw_free, m + 1)
        src = self.src[bass.ds(m, 1)].rearrange("a p k -> (a p) k")
        eng.dma_start(self.raw[:, n % 2].rearrange("p k n -> p (k n)"), src).then_inc(self.loaded[n % 2], 16)

    def split(self, eng, i, per, n):
        m = i * per + (self.base + n + 2)
        r = n % 2
        eng.wait_ge(self.loaded[r], i * (8 * per) + 8 * (self.base + n - r + 2) + 16)
        eng.wait_ge(self.used, m + 1)
        eng.sem_inc(self.turns, 1)
        self.nc.gpsimd.tensor_scalar(self.hi[:, r], self.raw[:, r], 1.0, 1.0, ALU.mult, ALU.mult).then_inc(self.hi_done, 1)
        eng.wait_ge(self.hi_done, m + 1)
        self.nc.gpsimd.tensor_tensor(self.lo[:, r], self.raw[:, r], self.hi[:, r].bitcast(F32),
                                     ALU.subtract).then_inc(self.ready, 1)
        eng.wait_ge(self.ready, m + 1)
        eng.sem_inc(self.raw_free, 1)

    def wait(self, eng, i, per, n):
        eng.wait_ge(self.ready, i * per + (self.base + n + 1))


def norm_phase(nc, K, name, xT, cols, pieces, gain, u_hi, u_lo):
    C = cols
    with ExitStack() as ctx:
        sq = ctx.enter_context(nc.sbuf_tensor(name + "_sq", [P, 2, C], F32))
        rs = ctx.enter_context(nc.sbuf_tensor(name + "_rs", [P, C], F32))
        rt = ctx.enter_context(nc.sbuf_tensor(name + "_rt", [P, C], F32))
        un = ctx.enter_context(nc.sbuf_tensor(name + "_un", [P, 2, C], F32))
        s = lambda n: semaphore(nc, ctx, name + n)
        squared, summed, rooted, inverted = s("_squared"), s("_summed"), s("_rooted"), s("_inverted")
        scaled, hi_ok, lo_pool, lo_dve = s("_scaled"), s("_hi"), s("_lo_pool"), s("_lo_dve")
        block = ctx.enter_context(nc.Block())
        ps = K.psum

        def low(eng, ops, done, k):
            eng.wait_ge(hi_ok, k + 1)
            ops.tensor_tensor(u_lo[:, k], un[:, k % 2], u_hi[:, k].bitcast(F32), ALU.subtract).then_inc(done, 1)

        @block.scalar
        def _(act):
            for k in range(KT):
                if k >= 2:
                    act.wait_ge(summed, k - 1)
                nc.scalar.activation(sq[:, k % 2], xT[:, k], ACT.Square).then_inc(squared, 1)
            act.wait_ge(summed, KT)
            for j, (a, b) in enumerate(pieces):
                nc.scalar.activation(rt[:, a:b], ps[:, 512 * j:512 * j + b - a], ACT.Sqrt, scale=1.0 / D,
                                     bias=K.eps[:, 0:1]).then_inc(rooted, 1)
            for k in range(KT):
                act.wait_ge(scaled, k + 1)
                nc.scalar.activation(u_hi[:, k], un[:, k % 2], ACT.Copy).then_inc(hi_ok, 1)

        @block.tensor
        def _(pe):
            for k in range(KT):
                pe.wait_ge(squared, k + 1)
                for j, (a, b) in enumerate(pieces):
                    last = nc.tensor.matmul(ps[:, 512 * j:512 * j + b - a], K.ones[:, :], sq[:, k % 2, a:b],
                                            start=(k == 0), stop=(k == KT - 1))
                last.then_inc(summed, 1)

        @block.vector
        def _(dve):
            dve.wait_ge(rooted, len(pieces))
            nc.vector.reciprocal(rs[:, :], rt[:, :]).then_inc(inverted, 1)
            dve.wait_ge(inverted, 1)
            for k in range(KT):
                if k >= 2:
                    dve.wait_ge(lo_pool if k % 2 == 0 else lo_dve, k // 2)
                nc.vector.scalar_tensor_tensor(un[:, k % 2], xT[:, k], gain[:, k:k + 1], rs[:, :],
                                               ALU.mult, ALU.mult).then_inc(scaled, 1)
                if k >= 2 and k % 2 == 0:
                    low(dve, nc.vector, lo_dve, k - 1)
            low(dve, nc.vector, lo_dve, KT - 1)

        @block.gpsimd
        def _(pool):
            for k in range(0, KT, 2):
                low(pool, nc.gpsimd, lo_pool, k)


def load_phase(nc, K, xT):
    with ExitStack() as ctx:
        xt = ctx.enter_context(nc.sbuf_tensor("x_tok", [P, CH + 1, D], F32))
        s = lambda n: semaphore(nc, ctx, n)
        const_in, out_xT = s("const_in"), s("xT_stored")
        x_in = [s(f"x_in{c}") for c in range(CH + 1)]
        turned, copied = s("x_turned"), s("x_copied")
        ms = s("eps_set")
        block = ctx.enter_context(nc.Block())
        ps = K.psum
        consts = [(K.ident, K.d["ident"]), (K.tri, K.d["tri"]), (K.gains, K.d["gains"]), (K.mask, K.d["mask"]), (K.pairs, K.d["pairs"])]

        @block.sync
        def _(sp):
            for dst, src in consts:
                sp.dma_start(dst[:, :], src).then_inc(const_in, 16)
            for c in range(CH + 1):
                n = META if c == 0 else P
                src = K.d["meta"] if c == 0 else K.d["x"][0, P * (c - 1):P * c, :]
                sp.dma_start(xt[0:n, c, :], src).then_inc(x_in[c], 16)
            for k in range(KT):
                sp.wait_ge(copied, 2 * (CH + 1))
                sp.dma_start(K.s["xT"][k], xT[:, k, META:L]).then_inc(out_xT, 16)
            sp.wait_ge(out_xT, 16 * KT)

        @block.vector
        def _(dve):
            dve.wait_ge(const_in, 16 * len(consts))
            nc.vector.tensor_copy(K.identb[:, :], K.ident[:, :])
            nc.vector.tensor_scalar(K.maskb[:, :], K.mask[:, :], NEG, None, ALU.mult)
            nc.vector.memset(K.eps[:, :], EPS)
            nc.vector.memset(K.ones[:, :], 1.0).then_inc(ms, 1)
            dve.wait_ge(ms, 1)

        @block.tensor
        def _(pe):
            pe.wait_ge(const_in, 16 * len(consts))
            for c in range(CH + 1):
                n = META if c == 0 else P
                pe.wait_ge(x_in[c], 16)
                for h in range(2):
                    u = 2 * c + h
                    if u >= 4:
                        pe.wait_ge(copied, u - 3)
                    for f in range(4):
                        last = nc.tensor.transpose(ps[:, 512 * (u % 4) + P * f:512 * (u % 4) + P * f + n],
                                                   xt[0:n, c, P * (4 * h + f):P * (4 * h + f + 1)], K.ident[0:n, 0:n])
                    last.then_inc(turned, 1)

        @block.scalar
        def _(act):
            for c in range(CH + 1):
                a, b = chunk_cols(c)
                for h in range(2):
                    u = 2 * c + h
                    act.wait_ge(turned, u + 1)
                    bank = ps[:, 512 * (u % 4):512 * (u % 4) + 512].rearrange("p (f n) -> p f n", f=4)
                    nc.scalar.activation(xT[:, 4 * h:4 * h + 4, a:b], bank[:, :, 0:b - a], ACT.Copy).then_inc(copied, 1)


def small_phase(nc, K, u_hi, u_lo, sm):
    NCH = CH + 1
    with ExitStack() as ctx:
        sb = lambda n, sh, dt=F32: ctx.enter_context(nc.sbuf_tensor(n, sh, dt))
        wraw, whi, wlo = sb("wdf_raw", [P, KT, SM]), sb("wdf_hi", [P, KT, SM], F32R), sb("wdf_lo", [P, KT, SM], F32R)
        brow = sb("dtf_bias", [P, SM])
        arow = sb("a_row", [P, SSD_H])
        aneg = sb("a_neg", [P, SSD_H])
        sgn = sb("dtf_sign", [P, SM])
        names = ["raw", "v", "e", "w", "l", "q", "t", "z", "sp"]
        B = {n: sb("dtf_" + n, [P, NCH, SM]) for n in names}
        adt = sb("adt", [P, NCH, SSD_H])
        acs = sb("acs", [P, NCH, SSD_H])
        alast = sb("alast", [P, NCH, SSD_H])
        fT = sb("fT", [ATT_H, L])
        ncT = sb("ncT", [ATT_H, L])
        onesL = sb("onesL", [ATT_H, L])
        s = lambda n: semaphore(nc, ctx, n)
        w_in, w_split, proj, V, A, G, X, pemm, st = (s("dtf_" + n) for n in
            ["loaded", "wsplit", "projected", "dve", "act", "pool", "x", "pe", "stored"])
        block = ctx.enter_context(nc.Block())
        ps = K.psum

        @block.sync
        def _(sp):
            K.W.credits(sp)
            sp.dma_start(wraw[:, :, :], K.d["wdf"]).then_inc(w_in, 16)
            sp.dma_start(brow[:, :], K.d["dtf_bias"].to_broadcast([P, SM])).then_inc(w_in, 16)
            sp.dma_start(arow[:, :], K.d["a_log"].to_broadcast([P, SSD_H])).then_inc(w_in, 16)
            for n in range(2):
                K.W.load(sp, 0, 0, n)
            sp.wait_ge(X, 1)
            sp.dma_start(K.s["nc"], ncT[:, :]).then_inc(st, 16)
            sp.wait_ge(st, 16)

        @block.gpsimd
        def _(pool):
            pool.wait_ge(w_in, 48)
            nc.gpsimd.tensor_copy(whi[:, :, :], wraw[:, :, :]).then_inc(G, 1)
            pool.wait_ge(G, 1)
            nc.gpsimd.tensor_tensor(wlo[:, :, :], wraw[:, :, :], whi[:, :, :].bitcast(F32), ALU.subtract).then_inc(w_split, 1)
            for n in range(2):
                K.W.split(pool, 0, 0, n)

        @block.tensor
        def _(pe):
            pe.wait_ge(w_split, 1)
            for c in range(NCH):
                a, b = chunk_cols(c)
                out = ps[0:b - a, SM * c:SM * (c + 1)]
                for k in range(KT):
                    nc.tensor.matmul(out, u_hi[:, k, a:b], whi[:, k], start=(k == 0), stop=False)
                    nc.tensor.matmul(out, u_hi[:, k, a:b], wlo[:, k], start=False, stop=False)
                    last = nc.tensor.matmul(out, u_lo[:, k, a:b], whi[:, k], start=False, stop=(k == KT - 1))
            last.then_inc(pemm, 1)
            pe.wait_ge(proj, 1)
            nc.tensor.matmul(ps[:, 512:768], K.tri[:, :], adt[:, 1:, :], start=True, stop=True)
            nc.tensor.matmul(ps[0:META, 768:800], K.tri[0:META, 0:META], adt[0:META, 0, :], start=True, stop=True)
            nc.tensor.matmul(ps[:, 1024:1280], K.ones[:, :], adt[:, 1:, :], start=True, stop=True)
            nc.tensor.matmul(ps[:, 1280:1312], K.ones[0:META, :], adt[0:META, 0, :], start=True, stop=True)
            for c in range(NCH):
                a, b = chunk_cols(c)
                last = nc.tensor.transpose(ps[0:ATT_H, 1536 + 512 * (c // 3) + P * (c % 3):1536 + 512 * (c // 3) + P * (c % 3) + b - a],
                                           B["sp"][0:b - a, c, SSD_H:SM], K.ident[0:b - a, 0:b - a])
            last.then_inc(pemm, 1)

        @block.scalar
        def _(act):
            act.wait_ge(w_in, 48)
            nc.scalar.activation(aneg[:, :], arow[:, :], ACT.Exp).then_inc(A, 1)
            act.wait_ge(V, 5)
            nc.scalar.activation(B["e"][:, :, :], B["e"][:, :, :], ACT.Exp, scale=-1.0).then_inc(A, 1)
            act.wait_ge(V, 6)
            nc.scalar.activation(B["l"][:, :, :], B["w"][:, :, :], ACT.Ln).then_inc(A, 1)
            act.wait_ge(V, 21)
            for g in range(GROUPS):
                nc.scalar.activation(sm[:, g, 3], sm[:, g, 3], ACT.Exp).then_inc(A, 1)
                nc.scalar.activation(sm[:, g, 4], alast[:, :, HG * g:HG * (g + 1)], ACT.Exp).then_inc(A, 1)
                nc.scalar.activation(sm[:, g, 5], acs[:, :, HG * g:HG * (g + 1)], ACT.Exp).then_inc(A, 1)

        @block.vector
        def _(dve):
            ch = Chain(dve, V)
            raw, v, e, w, l, q, t, z, sp = (B[n][:, :, :] for n in names)
            nc.vector.memset(sgn[:, 0:SSD_H], 1.0)
            nc.vector.memset(sgn[:, SSD_H:SM], -1.0)
            nc.vector.memset(onesL[:, :], 1.0)
            nc.vector.memset(acs[:, :, :], 0.0)
            ch.link(nc.vector.memset(raw, 0.0))
            dve.wait_ge(pemm, 1)
            nc.vector.tensor_copy(B["raw"][0:META, 0, :], ps[0:META, 0:SM])
            ch.link(nc.vector.tensor_copy(B["raw"][:, 1:, :], ps[:, SM:SM * NCH].rearrange("p (c n) -> p c n", n=SM)))
            dve.wait_ge(w_in, 48)
            bb = brow[:, :].unsqueeze(1).to_broadcast([P, NCH, SM])
            sg = sgn[:, :].unsqueeze(1).to_broadcast([P, NCH, SM])
            tt, ts = nc.vector.tensor_tensor, nc.vector.tensor_scalar
            ch.link(tt(v, raw, bb, ALU.add))
            ch.link(tt(v, v, sg, ALU.mult))
            ch.link(nc.vector.scalar_tensor_tensor(e, v, -1.0, v, ALU.mult, ALU.max))
            dve.wait_ge(A, 2)
            ch.link(ts(w, e, 1.0, None, ALU.add))
            ch.link(ts(t, w, -1.0, 1e-30, ALU.add, ALU.max))
            ch.link(nc.vector.reciprocal(q, t))
            ch.link(tt(q, q, e, ALU.mult))
            ch.link(ts(t, w, 1.0, None, ALU.is_equal))
            ch.link(tt(t, t, e, ALU.mult))
            dve.wait_ge(A, 3)
            ch.link(tt(q, q, l, ALU.mult))
            ch.link(tt(t, t, q, ALU.add))
            ch.link(nc.vector.scalar_tensor_tensor(sp, v, 0.0, t, ALU.max, ALU.add))
            dve.wait_ge(A, 1)
            ch.link(ts(aneg[:, :], aneg[:, :], -1.0, None, ALU.mult))
            tt(adt[:, :, :], B["sp"][:, :, 0:SSD_H], aneg[:, :].unsqueeze(1).to_broadcast([P, NCH, SSD_H]), ALU.mult).then_inc(proj, 1)
            dve.wait_ge(pemm, 2)
            nc.vector.tensor_copy(acs[:, 1:, :], ps[:, 512:768].rearrange("p (c h) -> p c h", h=SSD_H))
            nc.vector.tensor_copy(acs[0:META, 0, :], ps[0:META, 768:800])
            nc.vector.tensor_copy(alast[:, 1:, :], ps[:, 1024:1280].rearrange("p (c h) -> p c h", h=SSD_H))
            nc.vector.tensor_copy(alast[:, 0, :], ps[:, 1280:1312])
            for c in range(NCH):
                a, b = chunk_cols(c)
                o = 1536 + 512 * (c // 3) + P * (c % 3)
                m = nc.vector.tensor_scalar(fT[:, a:b], ps[0:ATT_H, o:o + b - a], 8.0, None, ALU.mult)
            ch.link(m)
            nc.vector.tensor_tensor_scan(ncT[:, :], onesL[:, :], fT[:, :], 0.0, ALU.mult, ALU.add).then_inc(X, 1)
            for g in range(GROUPS):
                h = slice(HG * g, HG * (g + 1))
                nc.vector.tensor_copy(sm[:, g, 0], adt[:, :, h])
                nc.vector.tensor_copy(sm[:, g, 1], acs[:, :, h])
                nc.vector.tensor_copy(sm[:, g, 2], B["sp"][:, :, h])
                ch.link(tt(sm[:, g, 3], alast[:, :, h], acs[:, :, h], ALU.subtract))
            ch.link(nc.vector.memset(onesL[:, 0:1], 1.0))


def ssd_phase(nc, K, u_hi, u_lo, sm):
    NCH, NP = CH + 1, 6 * 3
    with ExitStack() as ctx:
        sb = lambda n, sh, dt=F32: ctx.enter_context(nc.sbuf_tensor(n, sh, dt))
        W = K.W
        raw = sb("conv_in", [P, 2, 3 + L])
        feats = sb("conv_out", [P, 6, L])
        z = sb("z_gate", [P, 4, T])
        seg = sb("decay", [P, 2, HG, P])
        xdt, xst = sb("x_dt", [P, 2, 512]), sb("x_dt_decay", [P, 2, 512])
        ytok, yoff = sb("y_tok", [P, 2, 512]), sb("y_off", [P, 512])
        state = sb("state", [P, 512])
        btok, cb = sb("b_tok", [P, 2, P]), sb("cb", [P, 2, P])
        rms = sb("ssd_rms", [P, T])
        smg = sb("small_g", [P, 6, NCH, HG])
        cpg = sb("conv_par_g", [P, 38])
        par = sb("conv_par", [P, GROUPS, 38])
        s = lambda n: semaphore(nc, ctx, "s1_" + n)
        par_in, small_ok = s("par_in"), s("small_ok")
        proj_ok, raw_ok, conv_ok, silu_ok = s("proj"), s("raw"), s("conv"), s("silu")
        xturn, bturn, sums_ok = s("xturn"), s("bturn"), s("sums")
        zproj, zcopy, zsilu = s("zproj"), s("zcopy"), s("zsilu")
        ydiag_ok, yoff_ok, st_ok, yturn = s("ydiag"), s("yoff"), s("states"), s("yturn")
        xdt_ok, cb_ok, seg_ok, m_ok = s("xdt"), s("cb"), s("seg"), s("m")
        h_ok, t_ok, y_ok, y1_ok = s("h"), s("t"), s("y"), s("y1")
        b_ok, exp_ok, xst_ok = s("btok"), s("exp"), s("xst")
        u_ok, sq_ok, norm_sum, rooted, yf_ok, stored = s("u"), s("sq"), s("normsum"), s("rooted"), s("yf"), s("stored")
        dchain = s("dve_chain")
        block = ctx.enter_context(nc.Block())
        ps = K.psum
        bank = lambda n, w=512: ps[:, 512 * n:512 * n + w]
        y_dst = K.s["y"].rearrange("(g f) p t -> g f p t", g=GROUPS)

        @block.sync
        def _(sp):
            sp.dma_start(par[:, :, :], K.d["conv_par"]).then_inc(par_in, 16)
            sp.sem_inc(stored, 16)
            with sp.Fori(0, GROUPS) as g:
                for n in range(10):
                    W.load(sp, g, 10, n)
            sp.wait_ge(stored, 64 * GROUPS + 16)

        @block.gpsimd
        def _(pool):
            with pool.Fori(0, GROUPS) as g:
                for n in range(6):
                    W.split(pool, g, 10, n)
                for c in range(8):
                    Lc = META if c == 0 else P
                    pool.wait_ge(xdt_ok, g * 9 + c + 1)
                    if c >= 2:
                        pool.wait_ge(st_ok, g * 8 + c - 1)
                    nc.gpsimd.tensor_tensor(xst[0:Lc, c % 2].rearrange("p (h d) -> p h d", h=HG),
                                            xdt[0:Lc, c % 2].rearrange("p (h d) -> p h d", h=HG),
                                            smg[0:Lc, 3, c].unsqueeze(2).to_broadcast([Lc, HG, 64]), ALU.mult).then_inc(xst_ok, 1)
                    if c % 2 == 1:
                        W.split(pool, g, 10, 6 + c // 2)

        @block.tensor
        def _(pe):
            with pe.Fori(0, GROUPS) as g:
                pe.wait_ge(rooted, g * 2 + 2)
                for t in range(6):
                    W.wait(pe, g, 10, t)
                    for j, (a, b) in enumerate(THIRDS):
                        if t >= 2:
                            pe.wait_ge(raw_ok, g * NP + 3 * (t - 2) + j + 1)
                        gemm(nc, bank(3 * (t % 2) + j, b - a), W.hi[:, t % 2], W.lo[:, t % 2],
                             lambda k: u_hi[:, k, a:b], lambda k: u_lo[:, k, a:b]).then_inc(proj_ok, 1)

                def front(c):
                    a, b = chunk_cols(c)
                    n = b - a
                    if c >= 1:
                        pe.wait_ge(xdt_ok, g * 9 + c)
                    for f in range(4):
                        last = nc.tensor.transpose(ps[0:n, 1024 + P * f:1024 + P * f + P], feats[:, f, a:b], K.ident[:, :])
                    last.then_inc(xturn, 1)
                    if c >= 1:
                        pe.wait_ge(b_ok, g * 8 + c)
                    if c >= 2:
                        pe.wait_ge(cb_ok, g * 8 + c - 1)
                    if c <= 7:
                        last = nc.tensor.transpose(ps[0:n, 1536:1536 + P], feats[:, 4, a:b], K.ident[:, :])
                    if c >= 1:
                        last = nc.tensor.matmul(ps[:, 1664:1664 + P], feats[:, 4, a:b], feats[:, 5, a:b], start=True, stop=True)
                    last.then_inc(bturn, 1)
                    if c >= 1:
                        if c >= 2:
                            pe.wait_ge(seg_ok, g * 8 + c - 1)
                        for r in range(HG):
                            last = nc.tensor.matmul(ps[:, 2048 + P * r:2048 + P * (r + 1)],
                                                    smg[:, 0, c, r:r + 1].to_broadcast([P, P]), K.tri[:, :], start=True, stop=True)
                        last.then_inc(sums_ok, 1)

                def zunit(u):
                    t, h = 6 + u // 2, u % 2
                    if h == 0:
                        W.wait(pe, g, 10, t)
                    if u >= 1:
                        pe.wait_ge(zcopy, g * 8 + u)
                    else:
                        pe.wait_ge(raw_ok, g * NP + 13)
                    a, b = HALVES[h]
                    gemm(nc, bank(0), W.hi[:, t % 2], W.lo[:, t % 2],
                         lambda k: u_hi[:, k, a:b], lambda k: u_lo[:, k, a:b]).then_inc(zproj, 1)

                def turn_back(c):
                    pe.wait_ge(y_ok, g * 8 + c)
                    if c >= 2:
                        pe.wait_ge(y1_ok, g * 8 + c - 1)
                    for f in range(4):
                        last = nc.tensor.transpose(ps[:, 512 + P * f:512 + P * (f + 1)], ytok[:, c % 2, P * f:P * (f + 1)], K.ident[:, :])
                    last.then_inc(yturn, 1)

                zunit(0)
                pe.wait_ge(silu_ok, g * 6 + 6)
                pe.wait_ge(small_ok, g + 1)
                front(0)
                for c in range(NCH):
                    a, b = chunk_cols(c)
                    n = b - a
                    if c < 8:
                        front(c + 1)
                        if c + 1 < 8:
                            zunit(c + 1)
                    if c >= 1:
                        pe.wait_ge(m_ok, g * 8 + c)
                        if c >= 2:
                            pe.wait_ge(y_ok, g * 8 + c - 1)
                        for r in range(HG):
                            last = nc.tensor.matmul(ps[:, 3072 + 64 * r:3072 + 64 * (r + 1)], seg[:, c % 2, r],
                                                    xdt[:, c % 2, 64 * r:64 * (r + 1)], start=True, stop=True)
                        last.then_inc(ydiag_ok, 1)
                        pe.wait_ge(h_ok, g * 8 + c)
                        nc.tensor.matmul(bank(7), feats[:, 5, a:b], state[:, :], start=True, stop=True).then_inc(yoff_ok, 1)
                    if c >= 2:
                        turn_back(c - 1)
                    if c <= 7:
                        pe.wait_ge(xst_ok, g * 8 + c + 1)
                        pe.wait_ge(b_ok, g * 8 + c + 1)
                        if c >= 1:
                            pe.wait_ge(t_ok, g * 8 + c)
                        nc.tensor.matmul(bank(7), btok[0:n, c % 2], xst[0:n, c % 2], start=True, stop=True).then_inc(st_ok, 1)
                turn_back(8)
                for f in range(4):
                    pe.wait_ge(sq_ok, g * 4 + f + 1)
                    for h in range(2):
                        last = nc.tensor.matmul(bank(2 + h), K.ones[:, :], raw[:, f % 2, 3 + 512 * h:3 + 512 * (h + 1)],
                                                start=(f == 0), stop=(f == 3))
                    last.then_inc(norm_sum, 1)

        @block.scalar
        def _(act):
            act.sem_inc(rooted, 2)
            with act.Fori(0, GROUPS) as g:
                for t in range(6):
                    act.wait_ge(conv_ok, g * 6 + t + 1)
                    for j, (a, b) in enumerate(THIRDS):
                        act.wait_ge(proj_ok, g * NP + 3 * t + j + 1)
                        if j == 2:
                            act.sem_inc(W.used, 1)
                        nc.scalar.activation(raw[:, t % 2, 3 + a:3 + b], bank(3 * (t % 2) + j, b - a), ACT.Copy).then_inc(raw_ok, 1)
                    if t >= 1:
                        act.wait_ge(conv_ok, g * 6 + t + 2)
                        nc.scalar.activation(feats[:, t - 1], feats[:, t - 1], ACT.Silu).then_inc(silu_ok, 1)
                act.wait_ge(conv_ok, g * 6 + 8)
                nc.scalar.activation(feats[:, 5], feats[:, 5], ACT.Silu).then_inc(silu_ok, 1)
                for c in range(-1, 8):
                    if c >= 0:
                        act.wait_ge(seg_ok, g * 8 + c + 1)
                        nc.scalar.activation(seg[:, (c + 1) % 2], seg[:, (c + 1) % 2], ACT.Exp).then_inc(exp_ok, 1)
                    u = c + 1
                    if u < 8:
                        act.wait_ge(zproj, g * 8 + u + 1)
                        if u % 2 == 1:
                            act.sem_inc(W.used, 1)
                        nc.scalar.activation(z[:, u // 2, 512 * (u % 2):512 * (u % 2 + 1)], bank(0), ACT.Copy).then_inc(zcopy, 1)
                act.wait_ge(zcopy, g * 8 + 8)
                for f in range(4):
                    nc.scalar.activation(z[:, f], z[:, f], ACT.Silu).then_inc(zsilu, 1)
                for f in range(4):
                    act.wait_ge(u_ok, g * 4 + f + 1)
                    if f >= 2:
                        act.wait_ge(norm_sum, g * 4 + f - 1)
                    nc.scalar.activation(raw[:, f % 2, 3:3 + T], feats[:, f, META:L], ACT.Square).then_inc(sq_ok, 1)
                act.wait_ge(norm_sum, g * 4 + 4)
                for h in range(2):
                    nc.scalar.activation(rms[:, 512 * h:512 * (h + 1)], bank(2 + h), ACT.Sqrt, scale=1.0 / 512,
                                         bias=K.eps[:, 0:1]).then_inc(rooted, 1)
                for f in range(4):
                    act.wait_ge(yf_ok, g * 4 + f + 1)
                    act.dma_start(y_dst[g, f], feats[:, f, META:L]).then_inc(stored, 16)

        @block.vector
        def _(dve):
            dve.sem_inc(conv_ok, 2)
            nc.vector.memset(raw[:, :, 0:3], 0.0).then_inc(par_in, 16)
            dve.wait_ge(par_in, 32)
            with dve.Fori(0, GROUPS) as g:
                ch = Chain(dve, dchain, 1 + 6 * 3 + 7 + 1, g)
                tt, stt = nc.vector.tensor_tensor, nc.vector.scalar_tensor_tensor
                nc.vector.tensor_copy(smg[:, :, :, :], sm[:, g])
                ch.link(nc.vector.tensor_copy(cpg[:, :], par[:, g]))
                dve.sem_inc(small_ok, 1)
                dve.wait_ge(stored, g * 64 + 16)
                for t in range(6):
                    w = lambda k: cpg[:, 5 * t + k:5 * t + k + 1]
                    r, o = raw[:, t % 2], feats[:, t]
                    dve.wait_ge(raw_ok, g * NP + 3 * t + 3)
                    ch.link(nc.vector.tensor_scalar(o, r[:, 3:3 + L], w(3), w(4), ALU.mult, ALU.add))
                    ch.link(stt(o, r[:, 2:2 + L], w(2), o, ALU.mult, ALU.add))
                    ch.link(stt(o, r[:, 1:1 + L], w(1), o, ALU.mult, ALU.add))
                    stt(o, r[:, 0:L], w(0), o, ALU.mult, ALU.add).then_inc(conv_ok, 1)

                def make_xdt(c):
                    n = META if c == 0 else P
                    dve.wait_ge(xturn, g * 9 + c + 1)
                    if c >= 2:
                        dve.wait_ge(xst_ok, g * 8 + c - 1)
                    if c >= 3:
                        dve.wait_ge(ydiag_ok, g * 8 + c - 2)
                    tt(xdt[0:n, c % 2].rearrange("p (h d) -> p h d", h=HG), ps[0:n, 1024:1536].rearrange("p (h d) -> p h d", h=HG),
                       smg[0:n, 2, c].unsqueeze(2).to_broadcast([n, HG, 64]), ALU.mult).then_inc(xdt_ok, 1)

                def copy_b(c):
                    n = META if c == 0 else P
                    dve.wait_ge(bturn, g * 9 + c + 1)
                    if c >= 2:
                        dve.wait_ge(st_ok, g * 8 + c - 1)
                    nc.vector.tensor_copy(btok[0:n, c % 2], ps[0:n, 1536:1536 + P]).then_inc(b_ok, 1)

                make_xdt(0)
                copy_b(0)
                for c in range(NCH):
                    a, b = chunk_cols(c)
                    if c < 8:
                        d = c + 1
                        make_xdt(d)
                        if d < 8:
                            copy_b(d)
                        dve.wait_ge(bturn, g * 9 + d + 1)
                        tt(cb[:, d % 2], ps[:, 1664:1664 + P], K.tri[:, :], ALU.mult).then_inc(cb_ok, 1)
                        dve.wait_ge(sums_ok, g * 8 + d)
                        if d >= 3:
                            dve.wait_ge(ydiag_ok, g * 8 + d - 2)
                        for r in range(HG):
                            last = nc.vector.tensor_scalar(seg[:, d % 2, r], ps[:, 2048 + P * r:2048 + P * (r + 1)],
                                                           smg[:, 1, d, r:r + 1], smg[:, 1, d, r:r + 1], ALU.min, ALU.subtract)
                        last.then_inc(seg_ok, 1)
                    if c >= 1:
                        dve.wait_ge(yoff_ok, g * 8 + c)
                        tt(yoff[:, :].rearrange("p (h d) -> p h d", h=HG), bank(7).rearrange("p (h d) -> p h d", h=HG),
                           smg[:, 5, c].unsqueeze(2).to_broadcast([P, HG, 64]), ALU.mult).then_inc(t_ok, 1)
                        dve.wait_ge(t_ok, g * 8 + c)
                        dve.wait_ge(ydiag_ok, g * 8 + c)
                        if c >= 3:
                            dve.wait_ge(yturn, g * 8 + c - 2)
                        tt(ytok[:, c % 2], bank(6), yoff[:, :], ALU.add).then_inc(y_ok, 1)
                    if c <= 7:
                        if c == 0:
                            dve.wait_ge(st_ok, g * 8 + 1)
                            nc.vector.tensor_copy(state[:, :], bank(7)).then_inc(h_ok, 1)
                        else:
                            ch.link(tt(state[:, :].rearrange("p (h d) -> p h d", h=HG), state[:, :].rearrange("p (h d) -> p h d", h=HG),
                                       smg[:, 4, c].unsqueeze(2).to_broadcast([P, HG, 64]), ALU.mult))
                            dve.wait_ge(st_ok, g * 8 + c + 1)
                            tt(state[:, :], state[:, :], bank(7), ALU.add).then_inc(h_ok, 1)
                    if c < 8:
                        dve.wait_ge(exp_ok, g * 8 + c + 1)
                        dve.wait_ge(cb_ok, g * 8 + c + 1)
                        tt(seg[:, (c + 1) % 2], seg[:, (c + 1) % 2], cb[:, (c + 1) % 2].unsqueeze(1).to_broadcast([P, HG, P]),
                           ALU.mult).then_inc(m_ok, 1)
                    for e in ([c - 1] if 2 <= c < 8 else [7, 8] if c == 8 else []):
                        a, b = chunk_cols(e)
                        dve.wait_ge(yturn, g * 8 + e)
                        for f in range(4):
                            last = stt(feats[:, f, a:b], feats[:, f, a:b], cpg[:, 30 + f:31 + f], ps[:, 512 + P * f:512 + P * (f + 1)],
                                       ALU.mult, ALU.add)
                        last.then_inc(y1_ok, 1)
                dve.wait_ge(y1_ok, g * 8 + 8)
                for f in range(4):
                    dve.wait_ge(zsilu, g * 4 + f + 1)
                    tt(feats[:, f, META:L], feats[:, f, META:L], z[:, f], ALU.mult).then_inc(u_ok, 1)
                dve.wait_ge(rooted, g * 2 + 4)
                ch.link(nc.vector.reciprocal(rms[:, :], rms[:, :]))
                dve.wait_ge(sq_ok, g * 4 + 4)
                for f in range(4):
                    stt(feats[:, f, META:L], feats[:, f, META:L], cpg[:, 34 + f:35 + f], rms[:, :], ALU.mult, ALU.mult).then_inc(yf_ok, 1)
                dve.wait_ge(yf_ok, g * 4 + 4)
                assert ch.n == ch.per, ch.n


def ssd_out_phase(nc, K):
    NY = 16
    with ExitStack() as ctx:
        sb = lambda n, sh, dt=F32: ctx.enter_context(nc.sbuf_tensor(n, sh, dt))
        W = K.W
        yraw = sb("yo_raw", [P, NY, 512])
        y_hi, y_lo = sb("yo_hi", [P, NY, 512], F32R), sb("yo_lo", [P, NY, 512], F32R)
        res = sb("yo_out", [P, 2, 512])
        s = lambda n: semaphore(nc, ctx, "so_" + n)
        y_in = [s(f"yin{q}") for q in range(4)]
        hi_ok, lo_ok, done, copied, stored = s("hi"), s("lo"), s("done"), s("copied"), [s("stored0"), s("stored1")]
        block = ctx.enter_context(nc.Block())
        ps = K.psum
        y_src = K.s["y"].rearrange("(q t) p (h c) -> h q p t c", h=2, q=4)
        out = K.s["pssd"].rearrange("f p (h c) -> h f p c", h=2)

        @block.sync
        def _(sp):
            with sp.Fori(0, 2) as h:
                for k in range(NY):
                    W.load(sp, h, NY, k)
            for r in range(2):
                sp.wait_ge(stored[r], 16 * 8)

        @block.gpsimd
        def _(pool):
            with pool.Fori(0, 2) as h:
                for n in range(NY):
                    W.split(pool, h, NY, n)

        @block.tensor
        def _(pe):
            with pe.Fori(0, 2) as h:
                for f in range(8):
                    pe.wait_ge(copied, h * 8 + f + 1)
                    for p in range(2):
                        W.wait(pe, h, NY, 2 * f + p)
                        for k in range(KT):
                            if f == 0:
                                pe.wait_ge(lo_ok, h * NY + 8 * p + k + 1)
                            last = gemm_k(nc, ps[:, 512 * (f % 4):512 * (f % 4 + 1)], W.hi[:, p], W.lo[:, p],
                                          y_hi[:, 8 * p + k], y_lo[:, 8 * p + k], k, first=(p == 0), final=(p == 1))
                        last.then_inc(done, 1)

        @block.scalar
        def _(act):
            act.sem_inc(copied, 4)

            def fetch(h, q):
                if h == 1:
                    act.wait_ge(lo_ok, 4 * q + 4)
                act.dma_start(yraw[:, 4 * q:4 * q + 4], y_src[h, q]).then_inc(y_in[q], 16)

            def split(h, k):
                act.wait_ge(y_in[k // 4], 16 * h + 16)
                nc.scalar.activation(y_hi[:, k], yraw[:, k], ACT.Copy).then_inc(hi_ok, 1)

            def release(n):
                act.wait_ge(done, n + 1)
                act.sem_inc(W.used, 1)

            def finish(h, f):
                release(16 * h + 2 * f + 1)
                if h == 1 or f >= 2:
                    act.wait_ge(stored[f % 2], h * 64 + 16 * (f // 2))
                nc.scalar.activation(res[:, f % 2], ps[:, 512 * (f % 4):512 * (f % 4 + 1)], ACT.Copy).then_inc(copied, 1)
                act.wait_ge(copied, h * 8 + f + 5)
                act.dma_start(out[h, f], res[:, f % 2]).then_inc(stored[f % 2], 16)

            for q in range(4):
                fetch(0, q)
            for k in range(NY):
                split(0, k)
            for q in range(4):
                fetch(1, q)
            for f in range(7):
                release(2 * f)
                finish(0, f)
            release(14)
            for k in range(8):
                split(1, k)
            finish(0, 7)
            for k in range(8, NY):
                split(1, k)
            for f in range(8):
                release(16 + 2 * f)
                finish(1, f)

        @block.vector
        def _(dve):
            for k in range(2 * NY):
                dve.wait_ge(hi_ok, k + 1)
                nc.vector.tensor_tensor(y_lo[:, k % NY], yraw[:, k % NY], y_hi[:, k % NY].bitcast(F32), ALU.subtract).then_inc(lo_ok, 1)


def pieces_of(n):
    return [(a, min(a + 512, n)) for a in range(0, n, 512)]


def run_passes(eng, n, one):
    with eng.Fori(0, n // 2 - 1) as i:
        one(i * 2, 0, True)
        one(i * 2 + 1, 1, True)
    one(n - 2, 0, True)
    one(n - 1, 1, False)


def fox_phase(nc, K, u_hi, u_lo):
    PAIRS = ATT_H // 2
    NB = 16
    step = [(b // 8, b % 8) for b in range(NB)]
    keys = lambda i: META + P * (i + 1)
    groups = [(b, k0, min(4, step[b][1] + 2 - k0)) for b in range(NB) for k0 in range(0, step[b][1] + 2, 4)]
    NG = len(groups)
    last_of = [max(x for x in range(NG) if groups[x][0] == b) for b in range(NB)]
    by_act = [x % 2 == 1 for x in range(NG)]
    n_act, n_dve = sum(by_act), NG - sum(by_act)
    units = [(0, a, b) for a, b in HALVES] + [(1, a, b) for a, b in THIRDS] + [(2, a, b) for a, b in THIRDS] + \
            [(3, a, b) for a, b in HALVES]
    NU = len(units)
    spread = [(u, 3) for u in range(6)] + [(6, 2), (7, 2), (8, 3)] + [(NU + m, 1) for m in range(3)]
    B, PER = len(spread), len(spread) + 2
    use_of = {u: n for n, (u, _) in enumerate(spread)}
    use_of[NU - 1] = B + 1
    parts = lambda u: [(u, k) for k in range(KT if u < NU else 1)]
    shares = []
    for u, n in spread:
        shares += [parts(u)[(len(parts(u)) * m + n - 1) // n:(len(parts(u)) * (m + 1) + n - 1) // n] for m in range(n)]
    assert len(shares) == NG
    share = lambda x: shares[x]
    body, tail = [item for x in shares for item in x], parts(NU - 1)
    with ExitStack() as ctx:
        sb = lambda n, sh, dt=F32: ctx.enter_context(nc.sbuf_tensor(n, sh, dt))
        W = K.W
        qT, kT, vT, zT = sb("f_qT", [P, 2, T]), sb("f_kT", [P, 2, L]), sb("f_vT", [P, L]), sb("f_zT", [P, 2, T])
        vtok = sb("f_v", [P, 2, CH + 1, P])
        ncb = sb("f_decay", [P, 2, 2, L])
        S = sb("f_scores", [P, 3, L])
        pt = sb("f_pT", [P, 2, 4, P])
        otok = sb("f_o", [P, CH, P])
        yt = sb("f_y", [P, T])
        mx, nm, ls, rl = (sb(n, [P, 2, NB]) for n in ("f_max", "f_negmax", "f_sum", "f_rsum"))
        s = lambda n: semaphore(nc, ctx, "f_" + n)
        nc_in = [s("decay_in0"), s("decay_in1")]
        mm6, free6, carried = s("bank6_full"), s("bank6_free"), s("carried")
        qk_ok, ttr_ok, neg_ok, exp_ok = s("qk"), s("biased"), s("negmax"), s("exp")
        turned, copy_dve, copy_act, pv_ok = s("turned"), s("copy_dve"), s("copy_act"), s("pv")
        rl_ok, o_ok, z_ok, stored = s("rl"), s("o"), s("z"), s("stored")
        y1_turned, y1_read = s("y1_turned"), s("y1_read")
        block = ctx.enter_context(nc.Block())
        ps = K.psum
        sbase = lambda i: 0 if i % 2 else 1536
        TB, FB, OB = 2560, 3072, 3584
        y0_use = lambda p, more: (p + 1) * PER + (B if more else 0)
        nc_src = K.s["nc"].rearrange("(g j) l -> g j l", j=4)

        def wait_copy(eng, p, x):
            if by_act[x]:
                eng.wait_ge(copy_act, p * n_act + x // 2 + 1)
            else:
                eng.wait_ge(copy_dve, p * n_dve + x // 2 + 1)

        @block.sync
        def _(sp):
            with sp.Fori(0, PAIRS // 2) as i:
                for q in range(2):
                    for n in range(4):
                        W.load(sp, i, 8, 4 * q + n)
                    sp.wait_ge(ttr_ok, i * 2 * NB + q * NB + NB)
                    for j in range(2):
                        sp.dma_start(ncb[:, q, j], nc_src[i, 2 * q + j:2 * q + j + 1].to_broadcast([P, L])).then_inc(nc_in[q], 16)
            sp.wait_ge(stored, 16 * PAIRS + 16)

        @block.gpsimd
        def _(pool):
            with pool.Fori(0, PAIRS) as h:
                for n in range(4):
                    W.split(pool, h, 4, n)

        @block.tensor
        def _(pe):

            def project(p, r, item):
                u, k = item
                if k == 0:
                    pe.wait_ge(free6, p * PER + use_of[u] + 1)
                if u < NU:
                    t, a, b = units[u]
                    if k == 0 and (u == 0 or units[u - 1][0] != t):
                        W.wait(pe, p, 4, t)
                    last = gemm_k(nc, ps[:, FB:FB + b - a], W.hi[:, t % 2], W.lo[:, t % 2], u_hi[:, k, a:b], u_lo[:, k, a:b], k)
                    if k == KT - 1:
                        last.then_inc(mm6, 1)
                else:
                    for c in range(4 * (u - NU), min(4 * (u - NU) + 4, CH + 1)):
                        a, b = (META + P * c, META + P * (c + 1)) if c < CH else (0, META)
                        last = nc.tensor.transpose(ps[0:b - a, FB + P * (c % 4):FB + P * (c % 4 + 1)], vT[:, a:b], K.ident[:, :])
                    last.then_inc(mm6, 1)

            def scores(p, r, b):
                j, i = step[b]
                pe.wait_ge(ttr_ok, p * NB + 2 * NB + b - 1)
                if b == 0:
                    pe.wait_ge(free6, p * PER + use_of[4] + 2)
                d0, d1 = META + P * i, META + P * (i + 1)
                for a, e in pieces_of(keys(i)):
                    masked = d0 < e and d1 > a
                    last = nc.tensor.matmul(ps[:, sbase(i) + a:sbase(i) + e], qT[64 * j:64 * j + 64, r, P * i:P * (i + 1)],
                                            kT[64 * j:64 * j + 64, r, a:e], start=True, stop=not masked)
                    if masked:
                        x, y = max(a, d0), min(e, d1)
                        last = nc.tensor.matmul(ps[:, sbase(i) + x:sbase(i) + y], K.identb[:, :],
                                                K.maskb[:, x - d0:y - d0], start=False, stop=True)
                last.then_inc(qk_ok, 1)

            def turn(p, x):
                b, k0, n = groups[x]
                if k0 == 0:
                    pe.wait_ge(exp_ok, p * NB + b + 1)
                if x >= 1:
                    wait_copy(pe, p, x - 1)
                else:
                    pe.wait_ge(y1_read, p + 1)
                for m in range(n):
                    c = 0 if k0 + m == 0 else META + P * (k0 + m - 1)
                    last = nc.tensor.transpose(ps[:, TB + P * m:TB + P * (m + 1)], S[:, b % 3, c:c + P], K.ident[:, :])
                last.then_inc(turned, 1)

            def values(p, r, x):
                b, k0, n = groups[x]
                j, i = step[b]
                if k0 == 0:
                    pe.wait_ge(o_ok, p * NB + b + 1)
                wait_copy(pe, p, x)
                for m in range(n):
                    kb = k0 + m
                    rows, c = (META, CH) if kb == 0 else (P, kb - 1)
                    last = nc.tensor.matmul(ps[:, OB:OB + 64], pt[0:rows, x % 2, m], vtok[0:rows, r, c, 64 * j:64 * j + 64],
                                            start=(kb == 0), stop=(kb == i + 1))
                last.then_inc(pv_ok, 1)

            def one(p, r, more):
                for x in range(NG):
                    b, k0, n = groups[x]
                    turn(p, x)
                    if k0 == 0 and b + 2 < NB:
                        scores(p, r, b + 2)
                    if more:
                        for item in share(x):
                            project(p + 1, 1 - r, item)
                    if x >= 1:
                        values(p, r, x - 1)
                values(p, r, NG - 1)
                if more:
                    scores(p + 1, 1 - r, 0)
                pe.wait_ge(o_ok, p * NB + NB + 1)
                pe.wait_ge(free6, y0_use(p, more) + 1)
                for m in range(4):
                    last = nc.tensor.transpose(ps[:, FB + P * m:FB + P * (m + 1)], otok[:, m], K.ident[:, :])
                last.then_inc(mm6, 1)
                for m in range(4):
                    last = nc.tensor.transpose(ps[:, TB + P * m:TB + P * (m + 1)], otok[:, 4 + m], K.ident[:, :])
                last.then_inc(y1_turned, 1)
                if more:
                    scores(p + 1, 1 - r, 1)
                    for item in tail:
                        project(p + 1, 1 - r, item)

            for item in body:
                project(0, 0, item)
            scores(0, 0, 0)
            pe.wait_ge(free6, B + 1)
            pe.sem_inc(mm6, 1)
            scores(0, 0, 1)
            for item in tail:
                project(0, 0, item)
            run_passes(pe, PAIRS, one)

        @block.scalar
        def _(act):
            act.sem_inc(free6, 1)

            def empty6(p, r, u):
                act.wait_ge(mm6, p * PER + use_of[u] + 1)
                if u < NU:
                    t, a, b = units[u]
                    if u + 1 == NU or units[u + 1][0] != t:
                        act.sem_inc(W.used, 1)
                    dst = [qT[:, r, a - META:b - META], kT[:, r, a:b], vT[:, a:b], zT[:, r, a - META:b - META]][t]
                    nc.scalar.activation(dst, ps[:, FB:FB + b - a], ACT.Copy).then_inc(free6, 1)
                elif u < NU + 2:
                    m = u - NU
                    nc.scalar.activation(vtok[:, r, 4 * m:4 * m + 4].rearrange("p c n -> p (c n)"), ps[:, FB:FB + 512], ACT.Copy).then_inc(free6, 1)
                else:
                    nc.scalar.activation(vtok[0:META, r, CH], ps[0:META, FB:FB + P], ACT.Copy).then_inc(free6, 1)

            def exps(p, r, b):
                n = keys(step[b][1])
                act.wait_ge(neg_ok, p * NB + b + 1)
                nc.scalar.activation(S[:, b % 3, 0:n], S[:, b % 3, 0:n], ACT.Exp, bias=nm[:, r, b:b + 1],
                                     accum_out=ls[:, r, b:b + 1]).then_inc(exp_ok, 1)

            def one(p, r, more):
                for x in range(NG):
                    b, k0, n = groups[x]
                    if by_act[x]:
                        act.wait_ge(turned, p * NG + x + 1 + NG)
                        if x >= 2:
                            act.wait_ge(pv_ok, p * NG + x - 1)
                        nc.scalar.activation(pt[:, x % 2, 0:n].rearrange("p m n -> p (m n)"), ps[:, TB:TB + P * n], ACT.Copy).then_inc(copy_act, 1)
                    if k0 == 0 and b + 2 < NB:
                        exps(p, r, b + 2)
                    if x == NG // 2:
                        act.wait_ge(free6, (p + 1) * PER + 1)
                        nc.scalar.activation(zT[:, r], zT[:, r], ACT.Silu).then_inc(z_ok, 1)
                    if more:
                        for u, k in share(x):
                            if k == KT - 1 or u >= NU:
                                empty6(p + 1, 1 - r, u)
                if more:
                    exps(p + 1, 1 - r, 0)
                    exps(p + 1, 1 - r, 1)
                    empty6(p + 1, 1 - r, NU - 1)
                act.wait_ge(y1_read, p + 2)
                act.dma_start(y_dst(p), yt[:, :]).then_inc(stored, 16)

            def y_dst(p):
                return K.s["yatt"][bass.ds(p, 1)].rearrange("a p t -> (a p) t")

            for u, _ in spread:
                empty6(0, 0, u)
            act.wait_ge(free6, B + 1)
            act.sem_inc(free6, 1)
            exps(0, 0, 0)
            exps(0, 0, 1)
            empty6(0, 0, NU - 1)
            run_passes(act, PAIRS, one)

        @block.vector
        def _(dve):
            dve.sem_inc(ttr_ok, 2 * NB)
            dve.sem_inc(turned, NG)
            dve.sem_inc(o_ok, 1)
            dve.sem_inc(y1_read, 1)
            dve.sem_inc(stored, 16)

            def biased(p, r, b):
                j, i = step[b]
                n = keys(i)
                if b == 0:
                    dve.wait_ge(nc_in[r], p * 16 + 32 - 16 * r)
                dve.wait_ge(qk_ok, p * NB + b + 1)
                dve.wait_ge(turned, p * NG + last_of[b - 3] + 1 - (NG if b < 3 else 0) + NG)
                dve.sem_inc(carried, 1)
                nc.vector.tensor_tensor_reduce(out=S[:, b % 3, 0:n], in0=ps[:, sbase(i):sbase(i) + n], in1=ncb[:, r, j, 0:n],
                                               scale=0.125, scalar=-3e38, op0=ALU.add, op1=ALU.max,
                                               accum_out=mx[:, r, b:b + 1]).then_inc(ttr_ok, 1)
                dve.wait_ge(ttr_ok, p * NB + 2 * NB + b + 1)
                nc.vector.tensor_scalar(nm[:, r, b:b + 1], mx[:, r, b:b + 1], -1.0, None, ALU.mult).then_inc(neg_ok, 1)

            def one(p, r, more):
                for x in range(NG):
                    b, k0, n = groups[x]
                    if not by_act[x]:
                        dve.wait_ge(turned, p * NG + x + 1 + NG)
                        if x >= 2:
                            dve.wait_ge(pv_ok, p * NG + x - 1)
                        nc.vector.tensor_copy(pt[:, x % 2, 0:n].rearrange("p m n -> p (m n)"), ps[:, TB:TB + P * n]).then_inc(copy_dve, 1)
                    if k0 == 0 and b + 2 < NB:
                        biased(p, r, b + 2)
                    if x >= 1 and x - 1 == last_of[groups[x - 1][0]]:
                        output(p, r, groups[x - 1][0])
                output(p, r, NB - 1)
                dve.wait_ge(stored, p * 16 + 16)
                dve.wait_ge(z_ok, p + 1)
                dve.wait_ge(mm6, y0_use(p, more) + 1)
                nc.vector.tensor_tensor(yt[:, 0:512], ps[:, FB:FB + 512], zT[:, r, 0:512], ALU.mult).then_inc(free6, 1)
                dve.wait_ge(y1_turned, p + 1)
                nc.vector.tensor_tensor(yt[:, 512:T], ps[:, TB:TB + 512], zT[:, r, 512:T], ALU.mult).then_inc(y1_read, 1)
                if more:
                    biased(p + 1, 1 - r, 0)
                    biased(p + 1, 1 - r, 1)

            def output(p, r, b):
                j, i = step[b]
                dve.wait_ge(exp_ok, p * NB + b + 1)
                nc.vector.reciprocal(rl[:, r, b:b + 1], ls[:, r, b:b + 1]).then_inc(rl_ok, 1)
                dve.wait_ge(rl_ok, p * NB + b + 1)
                dve.wait_ge(pv_ok, p * NG + last_of[b] + 1)
                nc.vector.tensor_scalar(otok[:, i, 64 * j:64 * j + 64], ps[:, OB:OB + 64], rl[:, r, b:b + 1], None,
                                        ALU.mult).then_inc(o_ok, 1)

            biased(0, 0, 0)
            biased(0, 0, 1)
            run_passes(dve, PAIRS, one)


def merge_phase(nc, K, u_hi, u_lo):
    with ExitStack() as ctx:
        sb = lambda n, sh, dt=F32: ctx.enter_context(nc.sbuf_tensor(n, sh, dt))
        W = K.W
        raw = sb("m_raw", [P, 2, T])
        y_hi, y_lo = sb("m_yhi", [P, KT, T], F32R), sb("m_ylo", [P, KT, T], F32R)
        pssd = sb("m_pssd", [P, 2, T])
        sg, sa = sb("m_sg", [P, T]), sb("m_sa", [P, T])
        bias = sb("m_bias", [P, 2 * KT])
        s = lambda n: semaphore(nc, ctx, "m_" + n)
        y_in, hi_ok, lo_ok, p_in = [s("yin0"), s("yin1")], s("hi"), s("lo"), [s("pin0"), s("pin1")]
        b_in, unit, sig_ok, g1_ok, g2_ok, gm, m_ok = s("bin"), s("unit"), s("sig"), s("g1"), s("g2"), s("gm"), s("m")
        stored = [s("stored0"), s("stored1")]
        block = ctx.enter_context(nc.Block())
        ps = K.psum

        def store(act, f):
            act.wait_ge(m_ok, f + 1)
            act.dma_start(K.s["merged"][f], pssd[:, f % 2]).then_inc(stored[f % 2], 16)
            if f + 2 < KT:
                act.wait_ge(stored[f % 2], 16 * (f // 2 + 1))
                act.dma_start(pssd[:, f % 2], K.s["pssd"][f + 2]).then_inc(p_in[f % 2], 16)

        @block.sync
        def _(sp):
            sp.dma_start(bias[:, :], K.d["gate_bias"]).then_inc(b_in, 16)
            with sp.Fori(0, 4) as g:
                for n in range(6):
                    W.load(sp, g, 6, n)

        @block.gpsimd
        def _(pool):
            with pool.Fori(0, 4) as g:
                for n in range(6):
                    W.split(pool, g, 6, n)

        @block.tensor
        def _(pe):
            with pe.Fori(0, 4) as g:
                for q in range(2):
                    for n in range(3):
                        W.wait(pe, g, 6, 3 * q + n)
                        if n < 2:
                            pe.wait_ge(sig_ok, g * 8 + 4 * q + 2 * n + 2)
                        else:
                            pe.wait_ge(g2_ok, g * 4 + 2 * q + 2)
                            if q == 0:
                                pe.wait_ge(lo_ok, KT)
                        wl, wh = W.lo[:, (3 * q + n) % 2], W.hi[:, (3 * q + n) % 2]
                        for h in range(2):
                            if n < 2:
                                act_hi = lambda k: u_hi[:, k, META + 512 * h:META + 512 * (h + 1)]
                                act_lo = lambda k: u_lo[:, k, META + 512 * h:META + 512 * (h + 1)]
                            else:
                                act_hi = lambda k: y_hi[:, k, 512 * h:512 * (h + 1)]
                                act_lo = lambda k: y_lo[:, k, 512 * h:512 * (h + 1)]
                            gemm(nc, ps[:, 1024 * n + 512 * h:1024 * n + 512 * (h + 1)], wh, wl, act_hi, act_lo).then_inc(unit, 1)

        @block.scalar
        def _(act):
            act.sem_inc(sig_ok, 4)
            for k in range(2):
                act.dma_start(raw[:, k], K.s["yatt"][k]).then_inc(y_in[k], 16)
                act.dma_start(pssd[:, k], K.s["pssd"][k]).then_inc(p_in[k], 16)
            for k in range(KT):
                act.wait_ge(y_in[k % 2], 16 * (k // 2 + 1))
                nc.scalar.activation(y_hi[:, k], raw[:, k % 2], ACT.Copy).then_inc(hi_ok, 1)
                if k + 2 < KT:
                    act.wait_ge(lo_ok, k + 1)
                    act.dma_start(raw[:, k % 2], K.s["yatt"][k + 2]).then_inc(y_in[k % 2], 16)
            act.wait_ge(b_in, 16)
            for f in range(KT):
                for n in range(2):
                    for h in range(2):
                        act.wait_ge(unit, 6 * f + 2 * n + h + 1)
                        if h == 1:
                            act.sem_inc(W.used, 1)
                        if f >= 1:
                            act.wait_ge(g1_ok if n == 0 else g2_ok, 2 * f if n == 0 else 2 * f + 2)
                        nc.scalar.activation((sa if n else sg)[:, 512 * h:512 * (h + 1)], ps[:, 1024 * n + 512 * h:1024 * n + 512 * (h + 1)],
                                             ACT.Sigmoid, bias=bias[:, KT * n + f:KT * n + f + 1]).then_inc(sig_ok, 1)
                if f >= 1:
                    store(act, f - 1)
                act.wait_ge(unit, 6 * f + 6)
                act.sem_inc(W.used, 1)
            store(act, KT - 1)
            for f in (KT - 2, KT - 1):
                act.wait_ge(stored[f % 2], 64)

        @block.vector
        def _(dve):
            dve.sem_inc(g2_ok, 2)
            for k in range(KT):
                dve.wait_ge(hi_ok, k + 1)
                nc.vector.tensor_tensor(y_lo[:, k], raw[:, k % 2], y_hi[:, k].bitcast(F32), ALU.subtract).then_inc(lo_ok, 1)
            for f in range(KT):
                dve.wait_ge(p_in[f % 2], 16 * (f // 2 + 1))
                p = pssd[:, f % 2]
                for h in range(2):
                    c = slice(512 * h, 512 * (h + 1))
                    dve.wait_ge(sig_ok, 4 + 4 * f + h + 1)
                    nc.vector.tensor_tensor(p[:, c], p[:, c], sg[:, c], ALU.mult).then_inc(g1_ok, 1)
                for h in range(2):
                    c = slice(512 * h, 512 * (h + 1))
                    dve.wait_ge(unit, 6 * f + 4 + h + 1)
                    dve.wait_ge(sig_ok, 4 + 4 * f + 2 + h + 1)
                    nc.vector.tensor_tensor(sa[:, c], sa[:, c], ps[:, 2048 + 512 * h:2048 + 512 * (h + 1)], ALU.mult).then_inc(gm, 1)
                    dve.wait_ge(gm, 2 * f + h + 1)
                    dve.wait_ge(g1_ok, 2 * f + h + 1)
                    last = nc.vector.tensor_tensor(p[:, c], p[:, c], sa[:, c], ALU.add)
                    last.then_inc(g2_ok, 1)
                dve.wait_ge(g2_ok, 2 * f + 4)
                dve.sem_inc(m_ok, 1)


def linear_phase(nc, K, name, src, dst, add=False):
    with ExitStack() as ctx:
        sb = lambda n, sh, dt=F32: ctx.enter_context(nc.sbuf_tensor(name + n, sh, dt))
        W = K.W
        raw = sb("_raw", [P, 4, T])
        a_hi, a_lo = sb("_hi", [P, KT, T], F32R), sb("_lo", [P, KT, T], F32R)
        s = lambda n: semaphore(nc, ctx, name + n)
        a_in, hi_ok, lo_ok, unit, copied = [s(f"_in{r}") for r in range(4)], s("_hi_ok"), s("_lo_ok"), s("_unit"), s("_copied")
        block = ctx.enter_context(nc.Block())
        ps = K.psum

        @block.sync
        def _(sp):
            for k in range(2):
                W.load(sp, 0, 8, k)
            for k in range(KT):
                if k >= 4:
                    sp.wait_ge(lo_ok, k - 3)
                sp.dma_start(raw[:, k % 4], src[k]).then_inc(a_in[k % 4], 16)
            for k in range(2, KT):
                W.load(sp, 0, 8, k)

        @block.gpsimd
        def _(pool):
            for n in range(KT):
                W.split(pool, 0, 8, n)

        @block.tensor
        def _(pe):
            for f in range(KT):
                W.wait(pe, 0, 8, f)
                if f == 0:
                    for k in range(KT):
                        pe.wait_ge(lo_ok, k + 1)
                        for h in range(2):
                            last = gemm_k(nc, ps[:, 512 * h:512 * (h + 1)], W.hi[:, 0], W.lo[:, 0],
                                          a_hi[:, k, 512 * h:512 * (h + 1)], a_lo[:, k, 512 * h:512 * (h + 1)], k)
                            if k == KT - 1:
                                last.then_inc(unit, 1)
                    continue
                for h in range(2):
                    u = 2 * f + h
                    if u >= 8:
                        pe.wait_ge(copied, u - 7)
                    gemm(nc, ps[:, 512 * (u % 8):512 * (u % 8 + 1)], W.hi[:, f % 2], W.lo[:, f % 2],
                         lambda k: a_hi[:, k, 512 * h:512 * (h + 1)], lambda k: a_lo[:, k, 512 * h:512 * (h + 1)]).then_inc(unit, 1)

        @block.scalar
        def _(act):
            for k in range(KT):
                act.wait_ge(a_in[k % 4], 16 * (k // 4 + 1))
                nc.scalar.activation(a_hi[:, k], raw[:, k % 4], ACT.Copy).then_inc(hi_ok, 1)
            for u in range(2 * KT):
                act.wait_ge(unit, u + 1)
                if u % 2 == 1:
                    act.sem_inc(W.used, 1)
                if add:
                    continue
                nc.scalar.activation(dst[:, u // 2, 512 * (u % 2):512 * (u % 2 + 1)], ps[:, 512 * (u % 8):512 * (u % 8 + 1)],
                                     ACT.Copy).then_inc(copied, 1)

        @block.vector
        def _(dve):
            for k in range(KT):
                dve.wait_ge(hi_ok, k + 1)
                nc.vector.tensor_tensor(a_lo[:, k], raw[:, k % 4], a_hi[:, k].bitcast(F32), ALU.subtract).then_inc(lo_ok, 1)
            if add:
                for u in range(2 * KT):
                    dve.wait_ge(unit, u + 1)
                    at = dst[:, u // 2, 512 * (u % 2):512 * (u % 2 + 1)]
                    nc.vector.tensor_tensor(at, at, ps[:, 512 * (u % 8):512 * (u % 8 + 1)], ALU.add).then_inc(copied, 1)


def residual_phase(nc, K, o, gain, xr):
    with ExitStack() as ctx:
        sb = lambda n, sh, dt=F32: ctx.enter_context(nc.sbuf_tensor(n, sh, dt))
        sq, rs = sb("r_sq", [P, 2, T]), sb("r_rs", [P, T])
        s = lambda n: semaphore(nc, ctx, "r_" + n)
        x_in, squared, summed, rooted, inv, scaled, added = (s(n) for n in ["xin", "squared", "summed", "rooted", "inv", "scaled", "added"])
        added_pool = s("added_pool")
        POOL = 4
        block = ctx.enter_context(nc.Block())
        ps = K.psum

        @block.sync
        def _(sp):
            sp.dma_start(xr[:, :, :], K.s["xT"].rearrange("k p t -> p k t")).then_inc(x_in, 16)

        @block.scalar
        def _(act):
            for k in range(KT):
                if k >= 2:
                    act.wait_ge(summed, k - 1)
                nc.scalar.activation(sq[:, k % 2], o[:, k], ACT.Square).then_inc(squared, 1)
            act.wait_ge(summed, KT)
            for h in range(2):
                nc.scalar.activation(rs[:, 512 * h:512 * (h + 1)], ps[:, 512 * h:512 * (h + 1)], ACT.Sqrt, scale=1.0 / D,
                                     bias=K.eps[:, 0:1]).then_inc(rooted, 1)

        @block.tensor
        def _(pe):
            for k in range(KT):
                pe.wait_ge(squared, k + 1)
                for h in range(2):
                    last = nc.tensor.matmul(ps[:, 512 * h:512 * (h + 1)], K.ones[:, :], sq[:, k % 2, 512 * h:512 * (h + 1)],
                                            start=(k == 0), stop=(k == KT - 1))
                last.then_inc(summed, 1)

        @block.vector
        def _(dve):
            dve.wait_ge(rooted, 2)
            nc.vector.reciprocal(rs[:, :], rs[:, :]).then_inc(inv, 1)
            dve.wait_ge(inv, 1)
            for k in range(KT):
                nc.vector.scalar_tensor_tensor(o[:, k], o[:, k], gain[:, k:k + 1], rs[:, :], ALU.mult, ALU.mult).then_inc(scaled, 1)
            dve.wait_ge(x_in, 16)
            for k in range(POOL, KT):
                dve.wait_ge(scaled, k + 1)
                nc.vector.tensor_tensor(xr[:, k], xr[:, k], o[:, k], ALU.add).then_inc(added, 1)

        @block.gpsimd
        def _(pool):
            pool.wait_ge(x_in, 16)
            for k in range(POOL):
                pool.wait_ge(scaled, k + 1)
                nc.gpsimd.tensor_tensor(xr[:, k], xr[:, k], o[:, k], ALU.add).then_inc(added_pool, 1)


def mixer_phase(nc, K, name, dil, u_hi, u_lo):
    NPASS, NB, NI = 4, 16, 8
    step = [(b // 8, b % 8) for b in range(NB)] if dil else [(b % 2, b // 2) for b in range(NB)]
    LEN = 2 * T - P
    NT = NB if dil else NI
    SPR = NB // NT
    NS = 3 if dil else 4
    VW = 64 if dil else P
    NG = 2 * NT
    by_act = [x % 2 == 1 or not dil for x in range(NG)]
    n_act, n_dve = sum(by_act), NG - sum(by_act)
    units = [(t, 512 * h, 512 * (h + 1)) for t in range(4) for h in range(2)]
    NU, SUMS = len(units), 10
    order = [0, 1, SUMS, 2, SUMS + 1, 3, SUMS + 2, 4, SUMS + 3, 5, 6, 7, NU, NU + 1]
    USES, PER = len(order), len(order) + 2
    use_of = {u: n for n, u in enumerate(order)}
    items = [(u, k) for u in order for k in range(KT if u < NU else 1)]
    TAIL = 9
    body, tail = items[:-TAIL], items[-TAIL:]
    share = lambda x: body[len(body) * x // NG:len(body) * (x + 1) // NG]
    with ExitStack() as ctx:
        sb = lambda n, sh, dt=F32: ctx.enter_context(nc.sbuf_tensor(name + n, sh, dt))
        W = K.W
        qk = sb("_qk", [P, 2, 2, T])
        vT, zT = sb("_vT", [P, T]), sb("_zT", [P, 2, T])
        vtok = sb("_v", [P, 2, CH, P])
        dist = sb("_dist", [P, LEN])
        count = sb("_count", [P, LEN]) if dil else None
        bias = sb("_bias", [P, LEN])
        slopes, par = sb("_slopes", [P, 8]), sb("_par", [P, 3])
        S = sb("_scores", [P, NS, T])
        sq = sb("_sq", [P, 2, 512])
        pt = sb("_pT", [P, 2, 4, P])
        otok = sb("_o", [P, CH, P])
        osq = sb("_osq", [P, P])
        mx, nm, ls, rl = (sb(n, [P, 2, NB]) for n in ("_max", "_negmax", "_sum", "_rsum"))
        oss = sb("_oss", [P, NI])
        s = lambda n: semaphore(nc, ctx, name + "_" + n)
        par_in, full, free, squared, inv, normed = (s(n) for n in
            ["par", "bank56_full", "bank56_free", "squared", "inv", "normed"])
        bias_ok, qk_ok, ttr_ok, neg_ok, exp_ok, carried = (s(n) for n in ["bias", "qk", "biased", "negmax", "exp", "carried"])
        turned, copy_act, copy_dve, pv_ok, rl_ok, part_ok, w_ok, o_ok, ss_ok, or_ok, on_ok, z_ok = (s(n) for n in
            ["turned", "copy_act", "copy_dve", "pv", "rl", "part", "w", "o", "ss", "or", "on", "z"])
        stored = [s("stored0"), s("stored1")]
        block = ctx.enter_context(nc.Block())
        ps = K.psum
        TB, OB = 2048, 3584
        shared = lambda n: ps[:, 2560 + 512 * (n % 2):3072 + 512 * (n % 2)]
        tile0 = 4 if dil else 0
        n_par = 4 if dil else 3

        before_y = lambda p, more: p * PER + PER + (USES if more else 0)

        def wait_copy(eng, p, x):
            if by_act[x]:
                eng.wait_ge(copy_act, p * n_act + sum(by_act[:x]) + 1)
            else:
                eng.wait_ge(copy_dve, p * n_dve + x - sum(by_act[:x]) + 1)

        @block.sync
        def _(sp):
            sp.dma_start(dist[:, :], K.d["dist"]).then_inc(par_in, 16)
            if dil:
                sp.dma_start(count[:, :], K.d["count"]).then_inc(par_in, 16)
            sp.dma_start(slopes[:, :], K.d["slopes_dil"] if dil else K.d["slopes_diff"]).then_inc(par_in, 16)
            sp.dma_start(par[:, :], K.d["par_dil"] if dil else K.d["par_diff"]).then_inc(par_in, 16)

            def store(p):
                sp.wait_ge(free, before_y(p, p + 1 < NPASS) + 4)
                sp.dma_start(K.s["mix"][tile0 + p], zT[:, p % 2]).then_inc(stored[p % 2], 16)

            for p in range(NPASS):
                for n in range(4):
                    if n == 2 and p >= 2:
                        store(p - 2)
                    W.load(sp, p, 4, n)
            store(NPASS - 2)
            store(NPASS - 1)
            for r in range(2):
                sp.wait_ge(stored[r], 16 * NPASS // 2 + 16)

        @block.gpsimd
        def _(pool):
            with pool.Fori(0, NPASS) as h:
                for n in range(4):
                    W.split(pool, h, 4, n)

        @block.tensor
        def _(pe):

            def project(p, r, item):
                u, k = item
                n = use_of[u]
                out = shared(n)
                if k == 0:
                    pe.wait_ge(free, p * PER + max(n + 1, 2))
                if u >= SUMS:
                    pe.wait_ge(squared, p * 4 + u - SUMS + 1)
                    nc.tensor.matmul(out, K.pairs[:, :], sq[:, u % 2], start=True, stop=True).then_inc(full, 1)
                elif u < NU:
                    t, a, b = units[u]
                    if k == 0 and u % 2 == 0:
                        W.wait(pe, p, 4, t)
                    last = gemm_k(nc, out, W.hi[:, t % 2], W.lo[:, t % 2], u_hi[:, k, a:b], u_lo[:, k, a:b], k)
                    if k == KT - 1:
                        last.then_inc(full, 1)
                else:
                    for m in range(4):
                        c = 4 * (u - NU) + m
                        last = nc.tensor.transpose(out[:, P * m:P * (m + 1)], vT[:, P * c:P * (c + 1)], K.ident[:, :])
                    last.then_inc(full, 1)

            def scores(p, r, b):
                j, i = step[b]
                pe.wait_ge(ttr_ok, p * NB + b + 1)
                if b == 0:
                    pe.wait_ge(normed, p * 4 + 6)
                for f in range(2):
                    last = nc.tensor.matmul(ps[:, 1024 * (b % 2) + 512 * f:1024 * (b % 2) + 512 * (f + 1)],
                                            qk[64 * j:64 * j + 64, r, 0, P * i:P * (i + 1)],
                                            qk[64 * j:64 * j + 64, r, 1, 512 * f:512 * (f + 1)], start=True, stop=True)
                last.then_inc(qk_ok, 1)

            def turn(p, x):
                rd, g = x // 2, x % 2
                if g == 0:
                    pe.wait_ge(exp_ok if dil else w_ok, p * NT + rd + 1)
                if x >= 1:
                    wait_copy(pe, p, x - 1)
                for m in range(4):
                    last = nc.tensor.transpose(ps[:, TB + P * m:TB + P * (m + 1)],
                                               S[:, rd * SPR % NS, 512 * g + P * m:512 * g + P * (m + 1)], K.ident[:, :])
                last.then_inc(turned, 1)

            def values(p, r, x):
                rd, g = x // 2, x % 2
                j = step[rd][0] if dil else 0
                if g == 0:
                    pe.wait_ge(o_ok, p * NT + rd + 1)
                wait_copy(pe, p, x)
                for m in range(4):
                    last = nc.tensor.matmul(ps[:, OB:OB + VW], pt[:, x % 2, m], vtok[:, r, 4 * g + m, 64 * j:64 * j + VW],
                                            start=(g == 0 and m == 0), stop=(g == 1 and m == 3))
                last.then_inc(pv_ok, 1)

            def one(p, r, more):
                for x in range(NG):
                    turn(p, x)
                    if x % 2 == 0:
                        for b in range(x // 2 * SPR + 2, x // 2 * SPR + 2 + SPR):
                            if b < NB:
                                scores(p, r, b)
                    if more:
                        for item in share(x):
                            project(p + 1, 1 - r, item)
                    if x >= 1:
                        values(p, r, x - 1)
                values(p, r, NG - 1)
                if more:
                    scores(p + 1, 1 - r, 0)
                    scores(p + 1, 1 - r, 1)
                    for item in tail:
                        project(p + 1, 1 - r, item)
                if dil:
                    pe.wait_ge(o_ok, p * NT + NT + 1)
                else:
                    pe.wait_ge(on_ok, p + 1)
                pe.wait_ge(free, before_y(p, more) + 2)
                for hf in range(2):
                    for m in range(4):
                        last = nc.tensor.transpose(shared(hf)[:, P * m:P * (m + 1)], otok[:, 4 * hf + m], K.ident[:, :])
                    last.then_inc(full, 1)

            for item in items:
                project(0, 0, item)
            scores(0, 0, 0)
            scores(0, 0, 1)
            pe.wait_ge(free, USES + 2)
            pe.sem_inc(full, 2)
            run_passes(pe, NPASS, one)

        @block.scalar
        def _(act):
            act.sem_inc(free, 2)

            def serve(p, r, item):
                u, k = item
                if k < KT - 1 and u < NU:
                    return
                bank = shared(use_of[u])
                act.wait_ge(full, p * PER + use_of[u] + 1)
                if u >= SUMS:
                    nc.scalar.activation(sq[:, u % 2], bank, ACT.Sqrt, scale=1.0 / 64, bias=K.eps[:, 0:1]).then_inc(free, 1)
                elif u >= NU:
                    c = 4 * (u - NU)
                    nc.scalar.activation(vtok[:, r, c:c + 4].rearrange("p c n -> p (c n)"), bank, ACT.Copy).then_inc(free, 1)
                else:
                    t, a, b = units[u]
                    if u % 2 == 1:
                        act.sem_inc(W.used, 1)
                    if u < 4:
                        act.wait_ge(normed, p * 4 + u - 2 + 1 + 2)
                        nc.scalar.activation(sq[:, u % 2], bank, ACT.Square).then_inc(squared, 1)
                    if u == 6:
                        act.wait_ge(stored[r], p * 8 - 8 * r + 16)
                    dst = [qk[:, r, 0, a:b], qk[:, r, 1, a:b], vT[:, a:b], zT[:, r, a:b]][t]
                    nc.scalar.activation(dst, bank, ACT.Copy).then_inc(free, 1)

            def exps(p, r, b):
                act.wait_ge(neg_ok, p * NB + b + 1)
                nc.scalar.activation(S[:, b % NS], S[:, b % NS], ACT.Exp, bias=nm[:, r, b:b + 1],
                                     accum_out=ls[:, r, b:b + 1]).then_inc(exp_ok, 1)

            def output_squares(p, rd):
                act.wait_ge(o_ok, p * NT + rd + 2)
                nc.scalar.activation(osq[:, :], otok[:, rd], ACT.Square, accum_out=oss[:, rd:rd + 1]).then_inc(ss_ok, 1)
                act.wait_ge(ss_ok, p * (NT + 1) + rd + 1)

            def one(p, r, more):
                for x in range(NG):
                    if by_act[x]:
                        act.wait_ge(turned, p * NG + x + 1)
                        if x >= 2:
                            act.wait_ge(pv_ok, p * NG + x - 1)
                        nc.scalar.activation(pt[:, x % 2].rearrange("p m n -> p (m n)"), ps[:, TB:TB + 512], ACT.Copy).then_inc(copy_act, 1)
                    if x % 2 == 0:
                        for b in range(x // 2 * SPR + 2, x // 2 * SPR + 2 + SPR):
                            if b < NB:
                                exps(p, r, b)
                    elif not dil and x >= 3:
                        output_squares(p, x // 2 - 1)
                    if x == NG // 2:
                        act.wait_ge(free, p * PER + USES + 2)
                        nc.scalar.activation(zT[:, r], zT[:, r], ACT.Silu).then_inc(z_ok, 1)
                    if more:
                        for item in share(x):
                            serve(p + 1, 1 - r, item)
                if more:
                    exps(p + 1, 1 - r, 0)
                    exps(p + 1, 1 - r, 1)
                if not dil:
                    output_squares(p, NT - 1)
                    nc.scalar.activation(oss[:, :], oss[:, :], ACT.Sqrt, scale=1.0 / P, bias=K.eps[:, 0:1]).then_inc(ss_ok, 1)
                if more:
                    for item in tail:
                        serve(p + 1, 1 - r, item)

            for item in items:
                serve(0, 0, item)
            act.wait_ge(free, USES + 2)
            act.sem_inc(free, 2)
            exps(0, 0, 0)
            exps(0, 0, 1)
            run_passes(act, NPASS, one)

        @block.vector
        def _(dve):
            dve.sem_inc(ttr_ok, 2)
            dve.sem_inc(normed, 2)
            dve.sem_inc(o_ok, 1)
            for r in range(2):
                dve.sem_inc(stored[r], 16)
            dve.wait_ge(par_in, 16 * n_par)
            stt, tt = nc.vector.scalar_tensor_tensor, nc.vector.tensor_tensor

            def norm(p, r, item):
                u, k = item
                if u >= SUMS:
                    n = u - SUMS
                    t, a, b = units[n]
                    dve.wait_ge(free, p * PER + use_of[u] + 3)
                    nc.vector.reciprocal(sq[:, n % 2], sq[:, n % 2]).then_inc(inv, 1)
                    dve.wait_ge(inv, p * 4 + n + 1)
                    stt(qk[:, r, t, a:b], qk[:, r, t, a:b], par[:, t:t + 1], sq[:, n % 2], ALU.mult, ALU.mult).then_inc(normed, 1)

            def piece(run, n, m=1):
                c, at = slice(LEN - P * (n + m), LEN - P * n), slopes[:, bass.ds(run, 1)]
                if dil:
                    stt(bias[:, c], dist[:, c], at, count[:, c], ALU.mult, ALU.add).then_inc(bias_ok, 1)
                else:
                    nc.vector.tensor_scalar(bias[:, c], dist[:, c], at, None, ALU.mult).then_inc(bias_ok, 1)

            def biased(p, r, b, more):
                j, i = step[b]
                run = p * 2 + j if dil else p
                first, last = (True, True) if dil else (j == 0, j == 1)
                ahead = more or (dil and j == 0)
                if first:
                    piece(run, 7 + i)
                    dve.wait_ge(bias_ok, run * 15 + 8 + (2 * i if ahead else i))
                dve.wait_ge(qk_ok, p * NB + b + 1)
                if b >= NS:
                    rd = (b - NS) // SPR
                    dve.wait_ge(turned, p * NG + 2 * rd + 2)
                dve.sem_inc(carried, 1)
                o = T - P - P * i
                nc.vector.tensor_tensor_reduce(out=S[:, b % NS], in0=ps[:, 1024 * (b % 2):1024 * (b % 2 + 1)],
                                               in1=bias[:, o:o + T], scale=0.125, scalar=-3e38,
                                               op0=ALU.add, op1=ALU.max, accum_out=mx[:, r, b:b + 1]).then_inc(ttr_ok, 1)
                dve.wait_ge(ttr_ok, p * NB + b + 3)
                nc.vector.tensor_scalar(nm[:, r, b:b + 1], mx[:, r, b:b + 1], -1.0, None, ALU.mult).then_inc(neg_ok, 1)
                if last and ahead and i < 7:
                    piece(run + 1, i)

            def inverse(p, r, b):
                dve.wait_ge(exp_ok, p * NB + b + 1)
                nc.vector.reciprocal(rl[:, r, b:b + 1], ls[:, r, b:b + 1]).then_inc(rl_ok, 1)

            def mix(p, r, rd):
                b = 2 * rd
                inverse(p, r, b)
                inverse(p, r, b + 1)
                dve.wait_ge(rl_ok, p * NB + b + 2)
                nc.vector.tensor_scalar(S[:, (b + 1) % 4], S[:, (b + 1) % 4], rl[:, r, b + 1:b + 2], K.neglam[:, 0:1],
                                        ALU.mult, ALU.mult).then_inc(part_ok, 1)
                dve.wait_ge(part_ok, p * NT + rd + 1)
                stt(S[:, b % 4], S[:, b % 4], rl[:, r, b:b + 1], S[:, (b + 1) % 4], ALU.mult, ALU.add).then_inc(w_ok, 1)

            def output(p, r, rd):
                if dil:
                    j, i = step[rd]
                    inverse(p, r, rd)
                    dve.wait_ge(rl_ok, p * NB + rd + 1)
                    dve.wait_ge(pv_ok, p * NG + 2 * rd + 2)
                    nc.vector.tensor_scalar(otok[:, i, 64 * j:64 * j + 64], ps[:, OB:OB + 64], rl[:, r, rd:rd + 1], None,
                                            ALU.mult).then_inc(o_ok, 1)
                else:
                    dve.wait_ge(pv_ok, p * NG + 2 * rd + 2)
                    dve.sem_inc(carried, 1)
                    nc.vector.tensor_copy(otok[:, rd], ps[:, OB:OB + P]).then_inc(o_ok, 1)

            def one(p, r, more):
                for x in range(NG):
                    rd = x // 2
                    if not by_act[x]:
                        dve.wait_ge(turned, p * NG + x + 1)
                        if x >= 2:
                            dve.wait_ge(pv_ok, p * NG + x - 1)
                        nc.vector.tensor_copy(pt[:, x % 2].rearrange("p m n -> p (m n)"), ps[:, TB:TB + 512]).then_inc(copy_dve, 1)
                    if x % 2 == 0:
                        for b in range(rd * SPR + 2, rd * SPR + 2 + SPR):
                            if b < NB:
                                biased(p, r, b, more)
                        if rd >= 1:
                            output(p, r, rd - 1)
                    elif not dil and rd + 1 < NT:
                        mix(p, r, rd + 1)
                    if more and (x >= 1 if dil else x % 2 == 1):
                        for item in (share(x - 2) if not dil and x >= 3 else []) + share(x - 1):
                            norm(p + 1, 1 - r, item)
                output(p, r, NT - 1)
                if more:
                    ahead = not (isinstance(p, int) and p == NPASS - 2)
                    biased(p + 1, 1 - r, 0, ahead)
                    biased(p + 1, 1 - r, 1, ahead)
                    if not dil:
                        mix(p + 1, 1 - r, 0)
                if not dil:
                    dve.wait_ge(ss_ok, p * (NT + 1) + NT + 1)
                    nc.vector.reciprocal(oss[:, :], oss[:, :]).then_inc(or_ok, 1)
                    dve.wait_ge(or_ok, p + 1)
                    tt(otok[:, :, :], otok[:, :, :], oss[:, :].unsqueeze(2).to_broadcast([P, NI, P]), ALU.mult).then_inc(on_ok, 1)
                dve.wait_ge(z_ok, p + 1)
                for hf in range(2):
                    c = slice(512 * hf, 512 * (hf + 1))
                    dve.wait_ge(full, before_y(p, more) + hf + 1)
                    if dil:
                        tt(zT[:, r, c], shared(hf), zT[:, r, c], ALU.mult).then_inc(free, 1)
                    else:
                        stt(zT[:, r, c], shared(hf), K.outgain[:, 0:1], zT[:, r, c], ALU.mult, ALU.mult).then_inc(free, 1)

            for item in items:
                norm(0, 0, item)
            piece(0, 0, 7)
            dve.sem_inc(bias_ok, 6)
            biased(0, 0, 0, True)
            biased(0, 0, 1, True)
            if not dil:
                mix(0, 0, 0)
            run_passes(dve, NPASS, one)


def lambda_phase(nc, K):
    LAM0 = 0.8 - 0.6 * math.exp(0.0)
    with ExitStack() as ctx:
        sb = lambda n, sh: ctx.enter_context(nc.sbuf_tensor("lam_" + n, sh, F32))
        v, pr, e, par = sb("v", [P, 4, 64]), sb("pr", [P, 2, 64]), sb("e", [P, 2]), sb("par", [P, 3])
        s = lambda n: semaphore(nc, ctx, "lam_" + n)
        v_in, V, A = s("in"), s("dve"), s("act")
        block = ctx.enter_context(nc.Block())

        @block.sync
        def _(sp):
            sp.dma_start(v[:, :, :].rearrange("p a b -> p (a b)"), K.d["lambdas"].to_broadcast([P, 256])).then_inc(v_in, 16)
            sp.dma_start(par[:, :], K.d["par_diff"]).then_inc(v_in, 16)

        @block.scalar
        def _(act):
            act.wait_ge(V, 2)
            nc.scalar.activation(e[:, :], e[:, :], ACT.Exp).then_inc(A, 1)

        @block.vector
        def _(dve):
            ch = Chain(dve, V)
            dve.wait_ge(v_in, 32)
            vv = v[:, :, :].rearrange("p (a b) n -> p a b n", b=2)
            ch.link(nc.vector.tensor_tensor(pr[:, :, :], vv[:, :, 0], vv[:, :, 1], ALU.mult))
            ch.link(nc.vector.reduce_sum(e[:, :], pr[:, :, :], axis=mybir.AxisListType.X))
            dve.wait_ge(A, 1)
            ch.link(nc.vector.tensor_tensor(K.neglam[:, :], e[:, 1:2], e[:, 0:1], ALU.subtract))
            ch.link(nc.vector.tensor_scalar(K.neglam[:, :], K.neglam[:, :], -LAM0, None, ALU.add))
            ch.link(nc.vector.tensor_scalar(K.outgain[:, :], par[:, 2:3], 1.0 - LAM0, None, ALU.mult))


def final_phase(nc, K, u_hi, u_lo, xr):
    with ExitStack() as ctx:
        sb = lambda n, sh, dt=F32: ctx.enter_context(nc.sbuf_tensor("g_" + n, sh, dt))
        W = K.W
        p_in = sb("p", [P, CH, 2 * P])
        pT, p_hi, p_lo = sb("pT", [P, 2, T]), sb("p_hi", [P, 2, T], F32R), sb("p_lo", [P, 2, T], F32R)
        pw, pw_hi, pw_lo = sb("pw", [P, KT, 2 * P]), sb("pw_hi", [P, KT, 2, P], F32R), sb("pw_lo", [P, KT, 2, P], F32R)
        gate = sb("gate", [P, T])
        ot = sb("out", [P, 2, CH, P])
        s = lambda n: semaphore(nc, ctx, "g_" + n)
        in_p, in_w, pturn, p_ok, p_hi_ok, p_lo_ok, w_hi_ok, w_lo_ok = (s(n) for n in
            ["in_p", "in_w", "pturn", "p_ok", "p_hi", "p_lo", "w_hi", "w_lo"])
        gate_mm, ple_mm, sig_ok, prod_ok, sum_ok, turned, copied = (s(n) for n in
            ["gate_mm", "ple_mm", "sig", "prod", "sum", "turned", "copied"])
        stored = [s("stored0"), s("stored1")]
        block = ctx.enter_context(nc.Block())
        ps = K.psum
        out = K.d["out"][0].rearrange("(c p) (f n) -> f p c n", p=P, n=P)

        def back(act, f):
            for h in range(2):
                act.wait_ge(turned, 2 * f + h + 1)
                if f >= 2:
                    act.wait_ge(stored[f % 2], 16 * (f // 2))
                nc.scalar.activation(ot[:, f % 2, 4 * h:4 * h + 4].rearrange("p c n -> p (c n)"),
                                     ps[:, 2048 + 512 * h:2048 + 512 * (h + 1)], ACT.Copy).then_inc(copied, 1)

        @block.sync
        def _(sp):
            sp.dma_start(p_in[:, :, :], K.d["p"][0, 0].rearrange("(c p) n -> p c n", p=P)).then_inc(in_p, 16)
            sp.dma_start(pw[:, :, :], K.d["w_ple"].rearrange("f p k -> p f k")).then_inc(in_w, 16)
            for n in range(KT - 2):
                W.load(sp, 0, 8, n)
            for f in range(KT):
                sp.wait_ge(copied, 2 * f + 2)
                sp.dma_start(out[f], ot[:, f % 2]).then_inc(stored[f % 2], 16)
            for r in range(2):
                sp.wait_ge(stored[r], 64)

        @block.gpsimd
        def _(pool):
            pool.wait_ge(in_w, 16)
            w4 = pw[:, :, :].rearrange("p f (k n) -> p f k n", k=2)
            nc.gpsimd.tensor_copy(pw_hi[:, :, :, :], w4).then_inc(w_hi_ok, 1)
            pool.wait_ge(w_hi_ok, 1)
            nc.gpsimd.tensor_tensor(pw_lo[:, :, :, :].rearrange("p f k n -> p (f k n)"), pw[:, :, :].rearrange("p f k -> p (f k)"),
                                    pw_hi[:, :, :, :].rearrange("p f k n -> p (f k n)").bitcast(F32), ALU.subtract).then_inc(w_lo_ok, 1)
            for n in range(KT - 2):
                W.split(pool, 0, 8, n)

        @block.tensor
        def _(pe):
            pe.wait_ge(in_p, 16)
            for c in range(CH):
                if c == 4:
                    pe.wait_ge(p_ok, 2)
                for k in range(2):
                    last = nc.tensor.transpose(ps[:, 3072 + 512 * k + P * (c % 4):3072 + 512 * k + P * (c % 4 + 1)],
                                               p_in[:, c, P * k:P * (k + 1)], K.ident[:, :])
                last.then_inc(pturn, 1)

            def turn(f):
                pe.wait_ge(sum_ok, f + 1)
                for h in range(2):
                    if f >= 1:
                        pe.wait_ge(copied, 2 * f + h - 1)
                    for m in range(4):
                        last = nc.tensor.transpose(ps[:, 2048 + 512 * h + P * m:2048 + 512 * h + P * (m + 1)],
                                                   xr[:, f, 512 * h + P * m:512 * h + P * (m + 1)], K.ident[:, :])
                    last.then_inc(turned, 1)

            for f in range(KT):
                W.wait(pe, 0, 8, f)
                for h in range(2):
                    c = slice(512 * h, 512 * (h + 1))
                    if f >= 1:
                        pe.wait_ge(sig_ok, 2 * (f - 1) + h + 1)
                    gemm(nc, ps[:, c], W.hi[:, f % 2], W.lo[:, f % 2], lambda k: u_hi[:, k, c], lambda k: u_lo[:, k, c]).then_inc(gate_mm, 1)
                if f == 0:
                    pe.wait_ge(w_lo_ok, 1)
                    pe.wait_ge(p_lo_ok, 1)
                for h in range(2):
                    c = slice(512 * h, 512 * (h + 1))
                    if f >= 1:
                        pe.wait_ge(prod_ok, f)
                    gemm(nc, ps[:, 1024 + 512 * h:1024 + 512 * (h + 1)], pw_hi[:, f], pw_lo[:, f],
                         lambda k: p_hi[:, k, c], lambda k: p_lo[:, k, c], kk=2).then_inc(ple_mm, 1)
                if f >= 1:
                    turn(f - 1)
            turn(KT - 1)

        @block.scalar
        def _(act):
            for g in range(2):
                act.wait_ge(pturn, 4 * g + 4)
                for k in range(2):
                    nc.scalar.activation(pT[:, k, 512 * g:512 * (g + 1)], ps[:, 3072 + 512 * k:3072 + 512 * (k + 1)], ACT.Copy).then_inc(p_ok, 1)
            act.wait_ge(p_ok, 4)
            nc.scalar.activation(p_hi[:, :, :], pT[:, :, :], ACT.Copy).then_inc(p_hi_ok, 1)
            for f in range(KT):
                for h in range(2):
                    act.wait_ge(gate_mm, 2 * f + h + 1)
                    if h == 1:
                        act.sem_inc(W.used, 1)
                    if f >= 1:
                        act.wait_ge(sum_ok, f)
                    nc.scalar.activation(gate[:, 512 * h:512 * (h + 1)], ps[:, 512 * h:512 * (h + 1)], ACT.Sigmoid).then_inc(sig_ok, 1)
                if f >= 1:
                    back(act, f - 1)
            back(act, KT - 1)

        @block.vector
        def _(dve):
            dve.wait_ge(p_hi_ok, 1)
            nc.vector.tensor_tensor(p_lo[:, :, :], pT[:, :, :], p_hi[:, :, :].bitcast(F32), ALU.subtract).then_inc(p_lo_ok, 1)
            for f in range(KT):
                dve.wait_ge(ple_mm, 2 * f + 2)
                dve.wait_ge(sig_ok, 2 * f + 2)
                nc.vector.tensor_tensor(gate[:, :], gate[:, :], ps[:, 1024:2048], ALU.mult).then_inc(prod_ok, 1)
                dve.wait_ge(prod_ok, f + 1)
                nc.vector.tensor_tensor(xr[:, f], xr[:, f], gate[:, :], ALU.add).then_inc(sum_ok, 1)


def program(nc, d, s):
    K = Kernel(d, s)
    with ExitStack() as top:
        sb = lambda n, sh, dt=F32: top.enter_context(nc.sbuf_tensor(n, sh, dt))
        K.psum = top.enter_context(nc.psum_tensor("psum", [P, 4096], F32))
        K.ident, K.tri, K.ones = sb("ident", [P, P]), sb("tri", [P, P]), sb("ones", [P, P])
        K.identb, K.maskb = sb("identb", [P, P], BF16), sb("maskb", [P, P], BF16)
        K.eps = sb("eps", [P, 1])
        K.mask = sb("mask", [P, P])
        K.pairs = sb("pairs", [P, P])
        K.neglam, K.outgain = sb("neglam", [P, 1]), sb("outgain", [P, 1])
        K.gains = sb("gains", [P, 4 * KT])
        K.W = Weights(nc, top, K.d["w_all"])
        with ExitStack() as one:
            sb1 = lambda n, sh, dt=F32: one.enter_context(nc.sbuf_tensor(n, sh, dt))
            u_hi, u_lo = sb1("u_hi", [P, KT, L], F32R), sb1("u_lo", [P, KT, L], F32R)
            sm = sb1("ssd_small", [P, GROUPS, 6, CH + 1, HG])
            with ExitStack() as c0:
                xT = c0.enter_context(nc.sbuf_tensor("xT", [P, KT, L], F32))
                load_phase(nc, K, xT)
                clear_semaphores(nc)
                norm_phase(nc, K, "n0", xT, L, THIRDS, K.gains[:, 0:KT], u_hi, u_lo)
                clear_semaphores(nc)
            small_phase(nc, K, u_hi, u_lo, sm)
            clear_semaphores(nc)
            K.W.base = 0
            ssd_phase(nc, K, u_hi, u_lo, sm)
            clear_semaphores(nc)
            K.W.base = 10 * GROUPS
            ssd_out_phase(nc, K)
            clear_semaphores(nc)
            K.W.base = K.W.base + 32
            fox_phase(nc, K, u_hi, u_lo)
            clear_semaphores(nc)
            K.W.base = K.W.base + 4 * KT
            merge_phase(nc, K, u_hi, u_lo)
            clear_semaphores(nc)
        with ExitStack() as two:
            sb2 = lambda n, sh, dt=F32: two.enter_context(nc.sbuf_tensor(n, sh, dt))
            xr = sb2("x_res", [P, KT, T])
            with ExitStack() as c1:
                o = c1.enter_context(nc.sbuf_tensor("w_out_o", [P, KT, T], F32))
                K.W.base = K.W.base + 3 * KT
                linear_phase(nc, K, "l1", K.s["merged"], o)
                clear_semaphores(nc)
                residual_phase(nc, K, o, K.gains[:, KT:2 * KT], xr)
                clear_semaphores(nc)
            lambda_phase(nc, K)
            clear_semaphores(nc)
            with ExitStack() as c2:
                h_hi, h_lo = (c2.enter_context(nc.sbuf_tensor("h_" + n, [P, KT, T], F32R)) for n in ("hi", "lo"))
                norm_phase(nc, K, "n2", xr, T, [(0, 512), (512, 1024)], K.gains[:, 2 * KT:3 * KT], h_hi, h_lo)
                clear_semaphores(nc)
                K.W.base = K.W.base + KT
                mixer_phase(nc, K, "md", False, h_hi, h_lo)
                clear_semaphores(nc)
                K.W.base = K.W.base + 16
                mixer_phase(nc, K, "ml", True, h_hi, h_lo)
                clear_semaphores(nc)
            K.W.base = K.W.base + 16
            linear_phase(nc, K, "l2", K.s["mix"], xr, add=True)
            clear_semaphores(nc)
            with ExitStack() as c4:
                r_hi, r_lo = (c4.enter_context(nc.sbuf_tensor("r_" + n, [P, KT, T], F32R)) for n in ("hi", "lo"))
                norm_phase(nc, K, "n3", xr, T, [(0, 512), (512, 1024)], K.gains[:, 3 * KT:4 * KT], r_hi, r_lo)
                clear_semaphores(nc)
                K.W.base = K.W.base + KT
                final_phase(nc, K, r_hi, r_lo, xr)
                clear_semaphores(nc)


def tiles(np, w):
    k, n = w.shape[0] // P, w.shape[1] // P
    return w.reshape(k, P, n, P).transpose(2, 1, 0, 3).reshape(n, P, k * P)


def cols(v):
    return v.reshape(-1, P).transpose(1, 0)


def kernel(**inputs):
    import numpy as np
    import concourse.bacc as bacc
    from concourse import mybir as mb
    from concourse.bass_utils import run_bass_kernel_spmd as run

    I = {k: np.asarray(v) for k, v in inputs.items()}
    g = lambda n: I[n][0]
    A = {}
    A["x"], A["meta"] = I["x"], I["meta_tokens"]
    w = g("w_in")
    o_x, o_dt, o_za = 2048, 5120, 5152
    o_q, o_k, o_v, o_f, o_g = 6176, 7200, 8224, 9248, 9264
    tz, txs = tiles(np, w[:, 0:2048]), tiles(np, w[:, o_x:o_x + 2048])
    tb, tc = tiles(np, w[:, o_x + 2048:o_x + 2560]), tiles(np, w[:, o_x + 2560:o_x + 3072])
    w_ssd = np.concatenate([np.concatenate([txs[4 * i:4 * i + 4], tb[i:i + 1], tc[i:i + 1], tz[4 * i:4 * i + 4]]) for i in range(GROUPS)])
    A["wdf"] = np.concatenate([w[:, o_dt:o_dt + 32], w[:, o_f:o_f + 16]], axis=1).reshape(KT, P, SM).transpose(1, 0, 2)
    A["dtf_bias"] = np.concatenate([g("dt_bias"), g("fgate_bias")])[None]
    A["a_log"] = g("a_log")[None]
    A["gains"] = np.concatenate([cols(g("norm_pre")), cols(g("norm_post")), cols(g("mix_norm_g_2")), cols(g("ple_norm_g_2"))], axis=1)
    cw = np.concatenate([g("conv_w"), g("conv_b")[None]])
    cw = cw.reshape(5, 24, P).transpose(2, 1, 0)
    dsk = cols(np.broadcast_to(g("d_skip")[:, None], (SSD_H, 64)).reshape(-1))
    gn = cols(g("ssd_norm"))
    A["conv_par"] = np.stack([np.concatenate([cw[:, 4 * i:4 * i + 4].reshape(P, 20), cw[:, 16 + i], cw[:, 20 + i],
                                              dsk[:, 4 * i:4 * i + 4], gn[:, 4 * i:4 * i + 4]], axis=1) for i in range(GROUPS)], axis=1)
    A["mask"] = np.triu(np.ones((P, P), np.float32), 1)
    w_proj_ssd = tiles(np, g("w_proj_ssd")).reshape(KT, P, 2, KT * P).transpose(0, 2, 1, 3).reshape(16, P, KT * P)
    tq, tk, tv, tza = (tiles(np, w[:, o:o + 1024]) for o in (o_q, o_k, o_v, o_za))
    w_fox = np.stack([tq, tk, tv, tza], axis=1).reshape(32, P, KT * P)
    tgs, tga, twa = tiles(np, w[:, o_g:o_g + 1024]), tiles(np, w[:, o_g + 1024:o_g + 2048]), tiles(np, g("w_proj_att"))
    w_merge = np.stack([tgs, tga, twa], axis=1).reshape(24, P, KT * P)
    A["gate_bias"] = cols(g("gate_bias"))
    A["pairs"] = np.kron(np.eye(2, dtype=np.float32), np.ones((64, 64), np.float32))
    w2 = tiles(np, g("w_in_2"))
    w_diff = np.stack([w2[0:4], w2[4:8], w2[8:12], w2[24:28]], axis=1).reshape(16, P, KT * P)
    w_dil = np.stack([w2[12:16], w2[16:20], w2[20:24], w2[28:32]], axis=1).reshape(16, P, KT * P)
    A["w_ple"] = tiles(np, g("w_ple_proj_2"))
    A["w_all"] = np.concatenate([w_ssd, w_proj_ssd, w_proj_ssd, w_fox, w_merge, tiles(np, g("w_out")), w_diff, w_dil,
                                 tiles(np, g("w_out_2")), tiles(np, g("w_ple_gate_2"))])
    A["p"] = I["p_2"]
    A["lambdas"] = np.concatenate([g("lambda_q1_2"), g("lambda_k1_2"), g("lambda_q2_2"), g("lambda_k2_2")])[None]
    twice = lambda v: np.concatenate([v, v])
    A["par_diff"] = np.stack([twice(g("diff_q_norm_g_2")), twice(g("diff_k_norm_g_2")), g("diff_sub_norm_g_2")], axis=1)
    A["par_dil"] = np.stack([twice(g("dil_q_norm_g_2")), twice(g("dil_k_norm_g_2")), twice(g("dil_k_norm_g_2"))], axis=1)
    dist = np.abs(np.arange(P)[:, None] + (T - P) - np.arange(2 * T - P)[None, :])
    A["dist"] = dist.astype(np.float32)
    held = (dist <= 64) * 1 + ((dist <= 256) & (dist % 4 == 0)) + (dist % 16 == 0)
    A["count"] = np.where(held > 0, 8.0 * np.log(np.maximum(held, 1)), NEG).astype(np.float32)
    A["slopes_diff"] = np.broadcast_to(np.array([-8.0 * 2.0 ** (-2.0 * (i % 4 + 1)) for i in range(8)], np.float32), (P, 8))
    A["slopes_dil"] = np.broadcast_to(np.array([-8.0 * 2.0 ** (-(i + 1.0)) for i in range(8)], np.float32), (P, 8))
    A["ident"] = np.eye(P, dtype=np.float32)
    A["tri"] = np.triu(np.ones((P, P), np.float32))
    nc = bacc.Bacc("TRN2", target_bir_lowering=False, num_devices=1)
    arrays, ins = {}, {}
    for n, a in A.items():
        a = np.ascontiguousarray(a)
        arrays["in_" + n] = a
        ins[n] = (nc.dram_tensor("in_" + n, a.shape, mb.dt.from_np(a.dtype), kind="ExternalInput").ap())
    ins["out"] = nc.dram_tensor("out_0", (1, T, D), F32, kind="ExternalOutput").ap()
    s = {}
    s["xT"] = nc.dram_tensor("s_xT", (KT, P, T), F32, kind="Internal").ap()
    s["y"] = nc.dram_tensor("s_y", (16, P, T), F32, kind="Internal").ap()
    for n in ("pssd", "yatt", "merged", "mix"):
        s[n] = nc.dram_tensor("s_" + n, (KT, P, T), F32, kind="Internal").ap()
    s["nc"] = nc.dram_tensor("s_nc", (ATT_H, L), F32, kind="Internal").ap()
    program(nc, ins, s)
    r = run(nc, [arrays], core_ids=[0])
    return r.results[0]["out_0"]
```
